# Optimizing a Trainium2 kernel written in Bass

```python
import math
import jax, jax.numpy as jnp
from jax import lax
import numpy as np

D_MODEL = 1024
BATCH = 1
SEQ = 1024
DEPTH = 1

GLA_HEADS = 4
GLA_DK = 64
GLA_DV = 128
GLA_GATE_RANK = 16
GLA_GATE_TAU = 16.0
GLA_CHUNK = 64
DIFF_HEADS = 4
DIFF_DK = 64
DIFF_DV = 2 * DIFF_DK
ROPE_DIM = DIFF_DK // 4
ROPE_THETA = 500000.0
Q_BLOCK = 128
MIX_WIDTH = GLA_HEADS * GLA_DV + DIFF_HEADS * DIFF_DV

IN_SPLITS = [
    GLA_HEADS * GLA_DK,
    GLA_HEADS * GLA_DK,
    GLA_HEADS * GLA_DV,
    GLA_GATE_RANK,
    GLA_HEADS * GLA_DV,
    2 * DIFF_HEADS * DIFF_DK,
    2 * DIFF_HEADS * DIFF_DK,
    DIFF_HEADS * DIFF_DV,
]
IN_WIDTH = int(sum(IN_SPLITS))
SPLIT_IDX = [int(v) for v in np.cumsum(IN_SPLITS)[:-1]]

PEER_HEADS = 8
PEER_NKEYS = 128
PEER_EXPERTS = PEER_NKEYS * PEER_NKEYS
PEER_QDIM = 256
PEER_TOPK = 16
PEER_TOKEN_BLOCK = 128

RMS_EPS = 1e-6

kernel_name = "hymba_gla_diffattn_peer_block"

def rms_norm(x, g):
    xf = x.astype(jnp.float32)
    y = xf * lax.rsqrt(jnp.mean(xf * xf, axis=-1, keepdims=True) + RMS_EPS)
    return (y * g.astype(jnp.float32)).astype(x.dtype)

def rope_tables(positions):
    inv_freq = ROPE_THETA ** (-jnp.arange(0, ROPE_DIM, 2, dtype=jnp.float32) / ROPE_DIM)
    ang = positions.astype(jnp.float32)[..., None] * inv_freq
    return jnp.cos(ang), jnp.sin(ang)

def partial_rope(t, cos, sin):
    half = ROPE_DIM // 2
    x1 = t[..., :half].astype(jnp.float32)
    x2 = t[..., half:ROPE_DIM].astype(jnp.float32)
    rot = jnp.concatenate([x1 * cos - x2 * sin, x2 * cos + x1 * sin], axis=-1).astype(t.dtype)
    return jnp.concatenate([rot, t[..., ROPE_DIM:]], axis=-1)

def gla_chunked(q, k, v, log_a):
    B, H, S, dk = q.shape
    dv = v.shape[-1]
    n = S // GLA_CHUNK
    f32 = jnp.float32
    q = q.astype(f32).reshape(B, H, n, GLA_CHUNK, dk)
    k = k.astype(f32).reshape(B, H, n, GLA_CHUNK, dk)
    v = v.astype(f32).reshape(B, H, n, GLA_CHUNK, dv)
    b = jnp.cumsum(log_a.astype(f32).reshape(B, H, n, GLA_CHUNK, dk), axis=-2)
    b_end = b[..., -1:, :]
    q_t = q * jnp.exp(b)
    k_t = k * jnp.exp(-b)
    causal = jnp.tril(jnp.ones((GLA_CHUNK, GLA_CHUNK), dtype=bool))
    att = jnp.where(causal, jnp.einsum('bhncd,bhnsd->bhncs', q_t, k_t), 0.0)
    o_intra = jnp.einsum('bhncs,bhnsv->bhncv', att, v)
    chunk_kv = jnp.einsum('bhncd,bhncv->bhndv', k * jnp.exp(b_end - b), v)
    decay_end = jnp.exp(b_end[..., 0, :])

    def step(state, inp):
        dec, kv = inp
        return dec[..., None] * state + kv, state

    init = jnp.zeros((B, H, dk, dv), f32)
    _, states = lax.scan(step, init, (jnp.moveaxis(decay_end, 2, 0), jnp.moveaxis(chunk_kv, 2, 0)))
    states = jnp.moveaxis(states, 0, 2)
    o_inter = jnp.einsum('bhncd,bhndv->bhncv', q_t, states)
    return (o_intra + o_inter).reshape(B, H, S, dv)

def gla_mixer(gq, gk, gv, ga, gr, w_gate, b_gate, g_out):
    B, S, _ = gq.shape
    to_heads = lambda t, d: t.reshape(B, S, GLA_HEADS, d).transpose(0, 2, 1, 3)
    q = to_heads(gq, GLA_DK) * (GLA_DK ** -0.5)
    k = to_heads(gk, GLA_DK)
    v = to_heads(gv, GLA_DV)
    log_a = jax.nn.log_sigmoid((ga @ w_gate + b_gate).astype(jnp.float32)) / GLA_GATE_TAU
    log_a = to_heads(log_a, GLA_DK)
    o = gla_chunked(q, k, v, log_a).astype(gv.dtype)
    o = rms_norm(o, g_out).transpose(0, 2, 1, 3).reshape(B, S, GLA_HEADS * GLA_DV)
    return o * jax.nn.silu(gr)

def diff_mixer(dq, dk, dv, cos, sin, g_q, g_k, lq1, lk1, lq2, lk2, g_sub, lambda_init):
    B, S, _ = dq.shape
    q = dq.reshape(B, S, DIFF_HEADS, 2, DIFF_DK).transpose(0, 2, 3, 1, 4)
    k = dk.reshape(B, S, DIFF_HEADS, 2, DIFF_DK).transpose(0, 2, 3, 1, 4)
    v = dv.reshape(B, S, DIFF_HEADS, DIFF_DV).transpose(0, 2, 1, 3)
    c = cos[:, None, None]
    s_ = sin[:, None, None]
    q = partial_rope(rms_norm(q, g_q), c, s_)
    k = partial_rope(rms_norm(k, g_k), c, s_)
    lam = (jnp.exp(jnp.sum(lq1.astype(jnp.float32) * lk1.astype(jnp.float32)))
           - jnp.exp(jnp.sum(lq2.astype(jnp.float32) * lk2.astype(jnp.float32))) + lambda_init)
    scale = DIFF_DK ** -0.5
    nb = S // Q_BLOCK
    qb = jnp.moveaxis(q.reshape(B, DIFF_HEADS, 2, nb, Q_BLOCK, DIFF_DK), 3, 0)
    kidx = jnp.arange(S)

    def block(args):
        qblk, i = args
        sc = jnp.einsum('bhmqd,bhmkd->bhmqk', qblk, k).astype(jnp.float32) * scale
        qidx = i * Q_BLOCK + jnp.arange(Q_BLOCK)
        sc = jnp.where(kidx[None, :] <= qidx[:, None], sc, -jnp.inf)
        p = jax.nn.softmax(sc, axis=-1)
        a = p[:, :, 0] - lam * p[:, :, 1]
        return jnp.einsum('bhqk,bhkv->bhqv', a.astype(v.dtype), v)

    o = lax.map(block, (qb, jnp.arange(nb)))
    o = jnp.moveaxis(o, 0, 2).reshape(B, DIFF_HEADS, S, DIFF_DV)
    o = rms_norm(o, g_sub) * (1.0 - lambda_init)
    return o.transpose(0, 2, 1, 3).reshape(B, S, DIFF_HEADS * DIFF_DV)

def peer_mixer(x2, w_q, sub_keys, u, v):
    B, S, D = x2.shape
    T = B * S
    xt = x2.reshape(T, D)
    q = (xt @ w_q).reshape(T, PEER_HEADS, 2, PEER_QDIM // 2)
    s = jnp.einsum('thpd,hpkd->thpk', q, sub_keys).astype(jnp.float32)
    s_top, i_top = lax.top_k(s, PEER_TOPK)
    cand_s = (s_top[:, :, 0, :, None] + s_top[:, :, 1, None, :]).reshape(T, PEER_HEADS, PEER_TOPK * PEER_TOPK)
    cand_i = (i_top[:, :, 0, :, None] * PEER_NKEYS + i_top[:, :, 1, None, :]).reshape(T, PEER_HEADS, PEER_TOPK * PEER_TOPK)
    best_s, best_pos = lax.top_k(cand_s, PEER_TOPK)
    idx = jnp.take_along_axis(cand_i, best_pos, axis=-1)
    g = jax.nn.softmax(best_s, axis=-1).astype(x2.dtype)
    nblk = T // PEER_TOKEN_BLOCK
    E = PEER_HEADS * PEER_TOPK
    xb = xt.reshape(nblk, PEER_TOKEN_BLOCK, D)
    ib = idx.reshape(nblk, PEER_TOKEN_BLOCK, E)
    gb = g.reshape(nblk, PEER_TOKEN_BLOCK, E)

    def block(args):
        xc, ic, gc = args
        h = jnp.einsum('td,ted->te', xc, jnp.take(u, ic, axis=0))
        a = jax.nn.gelu(h, approximate=False) * gc
        return jnp.einsum('te,ted->td', a, jnp.take(v, ic, axis=0))

    return lax.map(block, (xb, ib, gb)).reshape(B, S, D)

def setup_inputs(seed: int = 0) -> dict:
    key = jax.random.key(seed)
    ks = jax.random.split(key, 24)
    f32 = jnp.float32
    L, D = DEPTH, D_MODEL
    nrm = lambda k, shape, sc: jax.random.normal(k, shape, f32) * sc
    x = jax.random.normal(ks[0], (BATCH, SEQ, D), f32)
    offsets = jax.random.randint(ks[1], (BATCH, 1), 0, 4096, dtype=jnp.int32)
    positions = (jnp.arange(SEQ, dtype=jnp.int32)[None, :] + offsets).astype(jnp.int32)
    return {
        "x": x,
        "positions": positions,
        "g_mix": 1.0 + nrm(ks[2], (L, D), 0.1),
        "w_in": nrm(ks[3], (L, D, IN_WIDTH), D ** -0.5),
        "w_gla_gate": nrm(ks[4], (L, GLA_GATE_RANK, GLA_HEADS * GLA_DK), GLA_GATE_RANK ** -0.5),
        "b_gla_gate": nrm(ks[5], (L, GLA_HEADS * GLA_DK), 0.1),
        "g_gla_out": 1.0 + nrm(ks[6], (L, GLA_DV), 0.1),
        "g_q": 1.0 + nrm(ks[7], (L, DIFF_DK), 0.1),
        "g_k": 1.0 + nrm(ks[8], (L, DIFF_DK), 0.1),
        "lambda_q1": nrm(ks[9], (L, DIFF_DK), 0.1),
        "lambda_k1": nrm(ks[10], (L, DIFF_DK), 0.1),
        "lambda_q2": nrm(ks[11], (L, DIFF_DK), 0.1),
        "lambda_k2": nrm(ks[12], (L, DIFF_DK), 0.1),
        "g_diff_sub": 1.0 + nrm(ks[13], (L, DIFF_DV), 0.1),
        "w_out": nrm(ks[14], (L, MIX_WIDTH, D), MIX_WIDTH ** -0.5),
        "g_ffn": 1.0 + nrm(ks[15], (L, D), 0.1),
        "w_peer_q": nrm(ks[16], (L, D, PEER_HEADS * PEER_QDIM), D ** -0.5),
        "peer_sub_keys": nrm(ks[17], (L, PEER_HEADS, 2, PEER_NKEYS, PEER_QDIM // 2), (PEER_QDIM // 2) ** -0.5),
        "peer_u": nrm(ks[18], (L, PEER_EXPERTS, D), D ** -0.5),
        "peer_v": nrm(ks[19], (L, PEER_EXPERTS, D), 0.5),
    }

def reference(x, positions, g_mix, w_in, w_gla_gate, b_gla_gate, g_gla_out, g_q, g_k,
              lambda_q1, lambda_k1, lambda_q2, lambda_k2, g_diff_sub, w_out, g_ffn,
              w_peer_q, peer_sub_keys, peer_u, peer_v):
    cos, sin = rope_tables(positions)
    h = x
    for l in range(DEPTH):
        lambda_init = 0.8 - 0.6 * math.exp(-0.3 * l)
        xn = rms_norm(h, g_mix[l])
        proj = xn @ w_in[l]
        gq, gk, gv, ga, gr, dq, dk, dv = jnp.split(proj, SPLIT_IDX, axis=-1)
        o_gla = gla_mixer(gq, gk, gv, ga, gr, w_gla_gate[l], b_gla_gate[l], g_gla_out[l])
        o_diff = diff_mixer(dq, dk, dv, cos, sin, g_q[l], g_k[l], lambda_q1[l], lambda_k1[l],
                            lambda_q2[l], lambda_k2[l], g_diff_sub[l], lambda_init)
        h = h + jnp.concatenate([o_gla, o_diff], axis=-1) @ w_out[l]
        h = h + peer_mixer(rms_norm(h, g_ffn[l]), w_peer_q[l], peer_sub_keys[l], peer_u[l], peer_v[l])
    return h


_drawn_inputs = setup_inputs


def setup_inputs(seed=0):
    import zlib

    import numpy as np

    out = dict(_drawn_inputs(seed))
    spreads = {}
    factors = {'lambda_q1': 2.794, 'lambda_k1': 5.286}
    for name, (base, spread) in spreads.items():
        noise = np.random.default_rng([zlib.crc32(name.encode()), seed]).standard_normal(out[name].shape)
        drawn = base * np.exp(spread * noise) if base else spread * noise
        out[name] = __import__('jax').numpy.asarray(drawn.astype(out[name].dtype))
    for name, factor in factors.items():
        out[name] = (out[name] * factor).astype(out[name].dtype)
    return out
```

```python
from contextlib import ExitStack

import numpy as np
import concourse.bass as bass
from concourse import mybir

F32 = mybir.dt.float32
F16 = mybir.dt.float16
BF16 = mybir.dt.bfloat16
I32 = mybir.dt.int32
U32 = mybir.dt.uint32
ALU = mybir.AluOpType
ACT = mybir.ActivationFunctionType
AX = mybir.AxisListType

P = 128
SEQ = 1024
D = 1024
KT = D // P
NT = SEQ // P
HALF = 512

GLA_H, GLA_DK, GLA_DV, GLA_RANK, GLA_TAU, CHUNK = 4, 64, 128, 16, 16.0, 64
DIFF_H, DIFF_DK, DIFF_DV = 4, 64, 128
ROPE = DIFF_DK // 4
HROPE = ROPE // 2
ROPE_THETA = 500000.0
LAMBDA_INIT = 0.8 - 0.6 * float(np.exp(-0.3 * 0))
EPS = 1e-6

PEER_H, NKEYS, QDIM, TOPK = 8, 128, 256, 16
PICKS = PEER_H * TOPK

S_ACT = 16.0
S_W = 64.0
UNSCALE = 1.0 / (S_ACT * S_W)
BASE = 64


class Names:
    pass


class Chain:

    def __init__(self, eng, sem, at=0):
        self.eng, self.sem, self.at, self.n = eng, sem, at, 0

    def step(self, ins):
        self.n += 1
        ins.then_inc(self.sem, 1)

    def wait(self):
        self.eng.wait_ge(self.sem, self.at + self.n)

    def link(self, ins):
        self.step(ins)
        self.wait()


class Space:

    def __init__(self, nc, ctx, tag):
        self.nc, self.ctx, self.tag = nc, ctx, tag

    def sb(self, name, shape, dt=F32):
        return self.ctx.enter_context(self.nc.sbuf_tensor(f"{self.tag}_{name}", shape, dt))

    def ps(self, name, shape, dt=F32):
        return self.ctx.enter_context(self.nc.psum_tensor(f"{self.tag}_{name}", shape, dt))

    def sem(self, name):
        return self.nc.alloc_semaphore(f"{self.tag}_{name}")


def lanes(ap, *shape):
    axis = shape[0]
    return ap.unsqueeze(axis).broadcast_to(list(shape[1:]))


def constants(nc, io, T):
    with ExitStack() as ctx:
        S = Space(nc, ctx, "c")
        loaded = S.sem("loaded")
        pool_step = S.sem("pool_step")
        vec_step = S.sem("vec_step")
        act_step = S.sem("act_step")
        gates = S.sem("gates")
        pos = S.sb("pos", [P, NT], I32)
        posf = S.sb("posf", [P, NT])
        freq = S.sb("freq", [P, HROPE])
        ang = S.sb("ang", [P, NT, HROPE])
        turns_i = S.sb("turns_i", [P, NT * HROPE], I32)
        turns = S.sb("turns", [P, NT * HROPE])
        wrap = S.sb("wrap", [P, NT * HROPE])
        lamv = S.sb("lamv", [P, 4, DIFF_DK])
        lamp = S.sb("lamp", [P, DIFF_DK])
        lams = S.sb("lams", [P, 2])
        lame = S.sb("lame", [P, 2])
        block = ctx.enter_context(nc.Block())

        @block.sync
        def _(sp):
            with nc.allow_non_contiguous_dma("columns of small weights"):
                sp.dma_start(pos[:], io.positions.rearrange("b (t p) -> p (b t)", p=P)).then_inc(loaded, 16)
                sp.dma_start(T.g_mix[:], io.g_mix.rearrange("l (k p) -> p (l k)", p=P)).then_inc(loaded, 16)
                sp.dma_start(T.g_ffn[:], io.g_ffn.rearrange("l (k p) -> p (l k)", p=P)).then_inc(loaded, 16)
                sp.dma_start(T.g_sub[:], io.g_diff_sub.rearrange("l p -> p l")).then_inc(loaded, 16)
                sp.dma_start(T.b_gate[:], io.b_gla_gate.rearrange("l (c p) -> p (l c)", p=P)).then_inc(loaded, 16)
            sp.dma_start(T.g_gla[:], io.g_gla_out[0, :].partition_broadcast(P)).then_inc(loaded, 16)
            sp.dma_start(T.g_q[:], io.g_q[0, :].partition_broadcast(P)).then_inc(loaded, 16)
            sp.dma_start(T.g_k[:], io.g_k[0, :].partition_broadcast(P)).then_inc(loaded, 16)
            sp.dma_start(T.w_gate[:], io.w_gla_gate[0]).then_inc(loaded, 16)
            for n, v in enumerate((io.lambda_q1, io.lambda_k1, io.lambda_q2, io.lambda_k2)):
                sp.dma_start(lamv[:, n, :], v[0, :].partition_broadcast(P)).then_inc(loaded, 16)

        @block.gpsimd
        def _(pool):
            c = Chain(pool, pool_step)
            c.step(nc.gpsimd.memset(T.ident[:], 0.0))
            c.step(nc.gpsimd.memset(T.causal[:], 0.0))
            c.step(nc.gpsimd.memset(T.tri[:], 1.0))
            c.step(nc.gpsimd.memset(T.mhalf[:], -0.5))
            c.step(nc.gpsimd.memset(T.eps[:], EPS))
            c.step(nc.gpsimd.iota(T.iota_i[:], [[1, P]], base=0, channel_multiplier=0))
            c.wait()
            c.step(nc.gpsimd.affine_select(out=T.ident[:], in_=T.ident[:], compare_op=ALU.not_equal, fill=1.0,
                                           base=0, pattern=[[-1, P]], channel_multiplier=1))
            c.step(nc.gpsimd.affine_select(out=T.causal[:], in_=T.causal[:], compare_op=ALU.is_ge, fill=-1e30,
                                           base=0, pattern=[[-1, P]], channel_multiplier=1))
            c.step(nc.gpsimd.affine_select(out=T.tri[:], in_=T.tri[:], compare_op=ALU.is_ge, fill=0.0,
                                           base=0, pattern=[[1, P]], channel_multiplier=-1))
            c.step(nc.gpsimd.tensor_copy(T.iota[:], T.iota_i[:]))
            c.wait()
            nc.gpsimd.memset(T.tri[0:CHUNK, CHUNK:P], 0.0).then_inc(gates, 1)

        @block.vector
        def _(dve):
            c = Chain(dve, vec_step)
            for j in range(HROPE):
                c.step(nc.vector.memset(freq[:, j:j + 1], float(np.float32(ROPE_THETA) ** np.float32(-2.0 * j / ROPE))))
            dve.wait_ge(loaded, 16 * 13)
            c.link(nc.vector.tensor_copy(posf[:], pos[:]))
            c.link(nc.vector.tensor_tensor(ang[:], lanes(posf[:], 2, P, NT, HROPE), lanes(freq[:], 1, P, NT, HROPE),
                                           ALU.mult))
            flat = ang[:].rearrange("p t j -> p (t j)")
            c.link(nc.vector.tensor_scalar(turns[:], flat, 1.0 / (2 * np.pi), None, ALU.mult))
            c.link(nc.vector.tensor_copy(turns_i[:], turns[:]))
            c.link(nc.vector.tensor_copy(turns[:], turns_i[:]))
            c1 = 6.28125
            c2 = float(np.floor((2 * np.pi - c1) * 2 ** 22) / 2 ** 22)
            c3 = float(2 * np.pi - c1 - c2)
            for part in (c1, c2, c3):
                c.link(nc.vector.scalar_tensor_tensor(flat, turns[:], -part, flat, ALU.mult, ALU.add))
            lim = 3.1415925
            c.link(nc.vector.tensor_scalar(T.sin[:].rearrange("p t j -> p (t j)"), flat, lim, -lim, ALU.min, ALU.max))
            c.link(nc.vector.tensor_scalar(wrap[:], flat, float(np.pi / 2), -2 * float(np.pi), ALU.is_gt, ALU.mult))
            c.link(nc.vector.scalar_tensor_tensor(flat, flat, float(np.pi / 2), wrap[:], ALU.add, ALU.add))
            c.link(nc.vector.tensor_scalar(T.cos[:].rearrange("p t j -> p (t j)"), flat, lim, -lim, ALU.min, ALU.max))
            for n in range(2):
                c.link(nc.vector.tensor_tensor(lamp[:], lamv[:, 2 * n, :], lamv[:, 2 * n + 1, :], ALU.mult))
                c.link(nc.vector.tensor_reduce(lams[:, n:n + 1], lamp[:], AX.X, ALU.add))
            nc.vector.tensor_scalar(T.g_mix[:], T.g_mix[:], S_W, None, ALU.mult).then_inc(gates, 1)
            nc.vector.tensor_scalar(T.g_ffn[:], T.g_ffn[:], S_ACT, None, ALU.mult).then_inc(gates, 1)
            nc.vector.tensor_scalar(T.g_sub[:], T.g_sub[:], S_ACT * (1.0 - LAMBDA_INIT), None,
                                    ALU.mult).then_inc(gates, 1)
            dve.wait_ge(act_step, 3)
            c.link(nc.vector.scalar_tensor_tensor(T.neg_lam[:], lame[:, 1:2], -LAMBDA_INIT, lame[:, 0:1],
                                                  ALU.add, ALU.subtract))

        @block.scalar
        def _(act):
            act.wait_ge(vec_step, HROPE + 16)
            nc.scalar.activation(lame[:], lams[:], ACT.Exp).then_inc(act_step, 1)
            nc.scalar.activation(T.sin[:], T.sin[:], ACT.Sin).then_inc(act_step, 1)
            nc.scalar.activation(T.cos[:], T.cos[:], ACT.Sin).then_inc(act_step, 1)


def split_mm(pe, out, a_hi, a_lo, b_hi, b_lo, first, last):
    pe.matmul(out, a_hi, b_hi, start=first, stop=False)
    pe.matmul(out, a_hi, b_lo, start=False, stop=False)
    return pe.matmul(out, a_lo, b_hi, start=False, stop=last)


COLS = [("qk", 0, 512), ("gv", 512, 512), ("gr", 1040, 512), ("dq", 1552, 512), ("dk", 2064, 512),
        ("dv", 2576, 512), ("ga", 1024, GLA_RANK)]


XR = 4


def project_in(nc, io, T):
    with ExitStack() as ctx:
        S = Space(nc, ctx, "a")
        x_in = S.sb("x_in", [P, XR, D])
        junk = S.sb("junk", [P, D], F16)
        ss = S.sb("ss", [P, NT])
        rstd = S.sb("rstd", [P, NT])
        w_in = S.sb("w_in", [P, 2, 2, HALF])
        w_hi = S.sb("w_hi", [P, 2, KT, HALF], F16)
        w_lo = S.sb("w_lo", [P, 2, KT, HALF], F16)
        sq = S.sb("sq", [P, 2, HALF])
        hss = S.sb("hss", [P, 2, 8])
        hr = S.sb("hr", [P, 2, 8])
        turned = [S.ps(f"turned{b}", [P, KT, P]) for b in range(2)]
        acc = [S.ps(f"acc{b}", [P, HALF]) for b in range(4)]

        x_loaded = [S.sem(f"x_loaded{b}") for b in range(XR)]
        w_loaded = [S.sem(f"w_loaded{b}") for b in range(2)]
        squared = S.sem("squared")
        rstd_done = S.sem("rstd_done")
        pool_step = S.sem("pool_step")
        normed = S.sem("normed")
        x_turned = S.sem("x_turned")
        hi_done = S.sem("hi_done")
        lo_done = S.sem("lo_done")
        w_hi_done = S.sem("w_hi_done")
        w_lo_done = S.sem("w_lo_done")
        acc_full = S.sem("acc_full")
        acc_free = S.sem("acc_free")
        head_sq = S.sem("head_sq")
        head_ss = S.sem("head_ss")
        head_r = S.sem("head_r")
        head_normed = S.sem("head_normed")
        head_g = S.sem("head_g")
        block = ctx.enter_context(nc.Block())

        PIECES = KT // 2
        gains = {"dq": T.g_q, "dk": T.g_k}
        dest = {"gv": T.gv, "gr": T.gr, "dq": T.dq, "dk": T.dk, "dv": T.dv}
        first_result = [8 * c for c in range(len(COLS))]

        @block.sync
        def _(sp):
            def load_w(c):
                _, c0, n = COLS[c]
                for q in range(PIECES):
                    r = c * PIECES + q
                    if r >= 2:
                        sp.wait_ge(w_lo_done, r - 1)
                    src = io.w_in[0, 2 * q * P:(2 * q + 2) * P, c0:c0 + n].rearrange("(k p) n -> p k n", p=P)
                    sp.dma_start(w_in[:, r % 2, :, 0:n], src).then_inc(w_loaded[r % 2], 16)

            for t in range(NT):
                if t >= XR:
                    sp.wait_ge(x_turned, t - XR + 1)
                sp.dma_start(x_in[:, t % XR, :], io.x[0, t * P:(t + 1) * P, :]).then_inc(x_loaded[t % XR], 16)
                if t == XR - 1:
                    load_w(0)
            for c in range(1, len(COLS)):
                load_w(c)

        @block.gpsimd
        def _(pool):
            c = Chain(pool, pool_step)
            for t in range(NT):
                pool.wait_ge(squared, t + 1)
                c.link(nc.gpsimd.tensor_scalar(rstd[:, t:t + 1], ss[:, t:t + 1], 1.0 / D, EPS, ALU.mult, ALU.add))
                nc.gpsimd.tensor_tensor(rstd[:, t:t + 1], rstd[:, t:t + 1], T.mhalf[:, 0:1],
                                        ALU.pow).then_inc(rstd_done, 1)
            base = c.n
            with pool.Fori(0, NT) as i:
                c = Chain(pool, pool_step, base + 2 * i)
                for b in range(2):
                    pool.wait_ge(head_ss, 2 * i + b + 1)
                    c.link(nc.gpsimd.tensor_tensor(hr[:, b, :], hss[:, b, :], T.eps[:, 0:8], ALU.add))
                    nc.gpsimd.tensor_tensor(hr[:, b, :], hr[:, b, :], T.mhalf[:, 0:8], ALU.pow).then_inc(head_r, 1)

        @block.scalar
        def _(act):
            act.sem_inc(acc_free, BASE)

            def split_w(c):
                n = COLS[c][2]
                if c >= 2:
                    act.wait_ge(acc_full, 8 * (c - 1))
                for q in range(PIECES):
                    r = c * PIECES + q
                    act.wait_ge(w_loaded[r % 2], 16 * (r // 2 + 1))
                    for j in range(2):
                        k = 2 * q + j
                        last = nc.scalar.activation(w_hi[:, c % 2, k, 0:n], w_in[:, r % 2, j, 0:n], ACT.Copy,
                                                    scale=T.g_mix[:, k:k + 1])
                    last.then_inc(w_hi_done, 1)

            def square(t):
                act.wait_ge(x_loaded[t % XR], 16 * (t // XR + 1))
                if t:
                    act.wait_ge(squared, t)
                nc.scalar.activation(junk[:], x_in[:, t % XR, :], ACT.Square,
                                     accum_out=ss[:, t:t + 1]).then_inc(squared, 1)

            square(0)
            split_w(0)
            for t in range(NT):
                if t + 1 < NT:
                    square(t + 1)
                act.wait_ge(x_turned, t + 1)
                nc.scalar.activation(T.act_hi[:, :, t * P:(t + 1) * P], turned[t % 2][:], ACT.Copy,
                                     scale=S_ACT).then_inc(hi_done, 1)
            split_w(1)
            for half in range(2):
                for j in range(4):
                    r = 4 * half + j
                    act.wait_ge(acc_full, r + 1)
                    nc.scalar.activation(T.gqk[:, j, half * HALF:(half + 1) * HALF], acc[r % 4][:], ACT.Copy,
                                         scale=UNSCALE).then_inc(acc_free, 1)
            for c in range(1, len(COLS) - 1):
                split_w(c + 1)
                name = COLS[c][0]
                if name == "dv":
                    act.wait_ge(acc_free, BASE + first_result[c])
                with act.Fori(0, NT // 4) as i:
                    for b in range(4):
                        act.wait_ge(acc_full, first_result[c] + 4 * i + b + 1)
                        if name in gains:
                            n0 = 8 * (name == "dk")
                            nc.scalar.activation(sq[:, b % 2, :], acc[b][:], ACT.Square,
                                                 scale=UNSCALE * DIFF_DK ** -0.5).then_inc(head_sq, 1)
                            act.wait_ge(head_ss, n0 + 4 * i + b + 1)
                        else:
                            f = ACT.Silu if name == "gr" else ACT.Copy
                            nc.scalar.activation(dest[name][:, bass.ds(4 * i + b, 1), :].rearrange("p a n -> p (a n)"),
                                                 acc[b][:], f, scale=UNSCALE).then_inc(acc_free, 1)
            c = len(COLS) - 1
            for half in range(2):
                act.wait_ge(acc_full, first_result[c] + half + 1)
                nc.scalar.activation(T.ga[:, half * HALF:(half + 1) * HALF], acc[half][0:GLA_RANK, :], ACT.Copy,
                                     scale=UNSCALE).then_inc(acc_free, 1)

        @block.vector
        def _(dve):
            def split_w(c):
                n = COLS[c][2]
                for q in range(PIECES):
                    r = c * PIECES + q
                    dve.wait_ge(w_hi_done, r + 1)
                    for j in range(2):
                        k = 2 * q + j
                        last = nc.vector.scalar_tensor_tensor(w_lo[:, c % 2, k, 0:n], w_in[:, r % 2, j, 0:n],
                                                              T.g_mix[:, k:k + 1], w_hi[:, c % 2, k, 0:n], ALU.mult,
                                                              ALU.subtract)
                    last.then_inc(w_lo_done, 1)

            def scale(t):
                dve.wait_ge(rstd_done, t + 1)
                nc.vector.tensor_scalar(x_in[:, t % XR, :], x_in[:, t % XR, :], rstd[:, t:t + 1], None,
                                        ALU.mult).then_inc(normed, 1)

            scale(0)
            split_w(0)
            for t in range(NT):
                if t + 1 < NT:
                    scale(t + 1)
                dve.wait_ge(hi_done, t + 1)
                toks = slice(t * P, (t + 1) * P)
                nc.vector.scalar_tensor_tensor(T.act_lo[:, :, toks], turned[t % 2][:], S_ACT, T.act_hi[:, :, toks],
                                               ALU.mult, ALU.subtract).then_inc(lo_done, 1)
            for c in range(1, len(COLS)):
                split_w(c)
                if COLS[c - 1][0] not in gains:
                    continue
                name = COLS[c - 1][0]
                n0 = 8 * (name == "dk")
                g = gains[name]
                with dve.Fori(0, NT // 4) as i:
                    for b in range(4):
                        dve.wait_ge(head_sq, n0 + 4 * i + b + 1)
                        nc.vector.tensor_reduce(hss[:, b % 2, :], sq[:, b % 2, :].rearrange("p (h d) -> p h d", h=8),
                                                AX.X, ALU.add).then_inc(head_ss, 1)
                        dve.wait_ge(head_r, n0 + 4 * i + b + 1)
                        tile = dest[name][:, bass.ds(4 * i + b, 1), :].rearrange("p a (h d) -> p (a h) d", h=8)
                        nc.vector.scalar_tensor_tensor(tile, acc[b][:].rearrange("p (h d) -> p h d", h=8), UNSCALE,
                                                       lanes(hr[:, b % 2, :], 2, P, 8, DIFF_DK), ALU.mult,
                                                       ALU.mult).then_inc(acc_free, 1)
                        dve.wait_ge(acc_free, BASE + first_result[c - 1] + 4 * i + b + 1)
                        nc.vector.tensor_tensor(tile, tile, lanes(g[:], 1, P, 8, DIFF_DK),
                                                ALU.mult).then_inc(head_normed, 1)

        @block.tensor
        def _(pe):
            def turn(t):
                pe.wait_ge(normed, t + 1)
                if t >= 2:
                    pe.wait_ge(lo_done, t - 1)
                for k in range(KT):
                    last = pe.transpose(turned[t % 2][:, k, :], x_in[:, t % XR, k * P:(k + 1) * P], T.ident[:])
                last.then_inc(x_turned, 1)

            turns = iter(range(NT))
            for t in range(NT // 2 + 2):
                turn(next(turns))
            pe.wait_ge(lo_done, NT // 2)
            pe.wait_ge(w_lo_done, PIECES)
            pe.wait_ge(acc_free, BASE)
            for half in range(2):
                if half:
                    pe.wait_ge(lo_done, NT)
                toks = slice(half * HALF, (half + 1) * HALF)
                for j in range(4):
                    r = 4 * half + j
                    if r >= 4:
                        pe.wait_ge(acc_free, BASE + r - 3)
                    for k in range(KT):
                        last = split_mm(pe, acc[r % 4][:], w_hi[:, 0, k, j * P:(j + 1) * P],
                                        w_lo[:, 0, k, j * P:(j + 1) * P], T.act_hi[:, k, toks], T.act_lo[:, k, toks],
                                        k == 0, k == KT - 1)
                    last.then_inc(acc_full, 1)
                    for t in turns:
                        turn(t)
                        break
            for c in range(1, len(COLS) - 1):
                pe.wait_ge(w_lo_done, PIECES * (c + 1))
                with pe.Fori(0, NT // 4) as i:
                    for b in range(4):
                        pe.wait_ge(acc_free, BASE - 3 + first_result[c] + 4 * i + b)
                        toks = bass.ds(i * (4 * P) + b * P, P)
                        for k in range(KT):
                            last = split_mm(pe, acc[b][:], T.act_hi[:, k, toks], T.act_lo[:, k, toks],
                                            w_hi[:, c % 2, k, :], w_lo[:, c % 2, k, :], k == 0, k == KT - 1)
                        last.then_inc(acc_full, 1)
            c = len(COLS) - 1
            pe.wait_ge(w_lo_done, PIECES * (c + 1))
            for half in range(2):
                pe.wait_ge(acc_free, BASE - 3 + first_result[c] + half)
                toks = slice(half * HALF, (half + 1) * HALF)
                for k in range(KT):
                    last = split_mm(pe, acc[half][0:GLA_RANK, :], w_hi[:, c % 2, k, 0:GLA_RANK],
                                    w_lo[:, c % 2, k, 0:GLA_RANK], T.act_hi[:, k, toks], T.act_lo[:, k, toks],
                                    k == 0, k == KT - 1)
                last.then_inc(acc_full, 1)


NCH = SEQ // CHUNK


def gla_states(nc, io, T):
    with ExitStack() as ctx:
        S = Space(nc, ctx, "b")
        lent = [x[:].rearrange("p k t -> p (k t)").bitcast(F32).rearrange("p (a c t) -> p a c t", a=2, c=2)
                for x in (T.act_hi, T.act_lo)]
        z, cum, grow = lent[0][:, 0], lent[0][:, 1], lent[1][:, 0]
        ke_n = lent[1][:, 1].rearrange("p c t -> p (c t)").rearrange("p (t n) -> p t n", t=NT)
        soft = S.sb("soft", [P, 2, SEQ])
        keep = S.sb("keep", [P, SEQ])
        fall = S.sb("fall", [P, 2, SEQ])
        ke = S.sb("ke", [P, 2, SEQ])
        decay = S.sb("decay", [P, 2, NCH])
        gate = [S.ps(f"gate{c}", [P, SEQ]) for c in range(2)]
        turned = [S.ps(f"turned{b}", [P, 2, P]) for b in range(2)]
        kv = [S.ps(f"kv{c}", [P, 2, 2 * GLA_DV]) for c in range(2)]
        gate_done = S.sem("gate_done")
        vec_step = S.sem("vec_step")
        act_step = S.sem("act_step")
        keep_done = S.sem("keep_done")
        z_done = S.sem("z_done")
        soft_done = S.sem("soft_done")
        cum_done = S.sem("cum_done")
        fall_ready = S.sem("fall_ready")
        factor = S.sem("factor")
        ke_done = S.sem("ke_done")
        ke_turned = S.sem("ke_turned")
        ke_out = S.sem("ke_out")
        kv_done = S.sem("kv_done")
        state_done = S.sem("state_done")
        decay_done = S.sem("decay_done")
        block = ctx.enter_context(nc.Block())

        @block.gpsimd
        def _(pool):
            c = Chain(pool, keep_done)
            c.link(nc.gpsimd.memset(keep[:], 1.0))
            c.step(nc.gpsimd.memset(keep[:].rearrange("p (c s) -> p c s", s=CHUNK)[:, :, 0:1], 0.0))
            c.step(nc.gpsimd.memset(T.state[:, 0], 0.0))

        @block.tensor
        def _(pe):
            for ct in range(2):
                for half in range(2):
                    toks = slice(half * HALF, (half + 1) * HALF)
                    last = pe.matmul(gate[ct][:, toks], T.w_gate[:, ct * P:(ct + 1) * P], T.ga[:, toks],
                                     start=True, stop=True)
                last.then_inc(gate_done, 1)
            pe.wait_ge(ke_done, 2)
            for t in range(NT):
                if t >= 2:
                    pe.wait_ge(ke_out, t - 1)
                for ct in range(2):
                    last = pe.transpose(turned[t % 2][:, ct, :], ke[:, ct, t * P:(t + 1) * P], T.ident[:])
                last.then_inc(ke_turned, 1)
            for t in range(NT):
                pe.wait_ge(ke_out, t + 1)
                for c in range(2):
                    if t:
                        pe.wait_ge(state_done, 2 * t + c - 1)
                    rows = slice(c * CHUNK, (c + 1) * CHUNK)
                    for ct in range(2):
                        last = pe.matmul(kv[c][:, ct, :], ke_n[rows, t, ct * P:(ct + 1) * P],
                                         T.gv[rows, t, ct * 2 * GLA_DV:(ct + 1) * 2 * GLA_DV], start=True, stop=True)
                    last.then_inc(kv_done, 1)

        @block.scalar
        def _(act):
            c = Chain(act, act_step)
            for ct in range(2):
                act.wait_ge(z_done, ct + 1)
                c.link(nc.scalar.activation(soft[:, ct, :], z[:, ct, :], ACT.Abs))
                c.link(nc.scalar.activation(soft[:, ct, :], soft[:, ct, :], ACT.Exp, scale=-1.0))
                nc.scalar.activation(soft[:, ct, :], soft[:, ct, :], ACT.Ln, bias=1.0).then_inc(soft_done, 1)
            for ct in range(2):
                act.wait_ge(cum_done, ct + 1)
                nc.scalar.activation(grow[:, ct, :], cum[:, ct, :], ACT.Exp, scale=1.0 / GLA_TAU).then_inc(factor, 1)
                nc.scalar.activation(soft[:, ct, :], cum[:, ct, :], ACT.Exp, scale=-1.0 / GLA_TAU).then_inc(factor, 1)
                act.wait_ge(fall_ready, ct + 1)
                nc.scalar.activation(fall[:, ct, :], fall[:, ct, :], ACT.Exp, scale=1.0 / GLA_TAU).then_inc(factor, 1)
            for t in range(NT):
                act.wait_ge(ke_turned, t + 1)
                nc.scalar.activation(ke_n[:, t, :], turned[t % 2][:].rearrange("p a b -> p (a b)"),
                                     ACT.Copy).then_inc(ke_out, 1)

        @block.vector
        def _(dve):
            c = Chain(dve, vec_step)
            for ct in range(2):
                dve.wait_ge(gate_done, ct + 1)
                nc.vector.tensor_scalar(z[:, ct, :], gate[ct][:], T.b_gate[:, ct:ct + 1], None,
                                        ALU.add).then_inc(z_done, 1)
            gr = T.gr[:].rearrange("p t (h v) -> p (t h) v", v=GLA_DV)
            c.link(nc.vector.tensor_tensor(gr, gr, lanes(T.g_gla[:], 1, P, NT * GLA_H, GLA_DV), ALU.mult))
            dve.wait_ge(keep_done, 3)
            for ct in range(2):
                dve.wait_ge(soft_done, ct + 1)
                c.link(nc.vector.scalar_tensor_tensor(z[:, ct, :], z[:, ct, :], 0.0, soft[:, ct, :], ALU.min,
                                                      ALU.subtract))
                nc.vector.tensor_tensor_scan(cum[:, ct, :], keep[:], z[:, ct, :], 0.0, ALU.mult,
                                             ALU.add).then_inc(cum_done, 1)
                dve.wait_ge(cum_done, ct + 1)
                by_chunk = cum[:, ct, :].rearrange("p (c s) -> p c s", s=CHUNK)
                nc.vector.tensor_tensor(fall[:, ct, :].rearrange("p (c s) -> p c s", s=CHUNK),
                                        by_chunk[:, :, CHUNK - 1:CHUNK].broadcast_to([P, NCH, CHUNK]), by_chunk,
                                        ALU.subtract).then_inc(fall_ready, 1)
            for ct in range(2):
                dve.wait_ge(factor, 3 * ct + 3)
                q, k = T.gqk[:, ct, :], T.gqk[:, 2 + ct, :]
                c.step(nc.vector.scalar_tensor_tensor(q, grow[:, ct, :], GLA_DK ** -0.5, q, ALU.mult, ALU.mult))
                nc.vector.tensor_tensor(ke[:, ct, :], k, fall[:, ct, :], ALU.mult).then_inc(ke_done, 1)
                dve.wait_ge(ke_done, ct + 1)
                c.step(nc.vector.tensor_tensor(k, k, soft[:, ct, :], ALU.mult))
                nc.vector.tensor_copy(decay[:, ct, :], grow[:, ct, :].rearrange("p (c s) -> p c s", s=CHUNK)[:, :,
                                      CHUNK - 1]).then_inc(decay_done, 1)
            dve.wait_ge(decay_done, 2)
            for n in range(NCH - 1):
                dve.wait_ge(kv_done, n + 1)
                if n:
                    dve.wait_ge(state_done, n)
                for ct in range(2):
                    for hh in range(2):
                        r = slice(hh * GLA_DK, (hh + 1) * GLA_DK)
                        last = nc.vector.scalar_tensor_tensor(
                            T.state[r, n + 1, ct, :], T.state[r, n, ct, :], decay[r, ct, n:n + 1],
                            kv[n % 2][r, ct, hh * GLA_DV:(hh + 1) * GLA_DV], ALU.mult, ALU.add)
                last.then_inc(state_done, 1)


def by_parity(ap, hh):
    return ap.rearrange("p (c h v) -> p c h v", c=2, h=2)[:, :, hh, :]


def gla_outputs(nc, io, T):
    with ExitStack() as ctx:
        S = Space(nc, ctx, "g")
        att_m = S.sb("att_m", [P, 2, GLA_H, P])
        sq = S.sb("sq", [P, 2, HALF])
        ss = S.sb("ss", [P, NT, GLA_H])
        o_n = S.sb("o_n", [P, 2, GLA_H, GLA_DV])
        att = [[S.ps(f"att{b}{hh}", [P, 2, HALF // 2])[:, :, 0:P] for hh in range(2)] for b in range(2)]
        o = [S.ps(f"o{hh}", [P, 2, HALF // 2])[:, :, 0:GLA_DV] for hh in range(2)]
        turned = [S.ps(f"turned{b}", [P, GLA_H, P]) for b in range(2)]
        att_done = S.sem("att_done")
        masked = S.sem("masked")
        o_done = S.sem("o_done")
        squared = S.sem("squared")
        summed = S.sem("summed")
        pool_step = S.sem("pool_step")
        rstd_done = S.sem("rstd_done")
        o_out = S.sem("o_out")
        o_turned = S.sem("o_turned")
        hi_done = S.sem("hi_done")
        lo_done = S.sem("lo_done")
        block = ctx.enter_context(nc.Block())

        @block.gpsimd
        def _(pool):
            c = Chain(pool, pool_step)
            for t in range(NT):
                pool.wait_ge(summed, t + 1)
                c.link(nc.gpsimd.tensor_scalar(ss[:, t, :], ss[:, t, :], 1.0 / GLA_DV, EPS, ALU.mult, ALU.add))
                nc.gpsimd.tensor_tensor(ss[:, t, :], ss[:, t, :], T.mhalf[:, 0:GLA_H],
                                        ALU.pow).then_inc(rstd_done, 1)

        @block.tensor
        def _(pe):
            def scores(t):
                if t >= 2:
                    pe.wait_ge(masked, t - 1)
                for h in range(GLA_H):
                    r = slice((h % 2) * GLA_DK, (h % 2 + 1) * GLA_DK)
                    toks = slice(t * P, (t + 1) * P)
                    last = pe.matmul(att[t % 2][h % 2][:, h // 2, :], T.gqk[r, 2 + h // 2, toks], T.gqk[r, h // 2, toks],
                                     start=True, stop=True)
                last.then_inc(att_done, 1)

            def outputs(t):
                pe.wait_ge(masked, t + 1)
                if t:
                    pe.wait_ge(o_out, t)
                for h in range(GLA_H):
                    r = slice((h % 2) * GLA_DK, (h % 2 + 1) * GLA_DK)
                    last = pe.matmul(o[h % 2][:, h // 2, :], att_m[:, t % 2, h, :], T.gv[:, t, h * GLA_DV:(h + 1) * GLA_DV],
                                     start=True, stop=False)
                    for c in range(2):
                        toks = slice(t * P + c * CHUNK, t * P + (c + 1) * CHUNK)
                        last = pe.matmul(o[h % 2][c * CHUNK:(c + 1) * CHUNK, h // 2, :], T.gqk[r, h // 2, toks],
                                         T.state[r, 2 * t + c, h // 2, :], start=False, stop=True)
                last.then_inc(o_done, 1)

            def turn(t):
                pe.wait_ge(o_out, t + 1)
                if t >= 2:
                    pe.wait_ge(lo_done, t - 1)
                for h in range(GLA_H):
                    last = pe.transpose(turned[t % 2][:, h, :], o_n[:, t % 2, h, :], T.ident[:])
                last.then_inc(o_turned, 1)

            scores(0)
            for t in range(NT + 1):
                if t + 1 < NT:
                    scores(t + 1)
                if t < NT:
                    outputs(t)
                if t:
                    turn(t - 1)

        @block.scalar
        def _(act):
            for t in range(NT + 1):
                if t < NT:
                    act.wait_ge(o_done, t + 1)
                    if t >= 2:
                        act.wait_ge(summed, t - 1)
                    for hh in range(2):
                        last = nc.scalar.activation(by_parity(sq[:, t % 2, :], hh), o[hh], ACT.Square)
                    last.then_inc(squared, 1)
                if t:
                    act.wait_ge(o_turned, t)
                    nc.scalar.activation(T.act_hi[:, 0:GLA_H, (t - 1) * P:t * P], turned[(t - 1) % 2][:], ACT.Copy,
                                         scale=S_ACT).then_inc(hi_done, 1)

        @block.vector
        def _(dve):
            def mask(t):
                dve.wait_ge(att_done, t + 1)
                if t >= 2:
                    dve.wait_ge(o_done, t - 1)
                for hh in range(2):
                    last = nc.vector.tensor_tensor(by_parity(att_m[:, t % 2].rearrange("p h c -> p (h c)"), hh),
                                                   att[t % 2][hh], lanes(T.tri[:], 1, P, 2, P), ALU.mult)
                last.then_inc(masked, 1)

            mask(0)
            for t in range(NT + 1):
                if t + 1 < NT:
                    mask(t + 1)
                if t < NT:
                    dve.wait_ge(squared, t + 1)
                    nc.vector.tensor_reduce(ss[:, t, :], sq[:, t % 2, :].rearrange("p (h v) -> p h v", h=GLA_H), AX.X,
                                            ALU.add).then_inc(summed, 1)
                    dve.wait_ge(rstd_done, t + 1)
                    if t >= 2:
                        dve.wait_ge(o_turned, t - 1)
                    for h in range(GLA_H):
                        last = nc.vector.scalar_tensor_tensor(o_n[:, t % 2, h, :], o[h % 2][:, h // 2, :], ss[:, t, h:h + 1],
                                                              T.gr[:, t, h * GLA_DV:(h + 1) * GLA_DV], ALU.mult,
                                                              ALU.mult)
                    last.then_inc(o_out, 1)
                if t:
                    dve.wait_ge(hi_done, t)
                    toks = slice((t - 1) * P, t * P)
                    nc.vector.scalar_tensor_tensor(T.act_lo[:, 0:GLA_H, toks], turned[(t - 1) % 2][:], S_ACT,
                                                   T.act_hi[:, 0:GLA_H, toks], ALU.mult,
                                                   ALU.subtract).then_inc(lo_done, 1)


def diff_attention(nc, io, T):
    SCALE = DIFF_DK ** -0.5
    units = [(b, h) for b in range(NT) for h in range(DIFF_H)]
    with ExitStack() as ctx:
        S = Space(nc, ctx, "d")
        q_t = S.sb("q_t", [P, DIFF_H, SEQ])
        k_t = S.sb("k_t", [P, DIFF_H, SEQ])
        ident = S.sb("ident", [P, P], BF16)
        causal = S.sb("causal", [P, P], BF16)
        rot = S.sb("rot", [P, 4, NT, 8, HROPE])
        mx = S.sb("mx", [P, 2, 2])
        sums = S.sb("sums", [P, 2, 2])
        inv = S.sb("inv", [P, 2, 2])
        mix = S.sb("mix", [P, 2])
        e = S.sb("e", [P, 2, 2, SEQ])
        a = S.sb("a", [P, 2, SEQ])
        a_t = S.sb("a_t", [P, 2, SEQ])
        junk = S.sb("junk", [P, DIFF_DV])
        ss = S.sb("ss", [P, 2])
        o_s = S.sb("o_s", [P, 2, DIFF_DV])
        o_n = S.sb("o_n", [P, 2, DIFF_H, DIFF_DV])
        sc = [S.ps(f"sc{m}", [P, SEQ]) for m in range(2)]
        a_ps = S.ps("a_ps", [P, SEQ])
        o = S.ps("o", [P, DIFF_DV])
        turned = S.ps("turned", [P, DIFF_H, P])
        mask_ready = S.sem("mask_ready")
        rot_step = S.sem("rot_step")
        pool_rot = S.sem("pool_rot")
        roped = S.sem("roped")
        qk_turned = S.sem("qk_turned")
        qk_out = S.sem("qk_out")
        scored = [S.sem(f"scored{m}") for m in range(2)]
        max_done = [S.sem(f"max_done{m}") for m in range(2)]
        vec_step = S.sem("vec_step")
        exp_done = [S.sem(f"exp_done{m}") for m in range(2)]
        combined = S.sem("combined")
        a_turned = S.sem("a_turned")
        a_out = S.sem("a_out")
        o_done = S.sem("o_done")
        o_scaled = S.sem("o_scaled")
        squared = S.sem("squared")
        pool_step = S.sem("pool_step")
        rstd_done = S.sem("rstd_done")
        o_out = S.sem("o_out")
        o_turned = S.sem("o_turned")
        hi_done = S.sem("hi_done")
        lo_done = S.sem("lo_done")
        block = ctx.enter_context(nc.Block())

        def rope(eng, x, tmp, c):
            v = x[:].rearrange("p t (h d) -> p t h d", d=DIFF_DK)
            x1, x2 = v[:, :, :, 0:HROPE], v[:, :, :, HROPE:ROPE]
            shape = [P, NT, 8, HROPE]
            cos, sin = (w[:].unsqueeze(2).broadcast_to(shape) for w in (T.cos, T.sin))
            for n, (u, w) in enumerate(((x1, cos), (x2, sin), (x2, cos), (x1, sin))):
                c.step(eng.tensor_tensor(tmp[n], u, w, ALU.mult))
            c.wait()
            c.step(eng.tensor_tensor(x1, tmp[0], tmp[1], ALU.subtract))
            return eng.tensor_tensor(x2, tmp[2], tmp[3], ALU.add)

        @block.gpsimd
        def _(pool):
            nc.gpsimd.tensor_copy(ident[:], T.ident[:]).then_inc(mask_ready, 1)
            nc.gpsimd.tensor_copy(causal[:], T.causal[:]).then_inc(mask_ready, 1)
            c = Chain(pool, pool_step)
            for u in range(len(units)):
                pool.wait_ge(squared, u + 1)
                s = ss[:, u % 2:u % 2 + 1]
                c.link(nc.gpsimd.tensor_scalar(s, s, 1.0 / DIFF_DV, EPS, ALU.mult, ALU.add))
                nc.gpsimd.tensor_tensor(s, s, T.mhalf[:, 0:1], ALU.pow).then_inc(rstd_done, 1)

        @block.tensor
        def _(pe):
            pe.wait_ge(mask_ready, 2)
            pe.wait_ge(roped, 2)
            n = 0
            for t in range(NT):
                for x in (T.dq, T.dk):
                    if n:
                        pe.wait_ge(qk_out, n)
                    for h in range(DIFF_H):
                        last = pe.transpose(turned[:, h, :], x[:, t, h * P:(h + 1) * P], T.ident[:])
                    last.then_inc(qk_turned, 1)
                    n += 1
            pe.wait_ge(qk_out, n)

            def scores(u, m):
                b, h = units[u]
                keys = (b + 1) * P
                if u:
                    pe.wait_ge(exp_done[m], u)
                r = slice(m * DIFF_DK, (m + 1) * DIFF_DK)
                for k0 in range(0, keys, HALF):
                    k1 = min(keys, k0 + HALF)
                    pe.matmul(sc[m][:, k0:k1], q_t[r, h, b * P:(b + 1) * P], k_t[r, h, k0:k1], start=True,
                              stop=(k1 < keys))
                pe.matmul(sc[m][:, b * P:keys], ident[:], causal[:], start=False, stop=True).then_inc(scored[m], 1)

            def turn_probs(u):
                b, h = units[u]
                pe.wait_ge(combined, u + 1)
                if u:
                    pe.wait_ge(a_out, u)
                for kb in range(b + 1):
                    last = pe.transpose(a_ps[:, kb * P:(kb + 1) * P], a[:, u % 2, kb * P:(kb + 1) * P], T.ident[:])
                last.then_inc(a_turned, 1)

            def values(u):
                b, h = units[u]
                pe.wait_ge(a_out, u + 1)
                if u:
                    pe.wait_ge(o_scaled, u)
                for kb in range(b + 1):
                    last = pe.matmul(o[:], a_t[:, u % 2, kb * P:(kb + 1) * P], T.dv[:, kb, h * DIFF_DV:(h + 1) * DIFF_DV],
                                     start=(kb == 0), stop=(kb == b))
                last.then_inc(o_done, 1)

            def turn(b):
                pe.wait_ge(o_out, DIFF_H * (b + 1))
                if b:
                    pe.wait_ge(lo_done, b)
                for h in range(DIFF_H):
                    last = pe.transpose(turned[:, h, :], o_n[:, b % 2, h, :], T.ident[:])
                last.then_inc(o_turned, 1)

            for m in range(2):
                scores(0, m)
            for u, (b, h) in enumerate(units):
                more = u + 1 < len(units)
                if more:
                    scores(u + 1, 0)
                turn_probs(u)
                if more:
                    scores(u + 1, 1)
                values(u)
                if h == 1 and b:
                    turn(b - 1)
            turn(NT - 1)

        @block.scalar
        def _(act):
            n = 0
            for t in range(NT):
                for x in (q_t, k_t):
                    act.wait_ge(qk_turned, n + 1)
                    nc.scalar.activation(x[:, :, t * P:(t + 1) * P], turned[:], ACT.Copy).then_inc(qk_out, 1)
                    n += 1

            def exps(u, m):
                b, h = units[u]
                act.wait_ge(max_done[m], u + 1)
                if u >= 2:
                    act.wait_ge(combined, u - 1)
                nc.scalar.activation(e[:, u % 2, m, 0:(b + 1) * P], sc[m][:, 0:(b + 1) * P], ACT.Exp,
                                     bias=mx[:, u % 2, m:m + 1], scale=SCALE,
                                     accum_out=sums[:, u % 2, m:m + 1]).then_inc(exp_done[m], 1)

            def probs_out(u):
                b, h = units[u]
                act.wait_ge(a_turned, u + 1)
                if u >= 2:
                    act.wait_ge(o_done, u - 1)
                nc.scalar.activation(a_t[:, u % 2, 0:(b + 1) * P], a_ps[:, 0:(b + 1) * P], ACT.Copy).then_inc(a_out, 1)

            def output(u):
                act.wait_ge(o_done, u + 1)
                if u >= 2:
                    act.wait_ge(o_out, u - 1)
                nc.scalar.activation(o_s[:, u % 2, :], o[:], ACT.Copy, scale=inv[:, u % 2, 0:1]).then_inc(o_scaled, 1)
                act.wait_ge(o_scaled, u + 1)
                if u:
                    act.wait_ge(squared, u)
                nc.scalar.activation(junk[:], o_s[:, u % 2, :], ACT.Square,
                                     accum_out=ss[:, u % 2:u % 2 + 1]).then_inc(squared, 1)

            def turned_hi(b):
                act.wait_ge(o_turned, b + 1)
                nc.scalar.activation(T.act_hi[:, DIFF_H:2 * DIFF_H, b * P:(b + 1) * P], turned[:], ACT.Copy,
                                     scale=T.g_sub[:, 0:1]).then_inc(hi_done, 1)

            for m in range(2):
                exps(0, m)
            for u, (b, h) in enumerate(units):
                probs_out(u)
                if u + 1 < len(units):
                    for m in range(2):
                        exps(u + 1, m)
                output(u)
                if h == 1 and b:
                    turned_hi(b - 1)
            turned_hi(NT - 1)

        @block.vector
        def _(dve):
            c = Chain(dve, rot_step)
            rope(nc.vector, T.dq, [rot[:, n] for n in range(4)], c).then_inc(roped, 1)
            dve.wait_ge(roped, 1)
            rope(nc.vector, T.dk, [rot[:, n] for n in range(4)], c).then_inc(roped, 1)
            c = Chain(dve, vec_step)

            def maximum(u, m):
                b, h = units[u]
                dve.wait_ge(scored[m], u + 1)
                if u >= 2:
                    dve.wait_ge(exp_done[m], u - 1)
                c.link(nc.vector.tensor_reduce(mx[:, u % 2, m:m + 1], sc[m][:, 0:(b + 1) * P], AX.X, ALU.max))
                nc.vector.tensor_scalar(mx[:, u % 2, m:m + 1], mx[:, u % 2, m:m + 1], -SCALE, None,
                                        ALU.mult).then_inc(max_done[m], 1)

            def combine(u):
                b, h = units[u]
                for m in range(2):
                    dve.wait_ge(exp_done[m], u + 1)
                if u >= 2:
                    dve.wait_ge(o_scaled, u - 1)
                    dve.wait_ge(a_turned, u - 1)
                c.link(nc.vector.reciprocal(inv[:, u % 2, :], sums[:, u % 2, :]))
                c.link(nc.vector.scalar_tensor_tensor(mix[:, u % 2:u % 2 + 1], inv[:, u % 2, 1:2], sums[:, u % 2, 0:1],
                                                      T.neg_lam[:], ALU.mult, ALU.mult))
                nc.vector.scalar_tensor_tensor(a[:, u % 2, 0:(b + 1) * P], e[:, u % 2, 1, 0:(b + 1) * P],
                                               mix[:, u % 2:u % 2 + 1], e[:, u % 2, 0, 0:(b + 1) * P], ALU.mult,
                                               ALU.add).then_inc(combined, 1)

            def norm(u):
                b, h = units[u]
                dve.wait_ge(rstd_done, u + 1)
                if h == 0 and b >= 2:
                    dve.wait_ge(o_turned, b - 1)
                nc.vector.tensor_scalar(o_n[:, b % 2, h, :], o_s[:, u % 2, :], ss[:, u % 2:u % 2 + 1], None,
                                        ALU.mult).then_inc(o_out, 1)

            def turned_lo(b):
                dve.wait_ge(hi_done, b + 1)
                toks = slice(b * P, (b + 1) * P)
                nc.vector.scalar_tensor_tensor(T.act_lo[:, DIFF_H:2 * DIFF_H, toks], turned[:], T.g_sub[:, 0:1],
                                               T.act_hi[:, DIFF_H:2 * DIFF_H, toks], ALU.mult,
                                               ALU.subtract).then_inc(lo_done, 1)

            for m in range(2):
                maximum(0, m)
            for u, (b, h) in enumerate(units):
                combine(u)
                if u + 1 < len(units):
                    for m in range(2):
                        maximum(u + 1, m)
                if u:
                    norm(u - 1)
                if h == 1 and b:
                    turned_lo(b - 1)
            norm(len(units) - 1)
            turned_lo(NT - 1)


def project_out(nc, io, T):
    with ExitStack() as ctx:
        S = Space(nc, ctx, "o")
        w_in = S.sb("w_in", [P, 2, D])
        w_hi = S.sb("w_hi", [P, KT, D], F16)
        w_lo = S.sb("w_lo", [P, KT, D], F16)
        x_in = S.sb("x_in", [P, 2, D])
        xs = S.sb("xs", [P, 2, D])
        junk = S.sb("junk", [P, D], F16)
        ss = S.sb("ss", [P, NT])
        acc = [S.ps(f"acc{b}", [P, D]) for b in range(2)]
        turned = [S.ps(f"turned{b}", [P, KT, P]) for b in range(2)]
        w_loaded = [S.sem(f"w_loaded{b}") for b in range(2)]
        x_loaded = [S.sem(f"x_loaded{b}") for b in range(2)]
        w_hi_done = S.sem("w_hi_done")
        w_lo_done = S.sem("w_lo_done")
        acc_done = S.sem("acc_done")
        h_done = S.sem("h_done")
        squared = S.sem("squared")
        pool_step = S.sem("pool_step")
        rstd_done = S.sem("rstd_done")
        normed = S.sem("normed")
        x_turned = S.sem("x_turned")
        hi_done = S.sem("hi_done")
        lo_done = S.sem("lo_done")
        block = ctx.enter_context(nc.Block())

        @block.sync
        def _(sp):
            for k in range(KT):
                if k >= 2:
                    sp.wait_ge(w_lo_done, k - 1)
                sp.dma_start(w_in[:, k % 2, :], io.w_out[0, k * P:(k + 1) * P, :]).then_inc(w_loaded[k % 2], 16)
            for t in range(NT):
                if t >= 2:
                    sp.wait_ge(h_done, t - 1)
                sp.dma_start(x_in[:, t % 2, :], io.x[0, t * P:(t + 1) * P, :]).then_inc(x_loaded[t % 2], 16)

        @block.gpsimd
        def _(pool):
            c = Chain(pool, pool_step)
            for t in range(NT):
                pool.wait_ge(squared, t + 1)
                c.link(nc.gpsimd.tensor_scalar(ss[:, t:t + 1], ss[:, t:t + 1], 1.0 / D, EPS, ALU.mult, ALU.add))
                nc.gpsimd.tensor_tensor(ss[:, t:t + 1], ss[:, t:t + 1], T.mhalf[:, 0:1], ALU.pow).then_inc(rstd_done, 1)

        @block.tensor
        def _(pe):
            def project(t):
                if t >= 2:
                    pe.wait_ge(h_done, t - 1)
                toks = slice(t * P, (t + 1) * P)
                for k in range(KT):
                    if t == 0:
                        pe.wait_ge(w_lo_done, k + 1)
                    for half in range(2):
                        cols = slice(half * HALF, (half + 1) * HALF)
                        last = split_mm(pe, acc[t % 2][:, cols], T.act_hi[:, k, toks], T.act_lo[:, k, toks],
                                        w_hi[:, k, cols], w_lo[:, k, cols], k == 0, k == KT - 1)
                last.then_inc(acc_done, 1)

            def turn(t):
                pe.wait_ge(normed, t + 1)
                if t >= 2:
                    pe.wait_ge(lo_done, t - 1)
                for k in range(KT):
                    last = pe.transpose(turned[t % 2][:, k, :], xs[:, t % 2, k * P:(k + 1) * P], T.ident[:])
                last.then_inc(x_turned, 1)

            project(0)
            for t in range(NT):
                if t + 1 < NT:
                    project(t + 1)
                turn(t)

        @block.scalar
        def _(act):
            for k in range(KT):
                act.wait_ge(w_loaded[k % 2], 16 * (k // 2 + 1))
                nc.scalar.activation(w_hi[:, k, :], w_in[:, k % 2, :], ACT.Copy, scale=S_W).then_inc(w_hi_done, 1)
            for t in range(NT + 1):
                if t < NT:
                    act.wait_ge(h_done, t + 1)
                    if t:
                        act.wait_ge(squared, t)
                    nc.scalar.activation(junk[:], T.h[:, t, :], ACT.Square,
                                         accum_out=ss[:, t:t + 1]).then_inc(squared, 1)
                if t:
                    act.wait_ge(x_turned, t)
                    for k in range(KT):
                        last = nc.scalar.activation(T.act_hi[:, k, (t - 1) * P:t * P], turned[(t - 1) % 2][:, k, :],
                                                    ACT.Copy, scale=T.g_ffn[:, k:k + 1])
                    last.then_inc(hi_done, 1)

        @block.vector
        def _(dve):
            for k in range(KT):
                dve.wait_ge(w_hi_done, k + 1)
                nc.vector.scalar_tensor_tensor(w_lo[:, k, :], w_in[:, k % 2, :], S_W, w_hi[:, k, :], ALU.mult,
                                               ALU.subtract).then_inc(w_lo_done, 1)
            for t in range(NT + 1):
                if t < NT:
                    dve.wait_ge(acc_done, t + 1)
                    dve.wait_ge(x_loaded[t % 2], 16 * (t // 2 + 1))
                    nc.vector.scalar_tensor_tensor(T.h[:, t, :], acc[t % 2][:], UNSCALE, x_in[:, t % 2, :], ALU.mult,
                                                   ALU.add).then_inc(h_done, 1)
                    dve.wait_ge(rstd_done, t + 1)
                    if t >= 2:
                        dve.wait_ge(x_turned, t - 1)
                    nc.vector.tensor_scalar(xs[:, t % 2, :], T.h[:, t, :], ss[:, t:t + 1], None,
                                            ALU.mult).then_inc(normed, 1)
                if t:
                    dve.wait_ge(hi_done, t)
                    toks = slice((t - 1) * P, t * P)
                    for k in range(KT):
                        last = nc.vector.scalar_tensor_tensor(T.act_lo[:, k, toks], turned[(t - 1) % 2][:, k, :],
                                                              T.g_ffn[:, k:k + 1], T.act_hi[:, k, toks], ALU.mult,
                                                              ALU.subtract)
                    last.then_inc(lo_done, 1)


S_U = 64.0
EARLY_R = 2
EARLY_S = 3
BLOCK = 64
NBLOCK = SEQ // BLOCK
TB = 32
NTB = SEQ // TB
N_EARLY = EARLY_R * PEER_H + EARLY_S * NBLOCK


class EarlyTiles:

    def __init__(self, nc, io, T, S, ring, first, count):
        self.nc, self.T, self.ring = nc, T, ring
        rows = io.peer_u[0, first * P:(first + count) * P, :]
        self.u_rows = rows.rearrange("(c b p) d -> c b p d", b=ring, p=P)
        self.kept_rows = T.kept[first * P:(first + count) * P, :].rearrange("(c b p) t -> c b p t", b=ring, p=P)
        self.u_in = [S.sb(f"u_in{b}", [P, D]) for b in range(ring)]
        self.u_hi = [S.sb(f"u_hi{b}", [P, KT, P], F16) for b in range(ring)]
        self.u_lo = [S.sb(f"u_lo{b}", [P, KT, P], F16) for b in range(ring)]
        self.u_all = S.sb("u_all", [P, KT, P])
        self.gel = [S.sb(f"gel{b}", [P, SEQ]) for b in range(ring)]
        self.u_ps = S.ps("u_ps", [P, KT, P])
        self.hid = [S.ps(f"hid{b}", [P, HALF]) for b in range(2)]
        self.u_loaded = [S.sem(f"u_loaded{b}") for b in range(ring)]
        self.u_turned = S.sem("u_turned")
        self.u_hi_done = S.sem("u_hi_done")
        self.u_all_done = S.sem("u_all_done")
        self.u_lo_done = S.sem("u_lo_done")
        self.hid_done = S.sem("hid_done")
        self.gelu_done = S.sem("gelu_done")
        self.kept = [S.sem(f"kept{b}") for b in range(ring)]

    def prime_tensor(self, pe):
        pe.sem_inc(self.hid_done, BASE)

    def prime_scalar(self, act):
        act.sem_inc(self.u_all_done, BASE)
        act.sem_inc(self.gelu_done, BASE)
        for b in range(self.ring):
            act.sem_inc(self.kept[b], BASE)

    def prime_gpsimd(self, pool):
        pool.sem_inc(self.u_lo_done, BASE)

    def load(self, sp, c, b, again=True):
        if again:
            sp.wait_ge(self.u_turned, (c - 1) * self.ring + b + 1)
        sp.dma_start(self.u_in[b][:], self.u_rows[c, b]).then_inc(self.u_loaded[b], 16)

    def keep(self, sp, c, b):
        sp.wait_ge(self.gelu_done, BASE + 2 * (c * self.ring + b) + 2)
        sp.dma_start(self.kept_rows[c, b], self.gel[b][:]).then_inc(self.kept[b], 16)

    def all_kept(self, sp, count):
        for b in range(self.ring):
            sp.wait_ge(self.kept[b], BASE + 16 * (count // self.ring))

    def turn(self, pe, c, b):
        pe.wait_ge(self.u_loaded[b], c * 16 + 16)
        pe.wait_ge(self.u_all_done, BASE + c * self.ring + b)
        for k in range(KT):
            last = pe.transpose(self.u_ps[:, k, :], self.u_in[b][:, k * P:(k + 1) * P], self.T.ident[:])
        last.then_inc(self.u_turned, 1)

    def split(self, act, c, b):
        n = c * self.ring + b
        act.wait_ge(self.u_turned, n + 1)
        act.wait_ge(self.hid_done, BASE + 2 * (n - self.ring) + 2)
        self.nc.scalar.activation(self.u_hi[b][:], self.u_ps[:], ACT.Copy, scale=S_U).then_inc(self.u_hi_done, 1)
        act.wait_ge(self.u_lo_done, BASE + n)
        self.nc.scalar.activation(self.u_all[:], self.u_ps[:], ACT.Copy, scale=S_U).then_inc(self.u_all_done, 1)

    def low(self, pool, c, b):
        n = c * self.ring + b
        pool.wait_ge(self.u_hi_done, n + 1)
        pool.wait_ge(self.u_all_done, BASE + n + 1)
        self.nc.gpsimd.tensor_tensor(self.u_lo[b][:], self.u_all[:], self.u_hi[b][:],
                                     ALU.subtract).then_inc(self.u_lo_done, 1)

    def hidden(self, pe, c, b, half):
        n = c * self.ring + b
        if half == 0:
            pe.wait_ge(self.u_lo_done, BASE + n + 1)
        pe.wait_ge(self.gelu_done, BASE + 2 * (n - 1) + half + 1)
        toks = slice(half * HALF, (half + 1) * HALF)
        for k in range(KT):
            last = split_mm(pe, self.hid[half][:], self.u_hi[b][:, k, :], self.u_lo[b][:, k, :],
                            self.T.act_hi[:, k, toks], self.T.act_lo[:, k, toks], k == 0, k == KT - 1)
        last.then_inc(self.hid_done, 1)

    def gelu(self, act, c, b, half):
        n = c * self.ring + b
        if half == 0:
            act.wait_ge(self.kept[b], BASE + 16 * c)
        act.wait_ge(self.hid_done, BASE + 2 * n + half + 1)
        self.nc.scalar.activation(self.gel[b][:, half * HALF:(half + 1) * HALF], self.hid[half][:], ACT.Gelu,
                                  scale=1.0 / (S_U * S_ACT)).then_inc(self.gelu_done, 1)


NSET = 2 * PEER_H
FLOOR = -3.0e38


def retrieve(nc, io, T):
    with ExitStack() as ctx:
        S = Space(nc, ctx, "r")
        E = EarlyTiles(nc, io, T, S, EARLY_R, 0, EARLY_R * PEER_H)
        w_in = S.sb("w_in", [P, KT, QDIM])
        w_hi = [S.sb(f"w_hi{b}", [P, KT, QDIM], F16) for b in range(2)]
        w_lo = [S.sb(f"w_lo{b}", [P, KT, QDIM], F16) for b in range(2)]
        keys_t = S.sb("keys_t", [P, NSET, P])
        q_t = S.sb("q_t", [P, 2, SEQ])
        s = T.picked_all[:, 0:2 * SEQ].rearrange("p (t m k) -> p t m k", t=NT, m=2)
        s2 = S.sb("s2", [P, NT, 2, NKEYS])
        keys = s2[:].rearrange("p t m k -> p (t m) k")
        top = S.sb("top", [P, NT, 2, TOPK])
        top_i = S.sb("top_i", [P, NT, 2, TOPK], U32)
        top_f = S.sb("top_f", [P, 2, NT, 2, TOPK], F16)
        cand = S.sb("cand", [P, NT, TOPK * TOPK])
        cand2 = s2[:].rearrange("p t m k -> p t (m k)")
        best = S.sb("best", [P, NT, TOPK])
        pos = S.sb("pos", [P, NT * TOPK], U32)
        part = S.sb("part", [P, 2, NT * TOPK], U32)
        part_f = S.sb("part_f", [P, 2, NT * TOPK], F16)
        weight = S.sb("weight", [P, NT, TOPK])
        total = S.sb("total", [P, NT])
        carrier = S.sb("carrier", [1, 1])
        match = S.sb("match", [P, 2, NT * TOPK, TOPK], F16)
        picked = [S.sb(f"picked{n}", [P, NT, PICKS]) for n in range(3)]
        bank = [S.ps(f"bank{r}", [P, 4, NKEYS]) for r in range(4)]

        w_loaded = S.sem("w_loaded")
        keys_loaded = S.sem("keys_loaded")
        w_scaled = S.sem("w_scaled")
        w_hi_done = S.sem("w_hi_done")
        w_lo_done = S.sem("w_lo_done")
        keys_turned = S.sem("keys_turned")
        keys_out = S.sem("keys_out")
        q_done = S.sem("q_done")
        q_out = S.sem("q_out")
        scored = S.sem("scored")
        s_out = S.sem("s_out")
        vec_step = S.sem("vec_step")
        s_used = S.sem("s_used")
        shifted = S.sem("shifted")
        weighted = S.sem("weighted")
        found = S.sem("found")
        matched = S.sem("matched")
        index_done = S.sem("index_done")
        weight_done = S.sem("weight_done")
        all_turned = S.sem("all_turned")
        all_out = S.sem("all_out")
        block = ctx.enter_context(nc.Block())
        PAIRS = PEER_H // 2

        @block.sync
        def _(sp):
            w_v = io.w_peer_q[0].rearrange("(k p) (h c) -> h p k c", p=P, c=QDIM)

            def load_w(h):
                sp.dma_start(w_in[:], w_v[h]).then_inc(w_loaded, 16)

            def step(hh, b, last):
                h = 2 * hh + b
                if not last:
                    sp.wait_ge(w_lo_done, h + 2)
                    load_w(h + 2)
                for r in range(EARLY_R):
                    E.keep(sp, h, r)
                    if not (last and b):
                        E.load(sp, h + 1, r)

            load_w(0)
            sp.dma_start(keys, io.peer_sub_keys[0].rearrange("h m k q -> k (h m) q")).then_inc(keys_loaded, 16)
            for r in range(EARLY_R):
                E.load(sp, 0, r, again=False)
            sp.wait_ge(w_lo_done, 1)
            load_w(1)
            with sp.Fori(0, PAIRS - 1) as hh:
                for b in range(2):
                    step(hh, b, False)
            for b in range(2):
                step(PAIRS - 1, b, True)
            E.all_kept(sp, EARLY_R * PEER_H)

        @block.tensor
        def _(pe):
            E.prime_tensor(pe)

            def queries(h, slot, first=False):
                pe.wait_ge(w_lo_done, h + 1)
                for r in range(4):
                    m, half = r // 2, r % 2
                    if first:
                        pe.wait_ge(keys_out, r + 1)
                    else:
                        pe.wait_ge(s_out, 4 * (h - 1) + r + 1)
                    toks, cols = slice(half * HALF, (half + 1) * HALF), slice(m * P, (m + 1) * P)
                    for k in range(KT):
                        last = split_mm(pe, bank[r][:].rearrange("p a b -> p (a b)"), w_hi[slot][:, k, cols],
                                        w_lo[slot][:, k, cols], T.act_hi[:, k, toks], T.act_lo[:, k, toks],
                                        k == 0, k == KT - 1)
                    last.then_inc(q_done, 1)

            def scores(h):
                for m in range(2):
                    pe.wait_ge(q_out, 4 * h + 2 * m + 2)
                    for g in range(2):
                        for j in range(4):
                            t = 4 * g + j
                            last = pe.matmul(bank[2 * m + g][:, j, :], q_t[:, m, t * P:(t + 1) * P],
                                             keys_t[:, bass.ds(2 * h + m, 1), :].rearrange("p a k -> p (a k)"),
                                             start=True, stop=True)
                        last.then_inc(scored, 1)

            def step(hh, b, last):
                h = 2 * hh + b
                E.turn(pe, h, 0)
                if not (last and b):
                    queries(h + 1, 1 - b)
                    scores(h + 1)
                E.hidden(pe, h, 0, 0)
                E.turn(pe, h, 1)
                E.hidden(pe, h, 0, 1)
                E.hidden(pe, h, 1, 0)
                E.hidden(pe, h, 1, 1)

            pe.wait_ge(keys_loaded, 16)
            for r in range(4):
                for j in range(4):
                    last = pe.transpose(bank[r][:, j, :], keys[:, 4 * r + j, :], T.ident[:])
                last.then_inc(keys_turned, 1)
            queries(0, 0, first=True)
            scores(0)
            with pe.Fori(0, PAIRS - 1) as hh:
                for b in range(2):
                    step(hh, b, False)
            for b in range(2):
                step(PAIRS - 1, b, True)
            pe.wait_ge(index_done, BASE + 2 * PEER_H)
            pe.wait_ge(weight_done, PEER_H)
            for n in range(3):
                for g in range(2):
                    r = 2 * n + g
                    if r >= 4:
                        pe.wait_ge(all_out, r - 3)
                    for j in range(4):
                        last = pe.transpose(bank[r % 4][:, j, :], picked[n][:, 4 * g + j, :], T.ident[:])
                    last.then_inc(all_turned, 1)

        @block.scalar
        def _(act):
            E.prime_scalar(act)

            def split_w(h, slot):
                act.wait_ge(w_loaded, 16 * h + 16)
                nc.scalar.activation(w_in[:], w_in[:], ACT.Copy, scale=S_W).then_inc(w_scaled, 1)
                act.wait_ge(w_scaled, h + 1)
                nc.scalar.activation(w_hi[slot][:], w_in[:], ACT.Copy).then_inc(w_hi_done, 1)

            def queries_out(h):
                for r in range(4):
                    m, half = r // 2, r % 2
                    act.wait_ge(q_done, 4 * h + r + 1)
                    nc.scalar.activation(q_t[:, m, half * HALF:(half + 1) * HALF],
                                         bank[r][:].rearrange("p a b -> p (a b)"), ACT.Copy,
                                         scale=UNSCALE).then_inc(q_out, 1)

            def scores_out(h, first=False):
                if not first:
                    act.wait_ge(s_used, h)
                for m in range(2):
                    for g in range(2):
                        act.wait_ge(scored, 4 * h + 2 * m + g + 1)
                        nc.scalar.activation(s[:, 4 * g:4 * g + 4, m, :], bank[2 * m + g][:],
                                             ACT.Copy).then_inc(s_out, 1)

            def step(hh, b, last):
                h = 2 * hh + b
                E.split(act, h, 0)
                if not last:
                    split_w(h + 2, b)
                if not (last and b):
                    act.wait_ge(scored, 4 * h + 4)
                    queries_out(h + 1)
                    scores_out(h + 1)
                E.gelu(act, h, 0, 0)
                E.split(act, h, 1)
                E.gelu(act, h, 0, 1)
                act.wait_ge(shifted, h + 1)
                nc.scalar.activation(weight[:], weight[:], ACT.Exp).then_inc(weighted, 1)
                E.gelu(act, h, 1, 0)
                E.gelu(act, h, 1, 1)

            split_w(0, 0)
            for r in range(4):
                act.wait_ge(keys_turned, r + 1)
                nc.scalar.activation(keys_t[:, 4 * r:4 * r + 4, :], bank[r][:], ACT.Copy).then_inc(keys_out, 1)
            split_w(1, 1)
            queries_out(0)
            scores_out(0, first=True)
            with act.Fori(0, PAIRS - 1) as hh:
                for b in range(2):
                    step(hh, b, False)
            for b in range(2):
                step(PAIRS - 1, b, True)
            for r in range(6):
                act.wait_ge(all_turned, r + 1)
                n, g = r // 2, r % 2
                nc.scalar.activation(T.picked_t[n][:, g * HALF:(g + 1) * HALF], bank[r % 4][:].rearrange(
                    "p a b -> p (a b)"), ACT.Copy).then_inc(all_out, 1)

        @block.gpsimd
        def _(pool):
            E.prime_gpsimd(pool)

            def low_w(h, slot):
                pool.wait_ge(w_hi_done, h + 1)
                nc.gpsimd.tensor_tensor(w_lo[slot][:], w_in[:], w_hi[slot][:], ALU.subtract).then_inc(w_lo_done, 1)

            def step(hh, b, last):
                h = 2 * hh + b
                E.low(pool, h, 0)
                if not last:
                    low_w(h + 2, b)
                E.low(pool, h, 1)
                for n in range(2):
                    pool.wait_ge(found, 2 * h + n + 1)
                    got = match[:, n].rearrange("p (t k) a -> p t k a", t=NT)
                    nc.gpsimd.tensor_tensor(got, got, top_f[:, b, :, n, :].unsqueeze(2).broadcast_to(
                        [P, NT, TOPK, TOPK]), ALU.mult).then_inc(matched, 1)

            for h in range(2):
                low_w(h, h)
            with pool.Fori(0, PAIRS - 1) as hh:
                for b in range(2):
                    step(hh, b, False)
            for b in range(2):
                step(PAIRS - 1, b, True)

        @block.vector
        def _(dve):
            dve.sem_inc(index_done, BASE)
            def top16(c, values, rest, out, idx):
                def settled():
                    c.wait()
                    c.step(nc.vector.tensor_copy(carrier[:], T.iota[0:1, 0:1]))

                settled()
                for v, o in zip(values, out):
                    c.step(nc.vector.max(o[:, 0:8], v))
                settled()
                for v, w, o, i in zip(values, rest, out, idx):
                    c.step(nc.vector.max_index(i[:, 0:8], o[:, 0:8], v))
                    c.step(nc.vector.match_replace(w, o[:, 0:8], v, FLOOR))
                settled()
                for w, o in zip(rest, out):
                    c.step(nc.vector.max(o[:, 8:16], w))
                settled()
                for w, o, i in zip(rest, out, idx):
                    c.step(nc.vector.max_index(i[:, 8:16], o[:, 8:16], w))
                c.wait()

            def index_sum(h, n):
                dve.wait_ge(matched, 2 * h + n + 1)
                out = picked[n][:, :, bass.ds(h * TOPK, TOPK)]
                nc.vector.tensor_reduce(out, match[:, n].rearrange("p (t k) a -> p t k a", t=NT), AX.X,
                                        ALU.add).then_inc(index_done, 1)

            STEPS = 134
            with dve.Fori(0, PEER_H // 2) as hh:
                for b in range(2):
                    h = 2 * hh + b
                    c = Chain(dve, vec_step, STEPS * h)
                    both = [(t, m) for t in range(NT) for m in range(2)]
                    dve.wait_ge(s_out, 4 * h + 4)
                    top16(c, [s[:, t, m, :] for t, m in both], [s2[:, t, m, :] for t, m in both],
                          [top[:, t, m, :] for t, m in both], [top_i[:, t, m, :] for t, m in both])
                    nc.vector.tensor_copy(top_f[:, b], top_i[:]).then_inc(s_used, 1)
                    c.step(nc.vector.tensor_tensor(
                        cand[:].rearrange("p t (a b) -> p t a b", a=TOPK),
                        top[:, :, 0, :].unsqueeze(3).broadcast_to([P, NT, TOPK, TOPK]),
                        top[:, :, 1, :].unsqueeze(2).broadcast_to([P, NT, TOPK, TOPK]), ALU.add))
                    c.wait()
                    tiles = range(NT)
                    top16(c, [cand[:, t, :] for t in tiles], [cand2[:, t, :] for t in tiles],
                          [best[:, t, :] for t in tiles], [pos[:, t * TOPK:(t + 1) * TOPK] for t in tiles])
                    c.step(nc.vector.tensor_scalar(part[:, 0, :], pos[:], 4, None, ALU.logical_shift_right))
                    c.step(nc.vector.tensor_scalar(part[:, 1, :], pos[:], TOPK - 1, None, ALU.bitwise_and))
                    nc.vector.tensor_tensor(weight[:], best[:], best[:, :, 0:1].broadcast_to([P, NT, TOPK]),
                                            ALU.subtract).then_inc(shifted, 1)
                    c.wait()
                    c.step(nc.vector.tensor_copy(part_f[:], part[:]))
                    c.wait()
                    if b:
                        for n in range(2):
                            index_sum(h - 1, n)
                    for n in range(2):
                        dve.wait_ge(index_done, BASE + 2 * h)
                        nc.vector.tensor_tensor(match[:, n], lanes(part_f[:, n, :], 2, P, NT * TOPK, TOPK),
                                                lanes(T.iota[:, 0:TOPK], 1, P, NT * TOPK, TOPK),
                                                ALU.is_equal).then_inc(found, 1)
                    dve.wait_ge(weighted, h + 1)
                    c.link(nc.vector.tensor_reduce(total[:], weight[:], AX.X, ALU.add))
                    c.link(nc.vector.reciprocal(total[:], total[:]))
                    nc.vector.tensor_tensor(picked[2][:, :, bass.ds(h * TOPK, TOPK)], weight[:],
                                            lanes(total[:], 2, P, NT, TOPK), ALU.mult).then_inc(weight_done, 1)
                    if b:
                        for n in range(2):
                            index_sum(h, n)
                    assert c.n == STEPS, c.n

BANK_T = 4
S_G = 1024.0


def spread_weights(nc, io, T):
    RING = 4
    STEPS = BLOCK // BANK_T
    with ExitStack() as ctx:
        S = Space(nc, ctx, "e")
        E = EarlyTiles(nc, io, T, S, EARLY_S, EARLY_R * PEER_H, EARLY_S * NBLOCK)
        iota = S.sb("iota", [P, P], F16)
        left = [S.sb(f"left{r}", [P, BANK_T, P], F16) for r in range(RING)]
        right = [S.sb(f"right{r}", [P, 2, BANK_T, P], F16) for r in range(RING)]
        w_hi16 = S.sb("w_hi16", [P, SEQ], F16)
        w_hi = S.sb("w_hi", [P, SEQ])
        stage = [S.sb(f"stage{b}", [P, NKEYS, TB]) for b in range(2)]
        tab = [S.ps(f"tab{r}", [P, BANK_T, P]) for r in range(RING)]
        vec_step = S.sem("vec_step")
        built = S.sem("built")
        spread = S.sem("spread")
        out = S.sem("out")
        stored = [S.sem(f"stored{b}") for b in range(2)]
        block = ctx.enter_context(nc.Block())
        key1_t, key2_t, w_lo = T.picked_t
        HALVES = {(r * STEPS + 1) // (2 * EARLY_S): (r // 2, r % 2) for r in range(2 * EARLY_S)}

        @block.vector
        def _(dve):
            c = Chain(dve, vec_step)
            c.link(nc.vector.tensor_scalar(w_lo, w_lo, S_G, None, ALU.mult))
            c.step(nc.vector.tensor_copy(iota[:], T.iota[:]))
            c.link(nc.vector.tensor_copy(w_hi16[:], w_lo))
            c.link(nc.vector.tensor_copy(w_hi[:], w_hi16[:]))
            c.link(nc.vector.tensor_tensor(w_lo, w_lo, w_hi[:], ALU.subtract))
            with dve.Fori(0, NBLOCK) as blk:
                for s in range(STEPS):
                    r = s % RING
                    dve.wait_ge(spread, BASE - RING + 1 + blk * STEPS + s)
                    nc.vector.tensor_tensor(left[r][:], lanes(T.iota[:], 1, P, BANK_T, P),
                                            lanes(key2_t[:, bass.ds(blk * BLOCK + s * BANK_T, BANK_T)], 2, P, BANK_T, P),
                                            ALU.is_equal)
                    for j in range(BANK_T):
                        tok = bass.ds(blk * BLOCK + (s * BANK_T + j), 1)
                        nc.vector.tensor_scalar(right[r][:, 0, j, :], iota[:], key1_t[:, tok], w_hi[:, tok],
                                                ALU.is_equal, ALU.mult)
                        last = nc.vector.tensor_scalar(right[r][:, 1, j, :], iota[:], key1_t[:, tok], w_lo[:, tok],
                                                       ALU.is_equal, ALU.mult)
                    last.then_inc(built, 1)

        @block.tensor
        def _(pe):
            E.prime_tensor(pe)
            pe.sem_inc(spread, BASE)

            def step(blk, last):
                for s in range(STEPS):
                    n, r = blk * STEPS + s, s % RING
                    pe.wait_ge(built, n + 1)
                    pe.wait_ge(out, BASE - RING + 1 + n)
                    for j in range(BANK_T):
                        for part in range(2):
                            mm = pe.matmul(tab[r][:, j, :], left[r][:, j, :], right[r][:, part, j, :],
                                           start=part == 0, stop=part == 1)
                    mm.then_inc(spread, 1)
                    if s in HALVES:
                        b, half = HALVES[s]
                        if half == 0 and b + 1 < EARLY_S:
                            E.turn(pe, blk, b + 1)
                        elif half == 0 and not last:
                            E.turn(pe, blk + 1, 0)
                        E.hidden(pe, blk, b, half)

            E.turn(pe, 0, 0)
            with pe.Fori(0, NBLOCK - 1) as blk:
                step(blk, False)
            step(NBLOCK - 1, True)

        @block.scalar
        def _(act):
            E.prime_scalar(act)
            act.sem_inc(out, BASE)
            for b in range(2):
                act.sem_inc(stored[b], BASE)

            def step(blk, last):
                for s in range(STEPS):
                    n, r = blk * STEPS + s, s % RING
                    slot, at = s // (STEPS // 2), s % (STEPS // 2) * BANK_T
                    if at == 0:
                        act.wait_ge(stored[slot], BASE + blk * 16)
                    act.wait_ge(spread, BASE + 1 + n)
                    nc.scalar.activation(stage[slot][:, :, at:at + BANK_T],
                                         tab[r][:].rearrange("p t i -> p i t"), ACT.Copy).then_inc(out, 1)
                    if s in HALVES:
                        b, half = HALVES[s]
                        if half == 0 and b + 1 < EARLY_S:
                            E.split(act, blk, b + 1)
                        elif half == 0 and not last:
                            E.split(act, blk + 1, 0)
                        E.gelu(act, blk, b, half)

            E.split(act, 0, 0)
            with act.Fori(0, NBLOCK - 1) as blk:
                step(blk, False)
            step(NBLOCK - 1, True)

        @block.gpsimd
        def _(pool):
            E.prime_gpsimd(pool)
            with pool.Fori(0, NBLOCK) as blk:
                for b in range(EARLY_S):
                    E.low(pool, blk, b)

        @block.sync
        def _(sp):
            def step(blk, last):
                for b in range(EARLY_S):
                    E.keep(sp, blk, b)
                    if not last:
                        E.load(sp, blk + 1, b)
                    if b >= 1:
                        sp.wait_ge(out, BASE + blk * STEPS + b * (STEPS // 2))
                        sp.dma_start(T.dense.rearrange("(c b) j r -> c b j r", b=2)[blk, b - 1],
                                     stage[b - 1][:].rearrange("p i t -> p (i t)")).then_inc(stored[b - 1], 16)

            for b in range(EARLY_S):
                E.load(sp, 0, b, again=False)
            with sp.Fori(0, NBLOCK - 1) as blk:
                step(blk, False)
            step(NBLOCK - 1, True)
            for slot in range(2):
                sp.wait_ge(stored[slot], BASE + 16 * NBLOCK)
            E.all_kept(sp, EARLY_S * NBLOCK)


S_A = 64.0
GROUP = 4
NE = NKEYS


def experts(nc, io, T):
    LOOP = 2 * GROUP
    LATE = (NE - N_EARLY) // LOOP
    TURNS = NE // LOOP
    with ExitStack() as ctx:
        S = Space(nc, ctx, "f")
        u_in = [S.sb(f"u_in{b}", [P, D]) for b in range(2)]
        v_in = [S.sb(f"v_in{b}", [P, D]) for b in range(2)]
        g_in = [S.sb(f"g_in{b}", [P, NTB, GROUP * TB]) for b in range(2)]
        u_hi = [S.sb(f"u_hi{b}", [P, KT, P], F16) for b in range(2)]
        u_lo = [S.sb(f"u_lo{b}", [P, KT, P], F16) for b in range(2)]
        gel = [S.sb(f"gel{b}", [P, SEQ]) for b in range(2)]
        a = [S.sb(f"a{b}", [P, SEQ]) for b in range(2)]
        a_hi = [[S.sb(f"a_hi{g}{j}", [P, SEQ], F16) for j in range(GROUP)] for g in range(2)]
        a_lo = [[S.sb(f"a_lo{g}{j}", [P, SEQ], F16) for j in range(GROUP)] for g in range(2)]
        v_hi = [[S.sb(f"v_hi{g}{j}", [P, D], F16) for j in range(GROUP)] for g in range(2)]
        v_lo = [[S.sb(f"v_lo{g}{j}", [P, D], F16) for j in range(GROUP)] for g in range(2)]
        u_ps = S.ps("u_ps", [P, KT, P])
        hid = [S.ps(f"hid{b}", [P, SEQ]) for b in range(2)]
        y = [S.ps(f"y{b}", [P, HALF]) for b in range(2)]

        v_loaded = [S.sem(f"v_loaded{b}") for b in range(2)]
        g_loaded = [S.sem(f"g_loaded{b}") for b in range(2)]
        u_loaded = [S.sem(f"u_loaded{b}") for b in range(2)]
        gel_loaded = [S.sem(f"gel_loaded{b}") for b in range(2)]
        u_turned = S.sem("u_turned")
        u_hi_done = S.sem("u_hi_done")
        u_lo_done = S.sem("u_lo_done")
        hid_done = S.sem("hid_done")
        gelu_done = S.sem("gelu_done")
        stored = S.sem("stored")
        y_done = S.sem("y_done")
        v_hi_done = S.sem("v_hi_done")
        a_hi_done = S.sem("a_hi_done")
        a_done = S.sem("a_done")
        a_lo_done = S.sem("a_lo_done")
        y_added = S.sem("y_added")
        v_lo_done = S.sem("v_lo_done")
        block = ctx.enter_context(nc.Block())

        YB = NT * (D // HALF)
        YS = YB // GROUP
        y_place = [(k // 2, k % 2) for k in range(YB)]

        @block.sync
        def _(sp):
            u_v = io.peer_u[0, N_EARLY * P:NE * P, :].rearrange("(c m p) d -> c m p d", m=LOOP, p=P)
            kept_v = T.kept.rearrange("(c m p) t -> c m p t", m=LOOP, p=P)
            out_v = io.out[0].rearrange("(t p) d -> p t d", p=P)

            def step(c, view, early):
                first, count = (0, N_EARLY) if early else (N_EARLY, NE - N_EARLY)
                v_v = io.peer_v[0, first * P:(first + count) * P, :].rearrange("(c m p) d -> c m p d", m=LOOP, p=P)
                g_v = T.dense[:, :, first * TB:(first + count) * TB].rearrange("b j (c g r) -> c g j b r", g=2,
                                                                              r=GROUP * TB)
                for m in range(LOOP):
                    n = c * LOOP + m
                    if m % GROUP == 0:
                        g = m // GROUP
                        sp.wait_ge(a_done, BASE + n - GROUP)
                        sp.dma_start(g_in[g][:], g_v[view, g]).then_inc(g_loaded[g], 16)
                    if early:
                        sp.wait_ge(a_done, BASE + n - 1)
                        sp.dma_start(gel[m % 2][:], kept_v[view, m]).then_inc(gel_loaded[m % 2], 16)
                    else:
                        sp.wait_ge(u_turned, BASE + n - 1)
                        sp.dma_start(u_in[m % 2][:], u_v[view, m]).then_inc(u_loaded[m % 2], 16)
                    sp.wait_ge(v_lo_done, BASE + n - 1)
                    sp.dma_start(v_in[m % 2][:], v_v[view, m]).then_inc(v_loaded[m % 2], 16)

            with sp.Fori(0, LATE) as c:
                step(c, c, False)
            with sp.Fori(0, TURNS - LATE) as e:
                step(e + LATE, e, True)
            for t in range(NT):
                sp.wait_ge(y_added, BASE + YB * (NE // GROUP - 1) + 2 * t + 2)
                sp.dma_start(out_v[:, t, :], T.h[:, t, :]).then_inc(stored, 16)
            sp.wait_ge(stored, 16 * NT)

        @block.tensor
        def _(pe):
            pe.sem_inc(u_turned, BASE)
            pe.sem_inc(hid_done, BASE)
            pe.sem_inc(y_done, BASE)

            def turn(n, m):
                pe.wait_ge(u_loaded[m % 2], n * 8 + (16 - 8 * (m % 2)))
                pe.wait_ge(u_lo_done, BASE + n)
                for k in range(KT):
                    last = pe.transpose(u_ps[:, k, :], u_in[m % 2][:, k * P:(k + 1) * P], T.ident[:])
                last.then_inc(u_turned, 1)

            def hidden(n, m):
                pe.wait_ge(u_lo_done, BASE + n + 1)
                pe.wait_ge(gelu_done, BASE + n - 1)
                for half in range(2):
                    toks = slice(half * HALF, (half + 1) * HALF)
                    for k in range(KT):
                        last = split_mm(pe, hid[m % 2][:, toks], u_hi[m % 2][:, k, :], u_lo[m % 2][:, k, :],
                                        T.act_hi[:, k, toks], T.act_lo[:, k, toks], k == 0, k == KT - 1)
                last.then_inc(hid_done, 1)

            def outputs(group_n, g, part):
                if part == 0:
                    pe.wait_ge(a_lo_done, BASE + GROUP * (group_n + 1))
                    pe.wait_ge(v_lo_done, BASE + GROUP * (group_n + 1))
                for k in range(part * YS, (part + 1) * YS):
                    t, half = y_place[k]
                    pe.wait_ge(y_added, BASE + YB * group_n + k - 1)
                    for j in range(GROUP):
                        toks, cols = slice(t * P, (t + 1) * P), slice(half * HALF, (half + 1) * HALF)
                        last = split_mm(pe, y[k % 2][:], a_hi[g][j][:, toks], a_lo[g][j][:, toks],
                                        v_hi[g][j][:, cols], v_lo[g][j][:, cols], j == 0, j == GROUP - 1)
                    last.then_inc(y_done, 1)

            def step(c, m, y_too=True, u_too=True, early=False):
                n = c * LOOP + m
                if u_too and not early:
                    turn(n + 1, m + 1)
                if not early:
                    hidden(n, m)
                if y_too:
                    outputs(2 * c + m // GROUP - 1, (m // GROUP + 1) % 2, m % GROUP)

            turn(0, 0)
            for m in range(LOOP):
                step(0, m, y_too=m >= GROUP)
            with pe.Fori(1, LATE - 1) as c:
                for m in range(LOOP):
                    step(c, m)
            for m in range(LOOP):
                step(LATE - 1, m, u_too=m < LOOP - 1)
            with pe.Fori(LATE, TURNS) as c:
                for m in range(LOOP):
                    step(c, m, early=True)
            for part in range(GROUP):
                outputs(NE // GROUP - 1, 1, part)

        @block.scalar
        def _(act):
            act.sem_inc(gelu_done, BASE)
            act.sem_inc(u_hi_done, BASE)
            act.sem_inc(v_hi_done, BASE)
            act.sem_inc(a_hi_done, BASE)

            def hi_u(n, m):
                act.wait_ge(u_turned, BASE + n + 1)
                act.wait_ge(hid_done, BASE + n - 1)
                nc.scalar.activation(u_hi[m % 2][:], u_ps[:], ACT.Copy, scale=S_U).then_inc(u_hi_done, 1)

            def step(c, m, u_too=True, early=False):
                n = c * LOOP + m
                g, j = m // GROUP, m % GROUP
                if u_too and not early:
                    hi_u(n + 1, m + 1)
                if j == 0:
                    act.wait_ge(y_done, BASE + YB * (2 * c + g - 1))
                act.wait_ge(v_loaded[m % 2], n * 8 + (16 - 8 * (m % 2)))
                nc.scalar.activation(v_hi[g][j][:], v_in[m % 2][:], ACT.Copy).then_inc(v_hi_done, 1)
                if not early:
                    act.wait_ge(hid_done, BASE + n + 1)
                    act.wait_ge(a_done, BASE + n - 1)
                    nc.scalar.activation(gel[m % 2][:], hid[m % 2][:], ACT.Gelu,
                                         scale=1.0 / (S_U * S_ACT)).then_inc(gelu_done, 1)
                act.wait_ge(a_done, BASE + n + 1)
                nc.scalar.activation(a_hi[g][j][:], a[m % 2][:], ACT.Copy).then_inc(a_hi_done, 1)

            hi_u(0, 0)
            with act.Fori(0, LATE - 1) as c:
                for m in range(LOOP):
                    step(c, m)
            for m in range(LOOP):
                step(LATE - 1, m, u_too=m < LOOP - 1)
            with act.Fori(LATE, TURNS) as c:
                for m in range(LOOP):
                    step(c, m, early=True)

        @block.gpsimd
        def _(pool):
            pool.sem_inc(v_lo_done, BASE)
            with pool.Fori(0, TURNS) as c:
                for m in range(LOOP):
                    n = c * LOOP + m
                    g, j = m // GROUP, m % GROUP
                    pool.wait_ge(v_hi_done, BASE + n + 1)
                    nc.gpsimd.tensor_tensor(v_lo[g][j][:], v_in[m % 2][:], v_hi[g][j][:],
                                            ALU.subtract).then_inc(v_lo_done, 1)

        @block.vector
        def _(dve):
            dve.sem_inc(u_lo_done, BASE)
            dve.sem_inc(a_done, BASE)
            dve.sem_inc(a_lo_done, BASE)
            dve.sem_inc(y_added, BASE)

            def lo_u(n, m):
                dve.wait_ge(u_hi_done, BASE + n + 1)
                nc.vector.scalar_tensor_tensor(u_lo[m % 2][:], u_ps[:], S_U, u_hi[m % 2][:], ALU.mult,
                                               ALU.subtract).then_inc(u_lo_done, 1)

            def add_y(group_n, k):
                t, half = y_place[k]
                cols = slice(half * HALF, (half + 1) * HALF)
                dve.wait_ge(y_done, BASE + YB * group_n + k + 1)
                dve.wait_ge(y_added, BASE + YB * (group_n - 1) + k + 1)
                nc.vector.scalar_tensor_tensor(T.h[:, t, cols], y[k % 2][:], 1.0 / S_A, T.h[:, t, cols], ALU.mult,
                                               ALU.add).then_inc(y_added, 1)

            def step(c, m, y_too=True, u_too=True, early=False):
                n = c * LOOP + m
                g, j = m // GROUP, m % GROUP
                if u_too and not early:
                    lo_u(n + 1, m + 1)
                if j == 0:
                    dve.wait_ge(g_loaded[g], c * 16 + 16)
                if early:
                    at = n - LATE * LOOP
                    dve.wait_ge(gel_loaded[m % 2], at * 8 + (16 - 8 * (m % 2)))
                    dve.wait_ge(a_hi_done, BASE + n - 1)
                else:
                    dve.wait_ge(gelu_done, BASE + n + 1)
                dve.wait_ge(a_lo_done, BASE + n - 1)
                nc.vector.scalar_tensor_tensor(
                    a[m % 2][:].rearrange("p (b t) -> p b t", t=TB), gel[m % 2][:].rearrange("p (b t) -> p b t", t=TB),
                    S_A / S_G, g_in[g][:].rearrange("p b (i t) -> p b i t", t=TB)[:, :, j, :], ALU.mult,
                    ALU.mult).then_inc(a_done, 1)
                if y_too:
                    add_y(2 * c + g - 1, j * YS)
                dve.wait_ge(a_hi_done, BASE + n + 1)
                nc.vector.tensor_tensor(a_lo[g][j][:], a[m % 2][:], a_hi[g][j][:], ALU.subtract).then_inc(a_lo_done, 1)
                if y_too:
                    for k in range(j * YS + 1, (j + 1) * YS):
                        add_y(2 * c + g - 1, k)

            lo_u(0, 0)
            for m in range(LOOP):
                step(0, m, y_too=m >= GROUP)
            with dve.Fori(1, LATE - 1) as c:
                for m in range(LOOP):
                    step(c, m)
            for m in range(LOOP):
                step(LATE - 1, m, u_too=m < LOOP - 1)
            with dve.Fori(LATE, TURNS) as c:
                for m in range(LOOP):
                    step(c, m, early=True)
            for k in range(YB):
                add_y(NE // GROUP - 1, k)


def allocate_constants(S):
    T = Names()
    T.ident = S.sb("ident", [P, P])
    T.causal = S.sb("causal", [P, P])
    T.tri = S.sb("tri", [P, P])
    T.iota = S.sb("iota", [P, P])
    T.iota_i = S.sb("iota_i", [P, P], I32)
    T.mhalf = S.sb("mhalf", [P, 8])
    T.eps = S.sb("eps", [P, 8])
    T.g_mix = S.sb("g_mix", [P, KT])
    T.g_ffn = S.sb("g_ffn", [P, KT])
    T.g_sub = S.sb("g_sub", [P, 1])
    T.b_gate = S.sb("b_gate", [P, 2])
    T.g_gla = S.sb("g_gla", [P, GLA_DV])
    T.g_q = S.sb("g_q", [P, DIFF_DK])
    T.g_k = S.sb("g_k", [P, DIFF_DK])
    T.w_gate = S.sb("w_gate", [GLA_RANK, GLA_H * GLA_DK])
    T.sin = S.sb("sin", [P, NT, HROPE])
    T.cos = S.sb("cos", [P, NT, HROPE])
    T.neg_lam = S.sb("neg_lam", [P, 1])
    T.act_hi = S.sb("act_hi", [P, KT, SEQ], F16)
    T.act_lo = S.sb("act_lo", [P, KT, SEQ], F16)
    return T


def allocate_diff(S, T):
    T.dq = S.sb("dq", [P, NT, HALF])
    T.dk = S.sb("dk", [P, NT, HALF])
    T.dv = S.sb("dv", [P, NT, HALF])


def allocate_gla(S, T):
    T.gqk = S.sb("gqk", [P, 4, SEQ])
    T.ga = S.sb("ga", [GLA_RANK, SEQ])
    T.gv = S.sb("gv", [P, NT, HALF])
    T.gr = S.sb("gr", [P, NT, HALF])


def stage(nc, program, io, T):
    with nc.cleanup_on_exit():
        program(nc, io, T)


def hybrid_block(nc, io):
    dense = nc.dram_tensor("dense_weights", [NTB, NKEYS, NKEYS * TB], F32, kind="Internal").ap()
    kept = nc.dram_tensor("early_tiles", [N_EARLY * NKEYS, SEQ], F32, kind="Internal").ap()
    with ExitStack() as whole:
        T = allocate_constants(Space(nc, whole, "p"))
        T.dense, T.kept = dense, kept
        stage(nc, constants, io, T)
        with ExitStack() as diff:
            allocate_diff(Space(nc, diff, "p"), T)
            with ExitStack() as gla:
                S = Space(nc, gla, "p")
                allocate_gla(S, T)
                stage(nc, project_in, io, T)
                T.state = S.sb("state", [P, NCH, 2, GLA_DV])
                stage(nc, gla_states, io, T)
                stage(nc, gla_outputs, io, T)
            stage(nc, diff_attention, io, T)
        T.h = Space(nc, whole, "p").sb("h", [P, NT, D])
        stage(nc, project_out, io, T)
        with ExitStack() as picks:
            S = Space(nc, picks, "p")
            T.picked_all = S.sb("picked_all", [P, 3 * SEQ])
            T.picked_t = [T.picked_all[:, n * SEQ:(n + 1) * SEQ] for n in range(3)]
            stage(nc, retrieve, io, T)
            stage(nc, spread_weights, io, T)
        stage(nc, experts, io, T)


_INS = ["x", "positions", "g_mix", "w_in", "w_gla_gate", "b_gla_gate", "g_gla_out", "g_q", "g_k", "lambda_q1",
        "lambda_k1", "lambda_q2", "lambda_k2", "g_diff_sub", "w_out", "g_ffn", "w_peer_q", "peer_sub_keys", "peer_u",
        "peer_v"]


def kernel(**inputs):
    import numpy as _np
    import concourse.bacc as _bacc
    from concourse import mybir as _mybir
    from concourse.bass_utils import run_bass_kernel_spmd as _run

    nc = _bacc.Bacc("TRN2", target_bir_lowering=False, num_devices=1)
    arrays, io = {}, Names()
    for name in _INS:
        a = _np.ascontiguousarray(inputs[name])
        arrays[f"in_{name}"] = a
        io.__dict__[name] = nc.dram_tensor(f"in_{name}", a.shape, _mybir.dt.from_np(a.dtype),
                                           kind="ExternalInput").ap()
    io.out = nc.dram_tensor("out", (1, SEQ, D), F32, kind="ExternalOutput").ap()
    hybrid_block(nc, io)
    r = _run(nc, [arrays], core_ids=[0])
    return r.results[0]["out"]
```

```python
from contextlib import ExitStack

import numpy as np
import concourse.bass as bass
from concourse import mybir

F32 = mybir.dt.float32
F16 = mybir.dt.float16
BF16 = mybir.dt.bfloat16
I32 = mybir.dt.int32
U32 = mybir.dt.uint32
ALU = mybir.AluOpType
ACT = mybir.ActivationFunctionType
AX = mybir.AxisListType

P = 128
SEQ = 1024
D = 1024
KT = D // P
NT = SEQ // P
HALF = 512

GLA_H, GLA_DK, GLA_DV, GLA_RANK, GLA_TAU, CHUNK = 4, 64, 128, 16, 16.0, 64
DIFF_H, DIFF_DK, DIFF_DV = 4, 64, 128
ROPE = DIFF_DK // 4
HROPE = ROPE // 2
ROPE_THETA = 500000.0
LAMBDA_INIT = 0.8 - 0.6 * float(np.exp(-0.3 * 0))
EPS = 1e-6

PEER_H, NKEYS, QDIM, TOPK = 8, 128, 256, 16
PICKS = PEER_H * TOPK

S_ACT = 16.0
S_W = 64.0
UNSCALE = 1.0 / (S_ACT * S_W)
BASE = 64


class Names:
    pass


class Chain:

    def __init__(self, eng, sem, at=0):
        self.eng, self.sem, self.at, self.n = eng, sem, at, 0

    def step(self, ins):
        self.n += 1
        ins.then_inc(self.sem, 1)

    def wait(self):
        self.eng.wait_ge(self.sem, self.at + self.n)

    def link(self, ins):
        self.step(ins)
        self.wait()


class Space:

    def __init__(self, nc, ctx, tag):
        self.nc, self.ctx, self.tag = nc, ctx, tag

    def sb(self, name, shape, dt=F32):
        return self.ctx.enter_context(self.nc.sbuf_tensor(f"{self.tag}_{name}", shape, dt))

    def ps(self, name, shape, dt=F32):
        return self.ctx.enter_context(self.nc.psum_tensor(f"{self.tag}_{name}", shape, dt))

    def sem(self, name):
        return self.nc.alloc_semaphore(f"{self.tag}_{name}")


def lanes(ap, *shape):
    axis = shape[0]
    return ap.unsqueeze(axis).broadcast_to(list(shape[1:]))


class Constants:

    def __init__(self, nc, io, T, S):
        self.nc, self.io, self.T = nc, io, T
        self.pos = S.sb("pos", [P, NT], I32)
        self.posf = S.sb("posf", [P, NT])
        self.freq = S.sb("freq", [P, HROPE])
        self.ang = S.sb("ang", [P, NT, HROPE])
        self.turns_i = S.sb("turns_i", [P, NT * HROPE], I32)
        self.turns = S.sb("turns", [P, NT * HROPE])
        self.wrap = S.sb("wrap", [P, NT * HROPE])
        self.lamv = S.sb("lamv", [P, 4, DIFF_DK])
        self.lamp = S.sb("lamp", [P, DIFF_DK])
        self.lams = S.sb("lams", [P, 2])
        self.lame = S.sb("lame", [P, 2])
        self.gain_loaded = S.sem("gain_loaded")
        self.gain_ready = S.sem("gain_ready")
        self.loaded = S.sem("loaded")
        self.masks_ready = S.sem("masks_ready")
        self.pool_step = S.sem("const_pool_step")
        self.vec_step = S.sem("const_vec_step")
        self.act_step = S.sem("const_act_step")
        self.gates = S.sem("gates")

    def load_gain(self, sp):
        with self.nc.allow_non_contiguous_dma("a column of small weights"):
            sp.dma_start(self.T.g_mix[:], self.io.g_mix.rearrange("l (k p) -> p (l k)", p=P)).then_inc(
                self.gain_loaded, 16)

    def load(self, sp):
        with self.nc.allow_non_contiguous_dma("columns of small weights"):
            sp.dma_start(self.pos[:], self.io.positions.rearrange("b (t p) -> p (b t)", p=P)).then_inc(self.loaded, 16)
            sp.dma_start(self.T.g_ffn[:], self.io.g_ffn.rearrange("l (k p) -> p (l k)", p=P)).then_inc(self.loaded, 16)
            sp.dma_start(self.T.g_sub[:], self.io.g_diff_sub.rearrange("l p -> p l")).then_inc(self.loaded, 16)
            sp.dma_start(self.T.b_gate[:], self.io.b_gla_gate.rearrange("l (c p) -> p (l c)", p=P)).then_inc(self.loaded, 16)
        sp.dma_start(self.T.g_gla[:], self.io.g_gla_out[0, :].partition_broadcast(P)).then_inc(self.loaded, 16)
        sp.dma_start(self.T.g_q[:], self.io.g_q[0, :].partition_broadcast(P)).then_inc(self.loaded, 16)
        sp.dma_start(self.T.g_k[:], self.io.g_k[0, :].partition_broadcast(P)).then_inc(self.loaded, 16)
        sp.dma_start(self.T.w_gate[:], self.io.w_gla_gate[0]).then_inc(self.loaded, 16)
        for n, v in enumerate((self.io.lambda_q1, self.io.lambda_k1, self.io.lambda_q2, self.io.lambda_k2)):
            sp.dma_start(self.lamv[:, n, :], v[0, :].partition_broadcast(P)).then_inc(self.loaded, 16)

    def masks(self, pool):
        c = Chain(pool, self.pool_step)
        c.step(self.nc.gpsimd.memset(self.T.ident[:], 0.0))
        c.step(self.nc.gpsimd.memset(self.T.causal[:], 0.0))
        c.step(self.nc.gpsimd.memset(self.T.tri[:], 1.0))
        c.step(self.nc.gpsimd.memset(self.T.mhalf[:], -0.5))
        c.step(self.nc.gpsimd.memset(self.T.eps[:], EPS))
        c.step(self.nc.gpsimd.iota(self.T.iota_i[:], [[1, P]], base=0, channel_multiplier=0))
        c.wait()
        c.step(self.nc.gpsimd.affine_select(out=self.T.ident[:], in_=self.T.ident[:], compare_op=ALU.not_equal, fill=1.0,
                                       base=0, pattern=[[-1, P]], channel_multiplier=1))
        c.step(self.nc.gpsimd.affine_select(out=self.T.causal[:], in_=self.T.causal[:], compare_op=ALU.is_ge, fill=-1e30,
                                       base=0, pattern=[[-1, P]], channel_multiplier=1))
        c.step(self.nc.gpsimd.affine_select(out=self.T.tri[:], in_=self.T.tri[:], compare_op=ALU.is_ge, fill=0.0,
                                       base=0, pattern=[[1, P]], channel_multiplier=-1))
        c.step(self.nc.gpsimd.tensor_copy(self.T.iota[:], self.T.iota_i[:]))
        c.wait()
        self.nc.gpsimd.memset(self.T.tri[0:CHUNK, CHUNK:P], 0.0).then_inc(self.masks_ready, 1)

    def gain(self, dve):
        dve.wait_ge(self.gain_loaded, 16)
        self.nc.vector.tensor_scalar(self.T.g_mix[:], self.T.g_mix[:], S_W, None, ALU.mult).then_inc(self.gain_ready, 1)

    def tables(self, dve):
        c = Chain(dve, self.vec_step)
        for j in range(HROPE):
            c.step(self.nc.vector.memset(self.freq[:, j:j + 1], float(np.float32(ROPE_THETA) ** np.float32(-2.0 * j / ROPE))))
        dve.wait_ge(self.loaded, 16 * 12)
        c.link(self.nc.vector.tensor_copy(self.posf[:], self.pos[:]))
        c.link(self.nc.vector.tensor_tensor(self.ang[:], lanes(self.posf[:], 2, P, NT, HROPE), lanes(self.freq[:], 1, P, NT, HROPE),
                                       ALU.mult))
        flat = self.ang[:].rearrange("p t j -> p (t j)")
        c.link(self.nc.vector.tensor_scalar(self.turns[:], flat, 1.0 / (2 * np.pi), None, ALU.mult))
        c.link(self.nc.vector.tensor_copy(self.turns_i[:], self.turns[:]))
        c.link(self.nc.vector.tensor_copy(self.turns[:], self.turns_i[:]))
        c1 = 6.28125
        c2 = float(np.floor((2 * np.pi - c1) * 2 ** 22) / 2 ** 22)
        c3 = float(2 * np.pi - c1 - c2)
        for part in (c1, c2, c3):
            c.link(self.nc.vector.scalar_tensor_tensor(flat, self.turns[:], -part, flat, ALU.mult, ALU.add))
        lim = 3.1415925
        c.link(self.nc.vector.tensor_scalar(self.T.sin[:].rearrange("p t j -> p (t j)"), flat, lim, -lim, ALU.min, ALU.max))
        c.link(self.nc.vector.tensor_scalar(self.wrap[:], flat, float(np.pi / 2), -2 * float(np.pi), ALU.is_gt, ALU.mult))
        c.link(self.nc.vector.scalar_tensor_tensor(flat, flat, float(np.pi / 2), self.wrap[:], ALU.add, ALU.add))
        c.link(self.nc.vector.tensor_scalar(self.T.cos[:].rearrange("p t j -> p (t j)"), flat, lim, -lim, ALU.min, ALU.max))
        for n in range(2):
            c.link(self.nc.vector.tensor_tensor(self.lamp[:], self.lamv[:, 2 * n, :], self.lamv[:, 2 * n + 1, :], ALU.mult))
            c.link(self.nc.vector.tensor_reduce(self.lams[:, n:n + 1], self.lamp[:], AX.X, ALU.add))
        self.nc.vector.tensor_scalar(self.T.g_ffn[:], self.T.g_ffn[:], S_ACT, None, ALU.mult).then_inc(self.gates, 1)
        self.nc.vector.tensor_scalar(self.T.g_sub[:], self.T.g_sub[:], S_ACT * (1.0 - LAMBDA_INIT), None,
                                ALU.mult).then_inc(self.gates, 1)

    def sines(self, act):
        act.wait_ge(self.vec_step, HROPE + 16)
        self.nc.scalar.activation(self.lame[:], self.lams[:], ACT.Exp).then_inc(self.act_step, 1)
        self.nc.scalar.activation(self.T.sin[:], self.T.sin[:], ACT.Sin).then_inc(self.act_step, 1)
        self.nc.scalar.activation(self.T.cos[:], self.T.cos[:], ACT.Sin).then_inc(self.act_step, 1)

    def finish(self, dve):
        c = Chain(dve, self.vec_step, HROPE + 16)
        dve.wait_ge(self.act_step, 3)
        c.link(self.nc.vector.scalar_tensor_tensor(self.T.neg_lam[:], self.lame[:, 1:2], -LAMBDA_INIT, self.lame[:, 0:1],
                                              ALU.add, ALU.subtract))


def split_mm(pe, out, a_hi, a_lo, b_hi, b_lo, first, last):
    pe.matmul(out, a_hi, b_hi, start=first, stop=False)
    pe.matmul(out, a_hi, b_lo, start=False, stop=False)
    return pe.matmul(out, a_lo, b_hi, start=False, stop=last)


COLS = [("qk", 0, 512), ("ga", 1024, GLA_RANK), ("gv", 512, 512), ("gr", 1040, 512), ("dq", 1552, 512),
        ("dk", 2064, 512), ("dv", 2576, 512)]
GA_T = SEQ // 4


XR = 4


def project_in(nc, io, T):
    with ExitStack() as ctx:
        S = Space(nc, ctx, "a")
        const = Constants(nc, io, T, S)
        x_in = S.sb("x_in", [P, XR, D])
        junk = S.sb("junk", [P, D], F16)
        ss = S.sb("ss", [P, NT])
        rstd = S.sb("rstd", [P, NT])
        w_in = S.sb("w_in", [P, 2, 2, HALF])
        w_hi = S.sb("w_hi", [P, 2, KT, HALF], F16)
        w_lo = S.sb("w_lo", [P, 2, KT, HALF], F16)
        sq = S.sb("sq", [P, 2, HALF])
        hss = S.sb("hss", [P, 2, 8])
        hr = S.sb("hr", [P, 2, 8])
        turned = [S.ps(f"turned{b}", [P, KT, P]) for b in range(2)]
        acc = [S.ps(f"acc{b}", [P, HALF]) for b in range(4)]

        x_loaded = [S.sem(f"x_loaded{b}") for b in range(XR)]
        w_loaded = [S.sem(f"w_loaded{b}") for b in range(2)]
        squared = S.sem("squared")
        rstd_done = S.sem("rstd_done")
        pool_step = S.sem("pool_step")
        normed = S.sem("normed")
        x_turned = S.sem("x_turned")
        hi_done = S.sem("hi_done")
        lo_done = S.sem("lo_done")
        w_hi_done = S.sem("w_hi_done")
        w_lo_done = S.sem("w_lo_done")
        acc_full = S.sem("acc_full")
        acc_free = S.sem("acc_free")
        head_sq = S.sem("head_sq")
        head_ss = S.sem("head_ss")
        head_r = S.sem("head_r")
        head_normed = S.sem("head_normed")
        rot_step = S.sem("rot_step")
        keep_done = S.sem("keep_done")
        ga_out = S.sem("ga_out")
        gate_done = S.sem("gate_done")
        z_done = S.sem("z_done")
        soft_step = S.sem("soft_step")
        soft_done = S.sem("soft_done")
        gate_step = S.sem("gate_step")
        cum_done = S.sem("cum_done")
        roped = S.sem("roped")
        block = ctx.enter_context(nc.Block())

        PIECES = KT // 2
        gains = {"dq": T.g_q, "dk": T.g_k}
        dest = {"gv": T.gv, "gr": T.gr, "dq": T.dq, "dk": T.dk, "dv": T.dv}
        first_result = [0]
        for name, _, _ in COLS:
            first_result.append(first_result[-1] + (4 if name == "ga" else 8))
        keep = sq[:].rearrange("p a b -> p (a b)")
        z, soft = x_in[:, 0:2], x_in[:, 2:4]
        ga = x_in[0:GLA_RANK, 3]
        gate = [x[:].rearrange("p k t -> p (k t)") for x in turned]

        @block.sync
        def _(sp):
            def load_w(c, q):
                _, c0, n = COLS[c]
                r = c * PIECES + q
                if r >= 2:
                    sp.wait_ge(w_lo_done, r - 1)
                src = io.w_in[0, 2 * q * P:(2 * q + 2) * P, c0:c0 + n].rearrange("(k p) n -> p k n", p=P)
                sp.dma_start(w_in[:, r % 2, :, 0:n], src).then_inc(w_loaded[r % 2], 16)

            def load_x(t):
                if t >= XR:
                    sp.wait_ge(x_turned, t - XR + 1)
                sp.dma_start(x_in[:, t % XR, :], io.x[0, t * P:(t + 1) * P, :]).then_inc(x_loaded[t % XR], 16)

            load_x(0)
            const.load_gain(sp)
            load_x(1)
            for q in range(PIECES):
                load_x(q + 2)
                load_w(0, q)
            const.load(sp)
            for t in range(PIECES + 2, NT):
                load_x(t)
            for c in range(1, len(COLS)):
                for q in range(PIECES):
                    load_w(c, q)

        @block.gpsimd
        def _(pool):
            const.masks(pool)
            nc.gpsimd.memset(keep, 1.0).then_inc(keep_done, 1)
            pool.wait_ge(keep_done, 1)
            nc.gpsimd.memset(keep.rearrange("p (c s) -> p c s", s=CHUNK)[:, :, 0:1], 0.0).then_inc(keep_done, 1)
            c = Chain(pool, pool_step)
            for t in range(NT):
                pool.wait_ge(squared, t + 1)
                c.link(nc.gpsimd.tensor_scalar(rstd[:, t:t + 1], ss[:, t:t + 1], 1.0 / D, EPS, ALU.mult, ALU.add))
                nc.gpsimd.tensor_tensor(rstd[:, t:t + 1], rstd[:, t:t + 1], T.mhalf[:, 0:1],
                                        ALU.pow).then_inc(rstd_done, 1)
            base = c.n
            with pool.Fori(0, NT) as i:
                c = Chain(pool, pool_step, base + 2 * i)
                for b in range(2):
                    pool.wait_ge(head_ss, 2 * i + b + 1)
                    c.link(nc.gpsimd.tensor_tensor(hr[:, b, :], hss[:, b, :], T.eps[:, 0:8], ALU.add))
                    nc.gpsimd.tensor_tensor(hr[:, b, :], hr[:, b, :], T.mhalf[:, 0:8], ALU.pow).then_inc(head_r, 1)

        @block.scalar
        def _(act):
            act.sem_inc(acc_free, BASE)

            def split_w(c, pieces=range(PIECES)):
                n = COLS[c][2]
                if c >= 2:
                    act.wait_ge(acc_full, first_result[c - 1])
                for q in pieces:
                    r = c * PIECES + q
                    act.wait_ge(w_loaded[r % 2], 16 * (r // 2 + 1))
                    for j in range(2):
                        k = 2 * q + j
                        last = nc.scalar.activation(w_hi[:, c % 2, k, 0:n], w_in[:, r % 2, j, 0:n], ACT.Copy,
                                                    scale=T.g_mix[:, k:k + 1])
                    last.then_inc(w_hi_done, 1)

            def square(t):
                act.wait_ge(x_loaded[t % XR], 16 * (t // XR + 1))
                if t:
                    act.wait_ge(squared, t)
                nc.scalar.activation(junk[:], x_in[:, t % XR, :], ACT.Square,
                                     accum_out=ss[:, t:t + 1]).then_inc(squared, 1)

            square(0)
            square(1)
            act.wait_ge(const.gain_ready, 1)
            for t in range(NT):
                act.wait_ge(x_turned, t + 1)
                nc.scalar.activation(T.act_hi[:, :, t * P:(t + 1) * P], turned[t % 2][:], ACT.Copy,
                                     scale=S_ACT).then_inc(hi_done, 1)
                if t + 2 < NT:
                    square(t + 2)
                if t < PIECES:
                    split_w(0, [t])
            split_w(1)
            for half in range(2):
                if half:
                    const.sines(act)
                for j in range(4):
                    r = 4 * half + j
                    act.wait_ge(acc_full, r + 1)
                    nc.scalar.activation(T.gqk[:, j, half * HALF:(half + 1) * HALF], acc[r % 4][:], ACT.Copy,
                                         scale=UNSCALE).then_inc(acc_free, 1)
            split_w(2)
            for r in range(4):
                act.wait_ge(acc_full, first_result[1] + r + 1)
                nc.scalar.activation(ga[:, r * GA_T:(r + 1) * GA_T], acc[r][0:GLA_RANK, 0:GA_T], ACT.Copy,
                                     scale=UNSCALE).then_inc(ga_out, 1)
            act.wait_ge(ga_out, 4)
            act.sem_inc(acc_free, 4)
            for c in range(2, len(COLS)):
                name = COLS[c][0]
                if name == "gr":
                    steps = Chain(act, soft_step)
                    act.wait_ge(z_done, 2)
                    steps.link(nc.scalar.activation(soft, z, ACT.Abs))
                    steps.link(nc.scalar.activation(soft, soft, ACT.Exp, scale=-1.0))
                    nc.scalar.activation(soft, soft, ACT.Ln, bias=1.0).then_inc(soft_done, 1)
                if c + 1 < len(COLS):
                    split_w(c + 1)
                if name == "dq":
                    act.wait_ge(cum_done, 2)
                if name == "dv":
                    act.wait_ge(acc_free, BASE + first_result[c])
                with act.Fori(0, NT // 4) as i:
                    for b in range(4):
                        act.wait_ge(acc_full, first_result[c] + 4 * i + b + 1)
                        if name in gains:
                            n0 = 8 * (name == "dk")
                            nc.scalar.activation(sq[:, b % 2, :], acc[b][:], ACT.Square,
                                                 scale=UNSCALE * DIFF_DK ** -0.5).then_inc(head_sq, 1)
                            act.wait_ge(head_ss, n0 + 4 * i + b + 1)
                        else:
                            f = ACT.Silu if name == "gr" else ACT.Copy
                            nc.scalar.activation(dest[name][:, bass.ds(4 * i + b, 1), :].rearrange("p a n -> p (a n)"),
                                                 acc[b][:], f, scale=UNSCALE).then_inc(acc_free, 1)

        @block.vector
        def _(dve):
            def split_w(c, pieces=range(PIECES)):
                n = COLS[c][2]
                for q in pieces:
                    r = c * PIECES + q
                    dve.wait_ge(w_hi_done, r + 1)
                    for j in range(2):
                        k = 2 * q + j
                        last = nc.vector.scalar_tensor_tensor(w_lo[:, c % 2, k, 0:n], w_in[:, r % 2, j, 0:n],
                                                              T.g_mix[:, k:k + 1], w_hi[:, c % 2, k, 0:n], ALU.mult,
                                                              ALU.subtract)
                    last.then_inc(w_lo_done, 1)

            def scale(t):
                dve.wait_ge(rstd_done, t + 1)
                nc.vector.tensor_scalar(x_in[:, t % XR, :], x_in[:, t % XR, :], rstd[:, t:t + 1], None,
                                        ALU.mult).then_inc(normed, 1)

            def rope(x, c):
                v = x[:].rearrange("p t (h d) -> p t h d", d=DIFF_DK)
                x1, x2 = v[:, :, :, 0:HROPE], v[:, :, :, HROPE:ROPE]
                shape = [P, NT, 8, HROPE]
                tmp = [x_in[:, 2 + n // 2, n % 2 * HALF:(n % 2 + 1) * HALF].rearrange(
                    "p (t h d) -> p t h d", t=NT, h=8) for n in range(4)]
                cos, sin = (w[:].unsqueeze(2).broadcast_to(shape) for w in (T.cos, T.sin))
                for n, (u, w) in enumerate(((x1, cos), (x2, sin), (x2, cos), (x1, sin))):
                    c.step(nc.vector.tensor_tensor(tmp[n], u, w, ALU.mult))
                c.wait()
                c.step(nc.vector.tensor_tensor(x1, tmp[0], tmp[1], ALU.subtract))
                c.link(nc.vector.tensor_tensor(x2, tmp[2], tmp[3], ALU.add))

            const.gain(dve)
            scale(0)
            scale(1)
            for t in range(NT):
                dve.wait_ge(hi_done, t + 1)
                toks = slice(t * P, (t + 1) * P)
                nc.vector.scalar_tensor_tensor(T.act_lo[:, :, toks], turned[t % 2][:], S_ACT, T.act_hi[:, :, toks],
                                               ALU.mult, ALU.subtract).then_inc(lo_done, 1)
                if t + 2 < NT:
                    scale(t + 2)
                if t < PIECES:
                    dve.wait_ge(const.gain_ready, 1)
                    split_w(0, [t])
            split_w(1)
            const.tables(dve)
            turning = Chain(dve, rot_step)
            for c in range(2, len(COLS) + 1):
                if c < len(COLS):
                    split_w(c)
                if COLS[c - 1][0] == "gv":
                    for ct in range(2):
                        dve.wait_ge(gate_done, ct + 1)
                        nc.vector.tensor_scalar(z[:, ct, :], gate[ct], T.b_gate[:, ct:ct + 1], None,
                                                ALU.add).then_inc(z_done, 1)
                    dve.wait_ge(z_done, 2)
                    dve.wait_ge(soft_done, 1)
                    dve.wait_ge(keep_done, 2)
                    steps = Chain(dve, gate_step)
                    steps.link(nc.vector.scalar_tensor_tensor(z, z, 0.0, soft, ALU.min, ALU.subtract))
                    for ct in range(2):
                        nc.vector.tensor_tensor_scan(T.cum[:, ct, :], keep, z[:, ct, :], 0.0, ALU.mult,
                                                     ALU.add).then_inc(cum_done, 1)
                if COLS[c - 1][0] not in gains:
                    continue
                name = COLS[c - 1][0]
                n0 = 8 * (name == "dk")
                g = gains[name]
                with dve.Fori(0, NT // 4) as i:
                    for b in range(4):
                        dve.wait_ge(head_sq, n0 + 4 * i + b + 1)
                        nc.vector.tensor_reduce(hss[:, b % 2, :], sq[:, b % 2, :].rearrange("p (h d) -> p h d", h=8),
                                                AX.X, ALU.add).then_inc(head_ss, 1)
                        dve.wait_ge(head_r, n0 + 4 * i + b + 1)
                        tile = dest[name][:, bass.ds(4 * i + b, 1), :].rearrange("p a (h d) -> p (a h) d", h=8)
                        nc.vector.scalar_tensor_tensor(tile, acc[b][:].rearrange("p (h d) -> p h d", h=8), UNSCALE,
                                                       lanes(hr[:, b % 2, :], 2, P, 8, DIFF_DK), ALU.mult,
                                                       ALU.mult).then_inc(acc_free, 1)
                        dve.wait_ge(acc_free, BASE + first_result[c - 1] + 4 * i + b + 1)
                        nc.vector.tensor_tensor(tile, tile, lanes(g[:], 1, P, 8, DIFF_DK),
                                                ALU.mult).then_inc(head_normed, 1)
                if name == "dq":
                    const.finish(dve)
                    gr = T.gr[:].rearrange("p t (h v) -> p (t h) v", v=GLA_DV)
                    turning.link(nc.vector.tensor_tensor(gr, gr, lanes(T.g_gla[:], 1, P, NT * GLA_H, GLA_DV), ALU.mult))
                dve.wait_ge(head_normed, n0 + NT)
                rope(dest[name], turning)

        @block.tensor
        def _(pe):
            def turn(t):
                pe.wait_ge(normed, t + 1)
                if t >= 2:
                    pe.wait_ge(lo_done, t - 1)
                for k in range(KT):
                    last = pe.transpose(turned[t % 2][:, k, :], x_in[:, t % XR, k * P:(k + 1) * P], T.ident[:])
                last.then_inc(x_turned, 1)

            pe.wait_ge(const.masks_ready, 1)
            turns = iter(range(NT))
            for t in range(NT // 2 + 2):
                turn(next(turns))
            pe.wait_ge(lo_done, NT // 2)
            pe.wait_ge(w_lo_done, PIECES)
            pe.wait_ge(acc_free, BASE)
            for half in range(2):
                if half:
                    pe.wait_ge(lo_done, NT)
                toks = slice(half * HALF, (half + 1) * HALF)
                for j in range(4):
                    r = 4 * half + j
                    if r >= 4:
                        pe.wait_ge(acc_free, BASE + r - 3)
                    for k in range(KT):
                        last = split_mm(pe, acc[r % 4][:], w_hi[:, 0, k, j * P:(j + 1) * P],
                                        w_lo[:, 0, k, j * P:(j + 1) * P], T.act_hi[:, k, toks], T.act_lo[:, k, toks],
                                        k == 0, k == KT - 1)
                    last.then_inc(acc_full, 1)
                    for t in turns:
                        turn(t)
                        break
            pe.wait_ge(w_lo_done, PIECES * 2)
            for r in range(4):
                pe.wait_ge(acc_free, BASE - 3 + first_result[1] + r)
                toks = slice(r * GA_T, (r + 1) * GA_T)
                for k in range(KT):
                    last = split_mm(pe, acc[r][0:GLA_RANK, 0:GA_T], w_hi[:, 1, k, 0:GLA_RANK],
                                    w_lo[:, 1, k, 0:GLA_RANK], T.act_hi[:, k, toks], T.act_lo[:, k, toks],
                                    k == 0, k == KT - 1)
                last.then_inc(acc_full, 1)
            for c in range(2, len(COLS)):
                pe.wait_ge(w_lo_done, PIECES * (c + 1))
                with pe.Fori(0, NT // 4) as i:
                    for b in range(4):
                        pe.wait_ge(acc_free, BASE - 3 + first_result[c] + 4 * i + b)
                        toks = bass.ds(i * (4 * P) + b * P, P)
                        for k in range(KT):
                            last = split_mm(pe, acc[b][:], T.act_hi[:, k, toks], T.act_lo[:, k, toks],
                                            w_hi[:, c % 2, k, :], w_lo[:, c % 2, k, :], k == 0, k == KT - 1)
                        last.then_inc(acc_full, 1)
                if COLS[c][0] == "gv":
                    pe.wait_ge(ga_out, 4)
                    for ct in range(2):
                        for half in range(2):
                            toks = slice(half * HALF, (half + 1) * HALF)
                            last = pe.matmul(gate[ct][:, toks], T.w_gate[:, ct * P:(ct + 1) * P], ga[:, toks],
                                             start=True, stop=True)
                        last.then_inc(gate_done, 1)


NCH = SEQ // CHUNK


def gla_states(nc, io, T):
    KVR = 4
    with ExitStack() as ctx:
        S = Space(nc, ctx, "b")
        lent = [x[:].rearrange("p k t -> p (k t)").bitcast(F32).rearrange("p (a c t) -> p a c t", a=2, c=2)
                for x in (T.act_hi, T.act_lo)]
        soft, grow = lent[0][:, 0], lent[1][:, 0]
        ke_n = lent[1][:, 1].rearrange("p c t -> p (c t)").rearrange("p (t n) -> p t n", t=NT)
        fall = S.sb("fall", [P, 2, SEQ])
        ke = S.sb("ke", [P, 2, SEQ])
        decay = S.sb("decay", [P, 2, NCH])
        turned = [S.ps(f"turned{b}", [P, 2, P]) for b in range(2)]
        kv = [S.ps(f"kv{b}", [P, 2, HALF // 2])[:, :, 0:GLA_DV] for b in range(KVR)]
        vec_step = S.sem("vec_step")
        fall_ready = S.sem("fall_ready")
        fall_done = S.sem("fall_done")
        factor = S.sem("factor")
        zeroed = S.sem("zeroed")
        ke_done = S.sem("ke_done")
        ke_turned = S.sem("ke_turned")
        ke_out = S.sem("ke_out")
        kv_done = S.sem("kv_done")
        state_done = S.sem("state_done")
        decay_done = S.sem("decay_done")
        block = ctx.enter_context(nc.Block())

        @block.gpsimd
        def _(pool):
            nc.gpsimd.memset(T.state[:, 0], 0.0).then_inc(zeroed, 1)

        @block.tensor
        def _(pe):
            pe.wait_ge(ke_done, 2)
            for t in range(NT):
                if t >= 2:
                    pe.wait_ge(ke_out, t - 1)
                for ct in range(2):
                    last = pe.transpose(turned[t % 2][:, ct, :], ke[:, ct, t * P:(t + 1) * P], T.ident[:])
                last.then_inc(ke_turned, 1)
            for t in range(NT):
                pe.wait_ge(ke_out, t + 1)
                for c in range(2):
                    n = 2 * t + c
                    if n >= KVR:
                        pe.wait_ge(state_done, n - KVR + 1)
                    rows = slice(c * CHUNK, (c + 1) * CHUNK)
                    for head in range(GLA_H):
                        ct, hh = head // 2, head % 2
                        last = pe.matmul(kv[n % KVR][hh * GLA_DK:(hh + 1) * GLA_DK, ct, :],
                                         ke_n[rows, t, head * GLA_DK:(head + 1) * GLA_DK],
                                         T.gv[rows, t, head * GLA_DV:(head + 1) * GLA_DV], start=True, stop=True)
                    last.then_inc(kv_done, 1)

        @block.scalar
        def _(act):
            for ct in range(2):
                act.wait_ge(fall_ready, ct + 1)
                nc.scalar.activation(fall[:, ct, :], fall[:, ct, :], ACT.Exp, scale=1.0 / GLA_TAU).then_inc(fall_done, 1)
            for ct in range(2):
                nc.scalar.activation(grow[:, ct, :], T.cum[:, ct, :], ACT.Exp, scale=1.0 / GLA_TAU).then_inc(factor, 1)
                nc.scalar.activation(soft[:, ct, :], T.cum[:, ct, :], ACT.Exp, scale=-1.0 / GLA_TAU).then_inc(factor, 1)
            for t in range(NT):
                act.wait_ge(ke_turned, t + 1)
                nc.scalar.activation(ke_n[:, t, :], turned[t % 2][:].rearrange("p a b -> p (a b)"),
                                     ACT.Copy).then_inc(ke_out, 1)

        @block.vector
        def _(dve):
            c = Chain(dve, vec_step)
            for ct in range(2):
                by_chunk = T.cum[:, ct, :].rearrange("p (c s) -> p c s", s=CHUNK)
                nc.vector.tensor_tensor(fall[:, ct, :].rearrange("p (c s) -> p c s", s=CHUNK),
                                        by_chunk[:, :, CHUNK - 1:CHUNK].broadcast_to([P, NCH, CHUNK]), by_chunk,
                                        ALU.subtract).then_inc(fall_ready, 1)
            for ct in range(2):
                dve.wait_ge(fall_done, ct + 1)
                nc.vector.tensor_tensor(ke[:, ct, :], T.gqk[:, 2 + ct, :], fall[:, ct, :], ALU.mult).then_inc(ke_done, 1)
            dve.wait_ge(zeroed, 1)
            dve.wait_ge(ke_done, 2)
            for ct in range(2):
                dve.wait_ge(factor, 2 * ct + 2)
                q, k = T.gqk[:, ct, :], T.gqk[:, 2 + ct, :]
                nc.vector.tensor_copy(decay[:, ct, :], grow[:, ct, :].rearrange("p (c s) -> p c s", s=CHUNK)[:, :,
                                      CHUNK - 1]).then_inc(decay_done, 1)
                c.step(nc.vector.scalar_tensor_tensor(q, grow[:, ct, :], GLA_DK ** -0.5, q, ALU.mult, ALU.mult))
                c.step(nc.vector.tensor_tensor(k, k, soft[:, ct, :], ALU.mult))
            dve.wait_ge(decay_done, 2)
            for n in range(NCH - 1):
                dve.wait_ge(kv_done, n + 1)
                if n:
                    dve.wait_ge(state_done, n)
                for ct in range(2):
                    last = nc.vector.scalar_tensor_tensor(T.state[:, n + 1, ct, :], T.state[:, n, ct, :],
                                                          decay[:, ct, n:n + 1], kv[n % KVR][:, ct, :], ALU.mult,
                                                          ALU.add)
                last.then_inc(state_done, 1)


def by_parity(ap, hh):
    return ap.rearrange("p (c h v) -> p c h v", c=2, h=2)[:, :, hh, :]


def gla_outputs(nc, io, T):
    with ExitStack() as ctx:
        S = Space(nc, ctx, "g")
        att_m = S.sb("att_m", [P, 2, GLA_H, P])
        o_s = S.sb("o_s", [P, 2, HALF])
        sq = S.sb("sq", [P, 2, HALF])
        ss = S.sb("ss", [P, NT, GLA_H])
        o_n = S.sb("o_n", [P, 2, GLA_H, GLA_DV])
        att = [[S.ps(f"att{b}{hh}", [P, 2, HALF // 2])[:, :, 0:P] for hh in range(2)] for b in range(2)]
        o = [S.ps(f"o{hh}", [P, 2, HALF // 2])[:, :, 0:GLA_DV] for hh in range(2)]
        turned = [S.ps(f"turned{b}", [P, GLA_H, P]) for b in range(2)]
        att_done = S.sem("att_done")
        masked = S.sem("masked")
        o_done = S.sem("o_done")
        o_free = S.sem("o_free")
        squared = S.sem("squared")
        summed = S.sem("summed")
        pool_step = S.sem("pool_step")
        rstd_done = S.sem("rstd_done")
        o_out = S.sem("o_out")
        o_turned = S.sem("o_turned")
        hi_done = S.sem("hi_done")
        lo_done = S.sem("lo_done")
        block = ctx.enter_context(nc.Block())

        @block.gpsimd
        def _(pool):
            c = Chain(pool, pool_step)
            for t in range(NT):
                pool.wait_ge(summed, t + 1)
                c.link(nc.gpsimd.tensor_scalar(ss[:, t, :], ss[:, t, :], 1.0 / GLA_DV, EPS, ALU.mult, ALU.add))
                nc.gpsimd.tensor_tensor(ss[:, t, :], ss[:, t, :], T.mhalf[:, 0:GLA_H],
                                        ALU.pow).then_inc(rstd_done, 1)

        @block.tensor
        def _(pe):
            def scores(t):
                if t >= 2:
                    pe.wait_ge(masked, t - 1)
                for h in range(GLA_H):
                    r = slice((h % 2) * GLA_DK, (h % 2 + 1) * GLA_DK)
                    toks = slice(t * P, (t + 1) * P)
                    last = pe.matmul(att[t % 2][h % 2][:, h // 2, :], T.gqk[r, 2 + h // 2, toks], T.gqk[r, h // 2, toks],
                                     start=True, stop=True)
                last.then_inc(att_done, 1)

            def outputs(t):
                pe.wait_ge(masked, t + 1)
                if t:
                    pe.wait_ge(o_free, t)
                for h in range(GLA_H):
                    r = slice((h % 2) * GLA_DK, (h % 2 + 1) * GLA_DK)
                    last = pe.matmul(o[h % 2][:, h // 2, :], att_m[:, t % 2, h, :], T.gv[:, t, h * GLA_DV:(h + 1) * GLA_DV],
                                     start=True, stop=False)
                    for c in range(2):
                        toks = slice(t * P + c * CHUNK, t * P + (c + 1) * CHUNK)
                        last = pe.matmul(o[h % 2][c * CHUNK:(c + 1) * CHUNK, h // 2, :], T.gqk[r, h // 2, toks],
                                         T.state[r, 2 * t + c, h // 2, :], start=False, stop=True)
                last.then_inc(o_done, 1)

            def turn(t):
                pe.wait_ge(o_out, t + 1)
                if t >= 2:
                    pe.wait_ge(lo_done, t - 1)
                for h in range(GLA_H):
                    last = pe.transpose(turned[t % 2][:, h, :], o_n[:, t % 2, h, :], T.ident[:])
                last.then_inc(o_turned, 1)

            scores(0)
            for t in range(NT + 2):
                if t + 1 < NT:
                    scores(t + 1)
                if t < NT:
                    outputs(t)
                if t >= 2:
                    turn(t - 2)

        @block.scalar
        def _(act):
            for t in range(NT + 2):
                if t < NT:
                    act.wait_ge(o_done, t + 1)
                    if t >= 2:
                        act.wait_ge(o_out, t - 1)
                    for hh in range(2):
                        last = nc.scalar.activation(by_parity(o_s[:, t % 2, :], hh), o[hh], ACT.Copy)
                    last.then_inc(o_free, 1)
                    act.wait_ge(o_free, t + 1)
                    nc.scalar.activation(sq[:, t % 2, :], o_s[:, t % 2, :], ACT.Square).then_inc(squared, 1)
                if t >= 2:
                    act.wait_ge(o_turned, t - 1)
                    nc.scalar.activation(T.act_hi[:, 0:GLA_H, (t - 2) * P:(t - 1) * P], turned[t % 2][:], ACT.Copy,
                                         scale=S_ACT).then_inc(hi_done, 1)

        @block.vector
        def _(dve):
            def mask(t):
                dve.wait_ge(att_done, t + 1)
                if t >= 2:
                    dve.wait_ge(o_done, t - 1)
                for hh in range(2):
                    last = nc.vector.tensor_tensor(by_parity(att_m[:, t % 2].rearrange("p h c -> p (h c)"), hh),
                                                   att[t % 2][hh], lanes(T.tri[:], 1, P, 2, P), ALU.mult)
                last.then_inc(masked, 1)

            def norm(t):
                dve.wait_ge(squared, t + 1)
                nc.vector.tensor_reduce(ss[:, t, :], sq[:, t % 2, :].rearrange("p (h v) -> p h v", h=GLA_H), AX.X,
                                        ALU.add).then_inc(summed, 1)
                dve.wait_ge(rstd_done, t + 1)
                if t >= 2:
                    dve.wait_ge(o_turned, t - 1)
                for h in range(GLA_H):
                    cols = slice(h * GLA_DV, (h + 1) * GLA_DV)
                    last = nc.vector.scalar_tensor_tensor(o_n[:, t % 2, h, :], o_s[:, t % 2, cols], ss[:, t, h:h + 1],
                                                          T.gr[:, t, cols], ALU.mult, ALU.mult)
                last.then_inc(o_out, 1)

            mask(0)
            for t in range(NT + 2):
                if t + 1 < NT:
                    mask(t + 1)
                if 1 <= t <= NT:
                    norm(t - 1)
                if t >= 2:
                    dve.wait_ge(hi_done, t - 1)
                    toks = slice((t - 2) * P, (t - 1) * P)
                    nc.vector.scalar_tensor_tensor(T.act_lo[:, 0:GLA_H, toks], turned[t % 2][:], S_ACT,
                                                   T.act_hi[:, 0:GLA_H, toks], ALU.mult,
                                                   ALU.subtract).then_inc(lo_done, 1)


def diff_attention(nc, io, T):
    SCALE = DIFF_DK ** -0.5
    units = [(b, h) for b in range(NT) for h in range(DIFF_H)]
    with ExitStack() as ctx:
        S = Space(nc, ctx, "d")
        q_t = S.sb("q_t", [P, DIFF_H, SEQ])
        k_t = S.sb("k_t", [P, DIFF_H, SEQ])
        ident = S.sb("ident", [P, P], BF16)
        causal = S.sb("causal", [P, P], BF16)
        mx = S.sb("mx", [P, 2, 2])
        sums = S.sb("sums", [P, 2, 2])
        inv = S.sb("inv", [P, 2, 2])
        mix = S.sb("mix", [P, 2])
        e = S.sb("e", [P, 2, 2, SEQ])
        a = S.sb("a", [P, 2, SEQ])
        a_t = S.sb("a_t", [P, 2, SEQ])
        junk = S.sb("junk", [P, DIFF_DV])
        ss = S.sb("ss", [P, 2])
        o_s = S.sb("o_s", [P, 2, DIFF_DV])
        o_n = S.sb("o_n", [P, 2, DIFF_H, DIFF_DV])
        sc = [S.ps(f"sc{m}", [P, SEQ]) for m in range(2)]
        qk_ps = [sc[n // 2][:, n % 2 * HALF:(n % 2 + 1) * HALF].rearrange("p (h t) -> p h t", h=DIFF_H)
                 for n in range(4)]
        a_ps = S.ps("a_ps", [P, SEQ])
        o = S.ps("o", [P, DIFF_DV])
        turned = S.ps("turned", [P, DIFF_H, P])
        mask_ready = S.sem("mask_ready")
        qk_turned = S.sem("qk_turned")
        qk_out = S.sem("qk_out")
        scored = [S.sem(f"scored{m}") for m in range(2)]
        max_done = [S.sem(f"max_done{m}") for m in range(2)]
        vec_step = S.sem("vec_step")
        exp_done = [S.sem(f"exp_done{m}") for m in range(2)]
        combined = S.sem("combined")
        a_turned = S.sem("a_turned")
        a_out = S.sem("a_out")
        o_done = S.sem("o_done")
        o_scaled = S.sem("o_scaled")
        squared = S.sem("squared")
        pool_step = S.sem("pool_step")
        rstd_done = S.sem("rstd_done")
        o_out = S.sem("o_out")
        o_turned = S.sem("o_turned")
        hi_done = S.sem("hi_done")
        lo_done = S.sem("lo_done")
        block = ctx.enter_context(nc.Block())

        @block.gpsimd
        def _(pool):
            nc.gpsimd.tensor_copy(ident[:], T.ident[:]).then_inc(mask_ready, 1)
            nc.gpsimd.tensor_copy(causal[:], T.causal[:]).then_inc(mask_ready, 1)
            c = Chain(pool, pool_step)
            for u in range(len(units)):
                pool.wait_ge(squared, u + 1)
                s = ss[:, u % 2:u % 2 + 1]
                c.link(nc.gpsimd.tensor_scalar(s, s, 1.0 / DIFF_DV, EPS, ALU.mult, ALU.add))
                nc.gpsimd.tensor_tensor(s, s, T.mhalf[:, 0:1], ALU.pow).then_inc(rstd_done, 1)

        @block.tensor
        def _(pe):
            pe.wait_ge(mask_ready, 2)
            n = 0
            for t in range(NT):
                for x in (T.dq, T.dk):
                    if n >= 4:
                        pe.wait_ge(qk_out, n - 3)
                    for h in range(DIFF_H):
                        last = pe.transpose(qk_ps[n % 4][:, h, :], x[:, t, h * P:(h + 1) * P], T.ident[:])
                    last.then_inc(qk_turned, 1)
                    n += 1
            pe.wait_ge(qk_out, n)

            def scores(u, m):
                b, h = units[u]
                keys = (b + 1) * P
                if u:
                    pe.wait_ge(exp_done[m], u)
                r = slice(m * DIFF_DK, (m + 1) * DIFF_DK)
                for k0 in range(0, keys, HALF):
                    k1 = min(keys, k0 + HALF)
                    pe.matmul(sc[m][:, k0:k1], q_t[r, h, b * P:(b + 1) * P], k_t[r, h, k0:k1], start=True,
                              stop=(k1 < keys))
                pe.matmul(sc[m][:, b * P:keys], ident[:], causal[:], start=False, stop=True).then_inc(scored[m], 1)

            def turn_probs(u):
                b, h = units[u]
                pe.wait_ge(combined, u + 1)
                if u:
                    pe.wait_ge(a_out, u)
                for kb in range(b + 1):
                    last = pe.transpose(a_ps[:, kb * P:(kb + 1) * P], a[:, u % 2, kb * P:(kb + 1) * P], T.ident[:])
                last.then_inc(a_turned, 1)

            def values(u):
                b, h = units[u]
                pe.wait_ge(a_out, u + 1)
                if u:
                    pe.wait_ge(o_scaled, u)
                for kb in range(b + 1):
                    last = pe.matmul(o[:], a_t[:, u % 2, kb * P:(kb + 1) * P], T.dv[:, kb, h * DIFF_DV:(h + 1) * DIFF_DV],
                                     start=(kb == 0), stop=(kb == b))
                last.then_inc(o_done, 1)

            def turn(b):
                pe.wait_ge(o_out, DIFF_H * (b + 1))
                if b:
                    pe.wait_ge(lo_done, b)
                for h in range(DIFF_H):
                    last = pe.transpose(turned[:, h, :], o_n[:, b % 2, h, :], T.ident[:])
                last.then_inc(o_turned, 1)

            for m in range(2):
                scores(0, m)
            for u, (b, h) in enumerate(units):
                more = u + 1 < len(units)
                if more:
                    scores(u + 1, 0)
                turn_probs(u)
                if more:
                    scores(u + 1, 1)
                values(u)
                if h == 1 and b:
                    turn(b - 1)
            turn(NT - 1)

        @block.scalar
        def _(act):
            n = 0
            for t in range(NT):
                for x in (q_t, k_t):
                    act.wait_ge(qk_turned, n + 1)
                    nc.scalar.activation(x[:, :, t * P:(t + 1) * P], qk_ps[n % 4], ACT.Copy).then_inc(qk_out, 1)
                    n += 1

            def exps(u, m):
                b, h = units[u]
                act.wait_ge(max_done[m], u + 1)
                if u >= 2:
                    act.wait_ge(combined, u - 1)
                nc.scalar.activation(e[:, u % 2, m, 0:(b + 1) * P], sc[m][:, 0:(b + 1) * P], ACT.Exp,
                                     bias=mx[:, u % 2, m:m + 1], scale=SCALE,
                                     accum_out=sums[:, u % 2, m:m + 1]).then_inc(exp_done[m], 1)

            def probs_out(u):
                b, h = units[u]
                act.wait_ge(a_turned, u + 1)
                if u >= 2:
                    act.wait_ge(o_done, u - 1)
                nc.scalar.activation(a_t[:, u % 2, 0:(b + 1) * P], a_ps[:, 0:(b + 1) * P], ACT.Copy).then_inc(a_out, 1)

            def output(u):
                act.wait_ge(o_done, u + 1)
                if u >= 2:
                    act.wait_ge(o_out, u - 1)
                nc.scalar.activation(o_s[:, u % 2, :], o[:], ACT.Copy, scale=inv[:, u % 2, 0:1]).then_inc(o_scaled, 1)
                act.wait_ge(o_scaled, u + 1)
                if u:
                    act.wait_ge(squared, u)
                nc.scalar.activation(junk[:], o_s[:, u % 2, :], ACT.Square,
                                     accum_out=ss[:, u % 2:u % 2 + 1]).then_inc(squared, 1)

            def turned_hi(b):
                act.wait_ge(o_turned, b + 1)
                nc.scalar.activation(T.act_hi[:, DIFF_H:2 * DIFF_H, b * P:(b + 1) * P], turned[:], ACT.Copy,
                                     scale=T.g_sub[:, 0:1]).then_inc(hi_done, 1)

            for m in range(2):
                exps(0, m)
            for u, (b, h) in enumerate(units):
                probs_out(u)
                if u + 1 < len(units):
                    for m in range(2):
                        exps(u + 1, m)
                output(u)
                if h == 1 and b:
                    turned_hi(b - 1)
            turned_hi(NT - 1)

        @block.vector
        def _(dve):
            c = Chain(dve, vec_step)

            def maximum(u, m):
                b, h = units[u]
                dve.wait_ge(scored[m], u + 1)
                if u >= 2:
                    dve.wait_ge(exp_done[m], u - 1)
                c.link(nc.vector.tensor_reduce(mx[:, u % 2, m:m + 1], sc[m][:, 0:(b + 1) * P], AX.X, ALU.max))
                nc.vector.tensor_scalar(mx[:, u % 2, m:m + 1], mx[:, u % 2, m:m + 1], -SCALE, None,
                                        ALU.mult).then_inc(max_done[m], 1)

            def combine(u):
                b, h = units[u]
                for m in range(2):
                    dve.wait_ge(exp_done[m], u + 1)
                if u >= 2:
                    dve.wait_ge(o_scaled, u - 1)
                    dve.wait_ge(a_turned, u - 1)
                c.link(nc.vector.reciprocal(inv[:, u % 2, :], sums[:, u % 2, :]))
                c.link(nc.vector.scalar_tensor_tensor(mix[:, u % 2:u % 2 + 1], inv[:, u % 2, 1:2], sums[:, u % 2, 0:1],
                                                      T.neg_lam[:], ALU.mult, ALU.mult))
                nc.vector.scalar_tensor_tensor(a[:, u % 2, 0:(b + 1) * P], e[:, u % 2, 1, 0:(b + 1) * P],
                                               mix[:, u % 2:u % 2 + 1], e[:, u % 2, 0, 0:(b + 1) * P], ALU.mult,
                                               ALU.add).then_inc(combined, 1)

            def norm(u):
                b, h = units[u]
                dve.wait_ge(rstd_done, u + 1)
                if h == 0 and b >= 2:
                    dve.wait_ge(o_turned, b - 1)
                nc.vector.tensor_scalar(o_n[:, b % 2, h, :], o_s[:, u % 2, :], ss[:, u % 2:u % 2 + 1], None,
                                        ALU.mult).then_inc(o_out, 1)

            def turned_lo(b):
                dve.wait_ge(hi_done, b + 1)
                toks = slice(b * P, (b + 1) * P)
                nc.vector.scalar_tensor_tensor(T.act_lo[:, DIFF_H:2 * DIFF_H, toks], turned[:], T.g_sub[:, 0:1],
                                               T.act_hi[:, DIFF_H:2 * DIFF_H, toks], ALU.mult,
                                               ALU.subtract).then_inc(lo_done, 1)

            for m in range(2):
                maximum(0, m)
            for u, (b, h) in enumerate(units):
                combine(u)
                if u + 1 < len(units):
                    for m in range(2):
                        maximum(u + 1, m)
                if u:
                    norm(u - 1)
                if h == 2 and b:
                    turned_lo(b - 1)
            norm(len(units) - 1)
            turned_lo(NT - 1)


def project_out(nc, io, T):
    with ExitStack() as ctx:
        S = Space(nc, ctx, "o")
        w_in = S.sb("w_in", [P, 2, D])
        w_hi = S.sb("w_hi", [P, KT, D], F16)
        w_lo = S.sb("w_lo", [P, KT, D], F16)
        x_in = S.sb("x_in", [P, 2, D])
        xs = S.sb("xs", [P, 2, D])
        junk = S.sb("junk", [P, D], F16)
        ss = S.sb("ss", [P, NT])
        acc = [S.ps(f"acc{b}", [P, D]) for b in range(2)]
        turned = [S.ps(f"turned{b}", [P, KT, P]) for b in range(2)]
        w_loaded = [S.sem(f"w_loaded{b}") for b in range(2)]
        x_loaded = [S.sem(f"x_loaded{b}") for b in range(2)]
        w_hi_done = S.sem("w_hi_done")
        w_lo_done = S.sem("w_lo_done")
        acc_done = S.sem("acc_done")
        h_done = S.sem("h_done")
        squared = S.sem("squared")
        pool_step = S.sem("pool_step")
        rstd_done = S.sem("rstd_done")
        normed = S.sem("normed")
        x_turned = S.sem("x_turned")
        hi_done = S.sem("hi_done")
        lo_done = S.sem("lo_done")
        block = ctx.enter_context(nc.Block())

        @block.sync
        def _(sp):
            for k in range(KT):
                if k >= 2:
                    sp.wait_ge(w_lo_done, k - 1)
                sp.dma_start(w_in[:, k % 2, :], io.w_out[0, k * P:(k + 1) * P, :]).then_inc(w_loaded[k % 2], 16)
            for t in range(NT):
                if t >= 2:
                    sp.wait_ge(h_done, t - 1)
                sp.dma_start(x_in[:, t % 2, :], io.x[0, t * P:(t + 1) * P, :]).then_inc(x_loaded[t % 2], 16)

        @block.gpsimd
        def _(pool):
            c = Chain(pool, pool_step)
            for t in range(NT):
                pool.wait_ge(squared, t + 1)
                c.link(nc.gpsimd.tensor_scalar(ss[:, t:t + 1], ss[:, t:t + 1], 1.0 / D, EPS, ALU.mult, ALU.add))
                nc.gpsimd.tensor_tensor(ss[:, t:t + 1], ss[:, t:t + 1], T.mhalf[:, 0:1], ALU.pow).then_inc(rstd_done, 1)

        @block.tensor
        def _(pe):
            def project(t):
                if t >= 2:
                    pe.wait_ge(h_done, t - 1)
                toks = slice(t * P, (t + 1) * P)
                for k in range(KT):
                    if t == 0:
                        pe.wait_ge(w_lo_done, k + 1)
                    for half in range(2):
                        cols = slice(half * HALF, (half + 1) * HALF)
                        last = split_mm(pe, acc[t % 2][:, cols], T.act_hi[:, k, toks], T.act_lo[:, k, toks],
                                        w_hi[:, k, cols], w_lo[:, k, cols], k == 0, k == KT - 1)
                last.then_inc(acc_done, 1)

            def turn(t):
                pe.wait_ge(normed, t + 1)
                if t >= 2:
                    pe.wait_ge(lo_done, t - 1)
                for k in range(KT):
                    last = pe.transpose(turned[t % 2][:, k, :], xs[:, t % 2, k * P:(k + 1) * P], T.ident[:])
                last.then_inc(x_turned, 1)

            project(0)
            for t in range(NT):
                if t + 1 < NT:
                    project(t + 1)
                turn(t)

        @block.scalar
        def _(act):
            for k in range(KT):
                act.wait_ge(w_loaded[k % 2], 16 * (k // 2 + 1))
                nc.scalar.activation(w_hi[:, k, :], w_in[:, k % 2, :], ACT.Copy, scale=S_W).then_inc(w_hi_done, 1)
            for t in range(NT + 1):
                if t < NT:
                    act.wait_ge(h_done, t + 1)
                    if t:
                        act.wait_ge(squared, t)
                    nc.scalar.activation(junk[:], T.h[:, t, :], ACT.Square,
                                         accum_out=ss[:, t:t + 1]).then_inc(squared, 1)
                if t:
                    act.wait_ge(x_turned, t)
                    for k in range(KT):
                        last = nc.scalar.activation(T.act_hi[:, k, (t - 1) * P:t * P], turned[(t - 1) % 2][:, k, :],
                                                    ACT.Copy, scale=T.g_ffn[:, k:k + 1])
                    last.then_inc(hi_done, 1)

        @block.vector
        def _(dve):
            for k in range(KT):
                dve.wait_ge(w_hi_done, k + 1)
                nc.vector.scalar_tensor_tensor(w_lo[:, k, :], w_in[:, k % 2, :], S_W, w_hi[:, k, :], ALU.mult,
                                               ALU.subtract).then_inc(w_lo_done, 1)
            for t in range(NT + 1):
                if t < NT:
                    dve.wait_ge(acc_done, t + 1)
                    dve.wait_ge(x_loaded[t % 2], 16 * (t // 2 + 1))
                    nc.vector.scalar_tensor_tensor(T.h[:, t, :], acc[t % 2][:], UNSCALE, x_in[:, t % 2, :], ALU.mult,
                                                   ALU.add).then_inc(h_done, 1)
                    dve.wait_ge(rstd_done, t + 1)
                    if t >= 2:
                        dve.wait_ge(x_turned, t - 1)
                    nc.vector.tensor_scalar(xs[:, t % 2, :], T.h[:, t, :], ss[:, t:t + 1], None,
                                            ALU.mult).then_inc(normed, 1)
                if t:
                    dve.wait_ge(hi_done, t)
                    toks = slice((t - 1) * P, t * P)
                    for k in range(KT):
                        last = nc.vector.scalar_tensor_tensor(T.act_lo[:, k, toks], turned[(t - 1) % 2][:, k, :],
                                                              T.g_ffn[:, k:k + 1], T.act_hi[:, k, toks], ALU.mult,
                                                              ALU.subtract)
                    last.then_inc(lo_done, 1)


S_U = 64.0
EARLY_R = 2
EARLY_S = 3
BLOCK = 64
NBLOCK = SEQ // BLOCK
TB = 32
NTB = SEQ // TB
N_EARLY = EARLY_R * PEER_H + EARLY_S * NBLOCK


class EarlyTiles:

    def __init__(self, nc, io, T, S, ring, first, count):
        self.nc, self.T, self.ring = nc, T, ring
        rows = io.peer_u[0, first * P:(first + count) * P, :]
        self.u_rows = rows.rearrange("(c b p) d -> c b p d", b=ring, p=P)
        self.kept_rows = T.kept[first * P:(first + count) * P, :].rearrange("(c b p) t -> c b p t", b=ring, p=P)
        self.u_in = [S.sb(f"u_in{b}", [P, D]) for b in range(ring)]
        self.u_hi = [S.sb(f"u_hi{b}", [P, KT, P], F16) for b in range(ring)]
        self.u_lo = [S.sb(f"u_lo{b}", [P, KT, P], F16) for b in range(ring)]
        self.u_all = S.sb("u_all", [P, KT, P])
        self.gel = [S.sb(f"gel{b}", [P, SEQ]) for b in range(ring)]
        self.u_ps = S.ps("u_ps", [P, KT, P])
        self.hid = [S.ps(f"hid{b}", [P, HALF]) for b in range(2)]
        self.u_loaded = [S.sem(f"u_loaded{b}") for b in range(ring)]
        self.u_turned = S.sem("u_turned")
        self.u_hi_done = S.sem("u_hi_done")
        self.u_all_done = S.sem("u_all_done")
        self.u_lo_done = S.sem("u_lo_done")
        self.hid_done = S.sem("hid_done")
        self.gelu_done = S.sem("gelu_done")
        self.kept = [S.sem(f"kept{b}") for b in range(ring)]

    def prime_tensor(self, pe):
        pe.sem_inc(self.hid_done, BASE)

    def prime_scalar(self, act):
        act.sem_inc(self.u_all_done, BASE)
        act.sem_inc(self.gelu_done, BASE)
        for b in range(self.ring):
            act.sem_inc(self.kept[b], BASE)

    def prime_gpsimd(self, pool):
        pool.sem_inc(self.u_lo_done, BASE)

    def load(self, sp, c, b, again=True):
        if again:
            sp.wait_ge(self.u_turned, (c - 1) * self.ring + b + 1)
        sp.dma_start(self.u_in[b][:], self.u_rows[c, b]).then_inc(self.u_loaded[b], 16)

    def keep(self, sp, c, b):
        sp.wait_ge(self.gelu_done, BASE + 2 * (c * self.ring + b) + 2)
        sp.dma_start(self.kept_rows[c, b], self.gel[b][:]).then_inc(self.kept[b], 16)

    def all_kept(self, sp, count):
        for b in range(self.ring):
            sp.wait_ge(self.kept[b], BASE + 16 * (count // self.ring))

    def turn(self, pe, c, b):
        pe.wait_ge(self.u_loaded[b], c * 16 + 16)
        pe.wait_ge(self.u_all_done, BASE + c * self.ring + b)
        for k in range(KT):
            last = pe.transpose(self.u_ps[:, k, :], self.u_in[b][:, k * P:(k + 1) * P], self.T.ident[:])
        last.then_inc(self.u_turned, 1)

    def split(self, act, c, b):
        n = c * self.ring + b
        act.wait_ge(self.u_turned, n + 1)
        act.wait_ge(self.hid_done, BASE + 2 * (n - self.ring) + 2)
        self.nc.scalar.activation(self.u_hi[b][:], self.u_ps[:], ACT.Copy, scale=S_U).then_inc(self.u_hi_done, 1)
        act.wait_ge(self.u_lo_done, BASE + n)
        self.nc.scalar.activation(self.u_all[:], self.u_ps[:], ACT.Copy, scale=S_U).then_inc(self.u_all_done, 1)

    def low(self, pool, c, b):
        n = c * self.ring + b
        pool.wait_ge(self.u_hi_done, n + 1)
        pool.wait_ge(self.u_all_done, BASE + n + 1)
        self.nc.gpsimd.tensor_tensor(self.u_lo[b][:], self.u_all[:], self.u_hi[b][:],
                                     ALU.subtract).then_inc(self.u_lo_done, 1)

    def hidden(self, pe, c, b, half):
        n = c * self.ring + b
        if half == 0:
            pe.wait_ge(self.u_lo_done, BASE + n + 1)
        pe.wait_ge(self.gelu_done, BASE + 2 * (n - 1) + half + 1)
        toks = slice(half * HALF, (half + 1) * HALF)
        for k in range(KT):
            last = split_mm(pe, self.hid[half][:], self.u_hi[b][:, k, :], self.u_lo[b][:, k, :],
                            self.T.act_hi[:, k, toks], self.T.act_lo[:, k, toks], k == 0, k == KT - 1)
        last.then_inc(self.hid_done, 1)

    def gelu(self, act, c, b, half):
        n = c * self.ring + b
        if half == 0:
            act.wait_ge(self.kept[b], BASE + 16 * c)
        act.wait_ge(self.hid_done, BASE + 2 * n + half + 1)
        self.nc.scalar.activation(self.gel[b][:, half * HALF:(half + 1) * HALF], self.hid[half][:], ACT.Gelu,
                                  scale=1.0 / (S_U * S_ACT)).then_inc(self.gelu_done, 1)


NSET = 2 * PEER_H
FLOOR = -3.0e38


def retrieve(nc, io, T):
    with ExitStack() as ctx:
        S = Space(nc, ctx, "r")
        E = EarlyTiles(nc, io, T, S, EARLY_R, 0, EARLY_R * PEER_H)
        w_in = S.sb("w_in", [P, KT, QDIM])
        w_hi = [S.sb(f"w_hi{b}", [P, KT, QDIM], F16) for b in range(2)]
        w_lo = [S.sb(f"w_lo{b}", [P, KT, QDIM], F16) for b in range(2)]
        keys_t = S.sb("keys_t", [P, NSET, P])
        q_t = S.sb("q_t", [P, 2, SEQ])
        s = T.picked_all[:, 0:2 * SEQ].rearrange("p (t m k) -> p t m k", t=NT, m=2)
        s2 = S.sb("s2", [P, NT, 2, NKEYS])
        keys = s2[:].rearrange("p t m k -> p (t m) k")
        top = S.sb("top", [P, NT, 2, TOPK])
        top_i = S.sb("top_i", [P, NT, 2, TOPK], U32)
        top_f = S.sb("top_f", [P, 2, NT, 2, TOPK], F16)
        cand = S.sb("cand", [P, NT, TOPK * TOPK])
        cand2 = s2[:].rearrange("p t m k -> p t (m k)")
        best = S.sb("best", [P, NT, TOPK])
        pos = S.sb("pos", [P, NT * TOPK], U32)
        part = S.sb("part", [P, 2, NT * TOPK], U32)
        part_f = S.sb("part_f", [P, 2, NT * TOPK], F16)
        weight = S.sb("weight", [P, NT, TOPK])
        total = S.sb("total", [P, NT])
        carrier = S.sb("carrier", [1, 1])
        match = S.sb("match", [P, 2, NT * TOPK, TOPK], F16)
        picked = [S.sb(f"picked{n}", [P, NT, PICKS]) for n in range(3)]
        bank = [S.ps(f"bank{r}", [P, 4, NKEYS]) for r in range(4)]

        w_loaded = S.sem("w_loaded")
        keys_loaded = S.sem("keys_loaded")
        w_scaled = S.sem("w_scaled")
        w_hi_done = S.sem("w_hi_done")
        w_lo_done = S.sem("w_lo_done")
        keys_turned = S.sem("keys_turned")
        keys_out = S.sem("keys_out")
        q_done = S.sem("q_done")
        q_out = S.sem("q_out")
        scored = S.sem("scored")
        s_out = S.sem("s_out")
        vec_step = S.sem("vec_step")
        s_used = S.sem("s_used")
        shifted = S.sem("shifted")
        weighted = S.sem("weighted")
        found = S.sem("found")
        matched = S.sem("matched")
        index_done = S.sem("index_done")
        weight_done = S.sem("weight_done")
        all_turned = S.sem("all_turned")
        all_out = S.sem("all_out")
        block = ctx.enter_context(nc.Block())
        PAIRS = PEER_H // 2

        @block.sync
        def _(sp):
            w_v = io.w_peer_q[0].rearrange("(k p) (h c) -> h p k c", p=P, c=QDIM)

            def load_w(h):
                sp.dma_start(w_in[:], w_v[h]).then_inc(w_loaded, 16)

            def step(hh, b, last):
                h = 2 * hh + b
                if not last:
                    sp.wait_ge(w_lo_done, h + 2)
                    load_w(h + 2)
                for r in range(EARLY_R):
                    E.keep(sp, h, r)
                    if not (last and b):
                        E.load(sp, h + 1, r)

            load_w(0)
            sp.dma_start(keys, io.peer_sub_keys[0].rearrange("h m k q -> k (h m) q")).then_inc(keys_loaded, 16)
            for r in range(EARLY_R):
                E.load(sp, 0, r, again=False)
            sp.wait_ge(w_lo_done, 1)
            load_w(1)
            with sp.Fori(0, PAIRS - 1) as hh:
                for b in range(2):
                    step(hh, b, False)
            for b in range(2):
                step(PAIRS - 1, b, True)
            E.all_kept(sp, EARLY_R * PEER_H)

        @block.tensor
        def _(pe):
            E.prime_tensor(pe)

            def queries(h, slot, first=False):
                pe.wait_ge(w_lo_done, h + 1)
                for r in range(4):
                    m, half = r // 2, r % 2
                    if first:
                        pe.wait_ge(keys_out, r + 1)
                    else:
                        pe.wait_ge(s_out, 4 * (h - 1) + r + 1)
                    toks, cols = slice(half * HALF, (half + 1) * HALF), slice(m * P, (m + 1) * P)
                    for k in range(KT):
                        last = split_mm(pe, bank[r][:].rearrange("p a b -> p (a b)"), w_hi[slot][:, k, cols],
                                        w_lo[slot][:, k, cols], T.act_hi[:, k, toks], T.act_lo[:, k, toks],
                                        k == 0, k == KT - 1)
                    last.then_inc(q_done, 1)

            def scores(h):
                for m in range(2):
                    pe.wait_ge(q_out, 4 * h + 2 * m + 2)
                    for g in range(2):
                        for j in range(4):
                            t = 4 * g + j
                            last = pe.matmul(bank[2 * m + g][:, j, :], q_t[:, m, t * P:(t + 1) * P],
                                             keys_t[:, bass.ds(2 * h + m, 1), :].rearrange("p a k -> p (a k)"),
                                             start=True, stop=True)
                        last.then_inc(scored, 1)

            def step(hh, b, last):
                h = 2 * hh + b
                E.turn(pe, h, 0)
                if not (last and b):
                    queries(h + 1, 1 - b)
                    scores(h + 1)
                E.hidden(pe, h, 0, 0)
                E.turn(pe, h, 1)
                E.hidden(pe, h, 0, 1)
                E.hidden(pe, h, 1, 0)
                E.hidden(pe, h, 1, 1)

            pe.wait_ge(keys_loaded, 16)
            for r in range(4):
                for j in range(4):
                    last = pe.transpose(bank[r][:, j, :], keys[:, 4 * r + j, :], T.ident[:])
                last.then_inc(keys_turned, 1)
            queries(0, 0, first=True)
            scores(0)
            with pe.Fori(0, PAIRS - 1) as hh:
                for b in range(2):
                    step(hh, b, False)
            for b in range(2):
                step(PAIRS - 1, b, True)
            pe.wait_ge(index_done, BASE + 2 * PEER_H)
            pe.wait_ge(weight_done, PEER_H)
            for n in range(3):
                for g in range(2):
                    r = 2 * n + g
                    if r >= 4:
                        pe.wait_ge(all_out, r - 3)
                    for j in range(4):
                        last = pe.transpose(bank[r % 4][:, j, :], picked[n][:, 4 * g + j, :], T.ident[:])
                    last.then_inc(all_turned, 1)

        @block.scalar
        def _(act):
            E.prime_scalar(act)

            def split_w(h, slot):
                act.wait_ge(w_loaded, 16 * h + 16)
                nc.scalar.activation(w_in[:], w_in[:], ACT.Copy, scale=S_W).then_inc(w_scaled, 1)
                act.wait_ge(w_scaled, h + 1)
                nc.scalar.activation(w_hi[slot][:], w_in[:], ACT.Copy).then_inc(w_hi_done, 1)

            def queries_out(h):
                for r in range(4):
                    m, half = r // 2, r % 2
                    act.wait_ge(q_done, 4 * h + r + 1)
                    nc.scalar.activation(q_t[:, m, half * HALF:(half + 1) * HALF],
                                         bank[r][:].rearrange("p a b -> p (a b)"), ACT.Copy,
                                         scale=UNSCALE).then_inc(q_out, 1)

            def scores_out(h, first=False):
                if not first:
                    act.wait_ge(s_used, h)
                for m in range(2):
                    for g in range(2):
                        act.wait_ge(scored, 4 * h + 2 * m + g + 1)
                        nc.scalar.activation(s[:, 4 * g:4 * g + 4, m, :], bank[2 * m + g][:],
                                             ACT.Copy).then_inc(s_out, 1)

            def step(hh, b, last):
                h = 2 * hh + b
                E.split(act, h, 0)
                if not last:
                    split_w(h + 2, b)
                if not (last and b):
                    act.wait_ge(scored, 4 * h + 4)
                    queries_out(h + 1)
                    scores_out(h + 1)
                E.gelu(act, h, 0, 0)
                E.split(act, h, 1)
                E.gelu(act, h, 0, 1)
                act.wait_ge(shifted, h + 1)
                nc.scalar.activation(weight[:], weight[:], ACT.Exp).then_inc(weighted, 1)
                E.gelu(act, h, 1, 0)
                E.gelu(act, h, 1, 1)

            split_w(0, 0)
            for r in range(4):
                act.wait_ge(keys_turned, r + 1)
                nc.scalar.activation(keys_t[:, 4 * r:4 * r + 4, :], bank[r][:], ACT.Copy).then_inc(keys_out, 1)
            split_w(1, 1)
            queries_out(0)
            scores_out(0, first=True)
            with act.Fori(0, PAIRS - 1) as hh:
                for b in range(2):
                    step(hh, b, False)
            for b in range(2):
                step(PAIRS - 1, b, True)
            for r in range(6):
                act.wait_ge(all_turned, r + 1)
                n, g = r // 2, r % 2
                nc.scalar.activation(T.picked_t[n][:, g * HALF:(g + 1) * HALF], bank[r % 4][:].rearrange(
                    "p a b -> p (a b)"), ACT.Copy).then_inc(all_out, 1)

        @block.gpsimd
        def _(pool):
            E.prime_gpsimd(pool)

            def low_w(h, slot):
                pool.wait_ge(w_hi_done, h + 1)
                nc.gpsimd.tensor_tensor(w_lo[slot][:], w_in[:], w_hi[slot][:], ALU.subtract).then_inc(w_lo_done, 1)

            def step(hh, b, last):
                h = 2 * hh + b
                E.low(pool, h, 0)
                if not last:
                    low_w(h + 2, b)
                E.low(pool, h, 1)
                for n in range(2):
                    pool.wait_ge(found, 2 * h + n + 1)
                    got = match[:, n].rearrange("p (t k) a -> p t k a", t=NT)
                    nc.gpsimd.tensor_tensor(got, got, top_f[:, b, :, n, :].unsqueeze(2).broadcast_to(
                        [P, NT, TOPK, TOPK]), ALU.mult).then_inc(matched, 1)

            for h in range(2):
                low_w(h, h)
            with pool.Fori(0, PAIRS - 1) as hh:
                for b in range(2):
                    step(hh, b, False)
            for b in range(2):
                step(PAIRS - 1, b, True)

        @block.vector
        def _(dve):
            dve.sem_inc(index_done, BASE)
            def top16(c, values, rest, out, idx):
                def settled():
                    c.wait()
                    c.step(nc.vector.tensor_copy(carrier[:], T.iota[0:1, 0:1]))

                settled()
                for v, o in zip(values, out):
                    c.step(nc.vector.max(o[:, 0:8], v))
                settled()
                for v, w, o, i in zip(values, rest, out, idx):
                    c.step(nc.vector.max_index(i[:, 0:8], o[:, 0:8], v))
                    c.step(nc.vector.match_replace(w, o[:, 0:8], v, FLOOR))
                settled()
                for w, o in zip(rest, out):
                    c.step(nc.vector.max(o[:, 8:16], w))
                settled()
                for w, o, i in zip(rest, out, idx):
                    c.step(nc.vector.max_index(i[:, 8:16], o[:, 8:16], w))
                c.wait()

            def index_sum(h, n):
                dve.wait_ge(matched, 2 * h + n + 1)
                out = picked[n][:, :, bass.ds(h * TOPK, TOPK)]
                nc.vector.tensor_reduce(out, match[:, n].rearrange("p (t k) a -> p t k a", t=NT), AX.X,
                                        ALU.add).then_inc(index_done, 1)

            STEPS = 134
            with dve.Fori(0, PEER_H // 2) as hh:
                for b in range(2):
                    h = 2 * hh + b
                    c = Chain(dve, vec_step, STEPS * h)
                    both = [(t, m) for t in range(NT) for m in range(2)]
                    dve.wait_ge(s_out, 4 * h + 4)
                    top16(c, [s[:, t, m, :] for t, m in both], [s2[:, t, m, :] for t, m in both],
                          [top[:, t, m, :] for t, m in both], [top_i[:, t, m, :] for t, m in both])
                    nc.vector.tensor_copy(top_f[:, b], top_i[:]).then_inc(s_used, 1)
                    c.step(nc.vector.tensor_tensor(
                        cand[:].rearrange("p t (a b) -> p t a b", a=TOPK),
                        top[:, :, 0, :].unsqueeze(3).broadcast_to([P, NT, TOPK, TOPK]),
                        top[:, :, 1, :].unsqueeze(2).broadcast_to([P, NT, TOPK, TOPK]), ALU.add))
                    c.wait()
                    tiles = range(NT)
                    top16(c, [cand[:, t, :] for t in tiles], [cand2[:, t, :] for t in tiles],
                          [best[:, t, :] for t in tiles], [pos[:, t * TOPK:(t + 1) * TOPK] for t in tiles])
                    c.step(nc.vector.tensor_scalar(part[:, 0, :], pos[:], 4, None, ALU.logical_shift_right))
                    c.step(nc.vector.tensor_scalar(part[:, 1, :], pos[:], TOPK - 1, None, ALU.bitwise_and))
                    nc.vector.tensor_tensor(weight[:], best[:], best[:, :, 0:1].broadcast_to([P, NT, TOPK]),
                                            ALU.subtract).then_inc(shifted, 1)
                    c.wait()
                    c.step(nc.vector.tensor_copy(part_f[:], part[:]))
                    c.wait()
                    if b:
                        for n in range(2):
                            index_sum(h - 1, n)
                    for n in range(2):
                        dve.wait_ge(index_done, BASE + 2 * h)
                        nc.vector.tensor_tensor(match[:, n], lanes(part_f[:, n, :], 2, P, NT * TOPK, TOPK),
                                                lanes(T.iota[:, 0:TOPK], 1, P, NT * TOPK, TOPK),
                                                ALU.is_equal).then_inc(found, 1)
                    dve.wait_ge(weighted, h + 1)
                    c.link(nc.vector.tensor_reduce(total[:], weight[:], AX.X, ALU.add))
                    c.link(nc.vector.reciprocal(total[:], total[:]))
                    nc.vector.tensor_tensor(picked[2][:, :, bass.ds(h * TOPK, TOPK)], weight[:],
                                            lanes(total[:], 2, P, NT, TOPK), ALU.mult).then_inc(weight_done, 1)
                    if b:
                        for n in range(2):
                            index_sum(h, n)
                    assert c.n == STEPS, c.n

BANK_T = 4
S_G = 1024.0


def spread_weights(nc, io, T):
    RING = 4
    STEPS = BLOCK // BANK_T
    with ExitStack() as ctx:
        S = Space(nc, ctx, "e")
        E = EarlyTiles(nc, io, T, S, EARLY_S, EARLY_R * PEER_H, EARLY_S * NBLOCK)
        iota = S.sb("iota", [P, P], F16)
        left = [S.sb(f"left{r}", [P, BANK_T, P], F16) for r in range(RING)]
        right = [S.sb(f"right{r}", [P, 2, BANK_T, P], F16) for r in range(RING)]
        w_hi16 = S.sb("w_hi16", [P, SEQ], F16)
        w_hi = S.sb("w_hi", [P, SEQ])
        stage = [S.sb(f"stage{b}", [P, NKEYS, TB]) for b in range(2)]
        tab = [S.ps(f"tab{r}", [P, BANK_T, P]) for r in range(RING)]
        vec_step = S.sem("vec_step")
        built = S.sem("built")
        spread = S.sem("spread")
        out = S.sem("out")
        stored = [S.sem(f"stored{b}") for b in range(2)]
        block = ctx.enter_context(nc.Block())
        key1_t, key2_t, w_lo = T.picked_t
        HALVES = {(r * STEPS + 1) // (2 * EARLY_S): (r // 2, r % 2) for r in range(2 * EARLY_S)}

        @block.vector
        def _(dve):
            c = Chain(dve, vec_step)
            c.link(nc.vector.tensor_scalar(w_lo, w_lo, S_G, None, ALU.mult))
            c.step(nc.vector.tensor_copy(iota[:], T.iota[:]))
            c.link(nc.vector.tensor_copy(w_hi16[:], w_lo))
            c.link(nc.vector.tensor_copy(w_hi[:], w_hi16[:]))
            c.link(nc.vector.tensor_tensor(w_lo, w_lo, w_hi[:], ALU.subtract))
            with dve.Fori(0, NBLOCK) as blk:
                for s in range(STEPS):
                    r = s % RING
                    dve.wait_ge(spread, BASE - RING + 1 + blk * STEPS + s)
                    nc.vector.tensor_tensor(left[r][:], lanes(T.iota[:], 1, P, BANK_T, P),
                                            lanes(key2_t[:, bass.ds(blk * BLOCK + s * BANK_T, BANK_T)], 2, P, BANK_T, P),
                                            ALU.is_equal)
                    for j in range(BANK_T):
                        tok = bass.ds(blk * BLOCK + (s * BANK_T + j), 1)
                        nc.vector.tensor_scalar(right[r][:, 0, j, :], iota[:], key1_t[:, tok], w_hi[:, tok],
                                                ALU.is_equal, ALU.mult)
                        last = nc.vector.tensor_scalar(right[r][:, 1, j, :], iota[:], key1_t[:, tok], w_lo[:, tok],
                                                       ALU.is_equal, ALU.mult)
                    last.then_inc(built, 1)

        @block.tensor
        def _(pe):
            E.prime_tensor(pe)
            pe.sem_inc(spread, BASE)

            def step(blk, last):
                for s in range(STEPS):
                    n, r = blk * STEPS + s, s % RING
                    pe.wait_ge(built, n + 1)
                    pe.wait_ge(out, BASE - RING + 1 + n)
                    for j in range(BANK_T):
                        for part in range(2):
                            mm = pe.matmul(tab[r][:, j, :], left[r][:, j, :], right[r][:, part, j, :],
                                           start=part == 0, stop=part == 1)
                    mm.then_inc(spread, 1)
                    if s in HALVES:
                        b, half = HALVES[s]
                        if half == 0 and b + 1 < EARLY_S:
                            E.turn(pe, blk, b + 1)
                        elif half == 0 and not last:
                            E.turn(pe, blk + 1, 0)
                        E.hidden(pe, blk, b, half)

            E.turn(pe, 0, 0)
            with pe.Fori(0, NBLOCK - 1) as blk:
                step(blk, False)
            step(NBLOCK - 1, True)

        @block.scalar
        def _(act):
            E.prime_scalar(act)
            act.sem_inc(out, BASE)
            for b in range(2):
                act.sem_inc(stored[b], BASE)

            def step(blk, last):
                for s in range(STEPS):
                    n, r = blk * STEPS + s, s % RING
                    slot, at = s // (STEPS // 2), s % (STEPS // 2) * BANK_T
                    if at == 0:
                        act.wait_ge(stored[slot], BASE + blk * 16)
                    act.wait_ge(spread, BASE + 1 + n)
                    nc.scalar.activation(stage[slot][:, :, at:at + BANK_T],
                                         tab[r][:].rearrange("p t i -> p i t"), ACT.Copy).then_inc(out, 1)
                    if s in HALVES:
                        b, half = HALVES[s]
                        if half == 0 and b + 1 < EARLY_S:
                            E.split(act, blk, b + 1)
                        elif half == 0 and not last:
                            E.split(act, blk + 1, 0)
                        E.gelu(act, blk, b, half)

            E.split(act, 0, 0)
            with act.Fori(0, NBLOCK - 1) as blk:
                step(blk, False)
            step(NBLOCK - 1, True)

        @block.gpsimd
        def _(pool):
            E.prime_gpsimd(pool)
            with pool.Fori(0, NBLOCK) as blk:
                for b in range(EARLY_S):
                    E.low(pool, blk, b)

        @block.sync
        def _(sp):
            def step(blk, last):
                for b in range(EARLY_S):
                    E.keep(sp, blk, b)
                    if not last:
                        E.load(sp, blk + 1, b)
                    if b >= 1:
                        sp.wait_ge(out, BASE + blk * STEPS + b * (STEPS // 2))
                        sp.dma_start(T.dense.rearrange("(c b) j r -> c b j r", b=2)[blk, b - 1],
                                     stage[b - 1][:].rearrange("p i t -> p (i t)")).then_inc(stored[b - 1], 16)

            for b in range(EARLY_S):
                E.load(sp, 0, b, again=False)
            with sp.Fori(0, NBLOCK - 1) as blk:
                step(blk, False)
            step(NBLOCK - 1, True)
            for slot in range(2):
                sp.wait_ge(stored[slot], BASE + 16 * NBLOCK)
            E.all_kept(sp, EARLY_S * NBLOCK)


S_A = 64.0
GROUP = 4
NE = NKEYS


def experts(nc, io, T):
    LOOP = 2 * GROUP
    LATE = (NE - N_EARLY) // LOOP
    TURNS = NE // LOOP
    with ExitStack() as ctx:
        S = Space(nc, ctx, "f")
        u_in = [S.sb(f"u_in{b}", [P, D]) for b in range(2)]
        v_in = [S.sb(f"v_in{b}", [P, D]) for b in range(2)]
        g_in = [S.sb(f"g_in{b}", [P, NTB, GROUP * TB]) for b in range(2)]
        u_hi = [S.sb(f"u_hi{b}", [P, KT, P], F16) for b in range(2)]
        u_lo = [S.sb(f"u_lo{b}", [P, KT, P], F16) for b in range(2)]
        gel = [S.sb(f"gel{b}", [P, SEQ]) for b in range(2)]
        a = [S.sb(f"a{b}", [P, SEQ]) for b in range(2)]
        a_hi = [[S.sb(f"a_hi{g}{j}", [P, SEQ], F16) for j in range(GROUP)] for g in range(2)]
        a_lo = [[S.sb(f"a_lo{g}{j}", [P, SEQ], F16) for j in range(GROUP)] for g in range(2)]
        v_hi = [[S.sb(f"v_hi{g}{j}", [P, D], F16) for j in range(GROUP)] for g in range(2)]
        v_lo = [[S.sb(f"v_lo{g}{j}", [P, D], F16) for j in range(GROUP)] for g in range(2)]
        u_ps = S.ps("u_ps", [P, KT, P])
        hid = [S.ps(f"hid{b}", [P, SEQ]) for b in range(2)]
        y = [S.ps(f"y{b}", [P, HALF]) for b in range(2)]

        v_loaded = [S.sem(f"v_loaded{b}") for b in range(2)]
        g_loaded = [S.sem(f"g_loaded{b}") for b in range(2)]
        u_loaded = [S.sem(f"u_loaded{b}") for b in range(2)]
        gel_loaded = [S.sem(f"gel_loaded{b}") for b in range(2)]
        u_turned = S.sem("u_turned")
        u_hi_done = S.sem("u_hi_done")
        u_lo_done = S.sem("u_lo_done")
        hid_done = S.sem("hid_done")
        gelu_done = S.sem("gelu_done")
        stored = S.sem("stored")
        y_done = S.sem("y_done")
        v_hi_done = S.sem("v_hi_done")
        a_hi_done = S.sem("a_hi_done")
        a_done = S.sem("a_done")
        a_lo_done = S.sem("a_lo_done")
        y_added = S.sem("y_added")
        v_lo_done = S.sem("v_lo_done")
        block = ctx.enter_context(nc.Block())

        YB = NT * (D // HALF)
        YS = YB // GROUP
        y_place = [(k // 2, k % 2) for k in range(YB)]

        @block.sync
        def _(sp):
            u_v = io.peer_u[0, N_EARLY * P:NE * P, :].rearrange("(c m p) d -> c m p d", m=LOOP, p=P)
            kept_v = T.kept.rearrange("(c m p) t -> c m p t", m=LOOP, p=P)
            out_v = io.out[0].rearrange("(t p) d -> p t d", p=P)

            def step(c, view, early):
                first, count = (0, N_EARLY) if early else (N_EARLY, NE - N_EARLY)
                v_v = io.peer_v[0, first * P:(first + count) * P, :].rearrange("(c m p) d -> c m p d", m=LOOP, p=P)
                g_v = T.dense[:, :, first * TB:(first + count) * TB].rearrange("b j (c g r) -> c g j b r", g=2,
                                                                              r=GROUP * TB)
                for m in range(LOOP):
                    n = c * LOOP + m
                    if m % GROUP == 0:
                        g = m // GROUP
                        sp.wait_ge(a_done, BASE + n - GROUP)
                        sp.dma_start(g_in[g][:], g_v[view, g]).then_inc(g_loaded[g], 16)
                    if early:
                        sp.wait_ge(a_done, BASE + n - 1)
                        sp.dma_start(gel[m % 2][:], kept_v[view, m]).then_inc(gel_loaded[m % 2], 16)
                    else:
                        sp.wait_ge(u_turned, BASE + n - 1)
                        sp.dma_start(u_in[m % 2][:], u_v[view, m]).then_inc(u_loaded[m % 2], 16)
                    sp.wait_ge(v_lo_done, BASE + n - 1)
                    sp.dma_start(v_in[m % 2][:], v_v[view, m]).then_inc(v_loaded[m % 2], 16)

            with sp.Fori(0, LATE) as c:
                step(c, c, False)
            with sp.Fori(0, TURNS - LATE) as e:
                step(e + LATE, e, True)
            for t in range(NT):
                sp.wait_ge(y_added, BASE + YB * (NE // GROUP - 1) + 2 * t + 2)
                sp.dma_start(out_v[:, t, :], T.h[:, t, :]).then_inc(stored, 16)
            sp.wait_ge(stored, 16 * NT)

        @block.tensor
        def _(pe):
            pe.sem_inc(u_turned, BASE)
            pe.sem_inc(hid_done, BASE)
            pe.sem_inc(y_done, BASE)

            def turn(n, m):
                pe.wait_ge(u_loaded[m % 2], n * 8 + (16 - 8 * (m % 2)))
                pe.wait_ge(u_lo_done, BASE + n)
                for k in range(KT):
                    last = pe.transpose(u_ps[:, k, :], u_in[m % 2][:, k * P:(k + 1) * P], T.ident[:])
                last.then_inc(u_turned, 1)

            def hidden(n, m):
                pe.wait_ge(u_lo_done, BASE + n + 1)
                pe.wait_ge(gelu_done, BASE + n - 1)
                for half in range(2):
                    toks = slice(half * HALF, (half + 1) * HALF)
                    for k in range(KT):
                        last = split_mm(pe, hid[m % 2][:, toks], u_hi[m % 2][:, k, :], u_lo[m % 2][:, k, :],
                                        T.act_hi[:, k, toks], T.act_lo[:, k, toks], k == 0, k == KT - 1)
                last.then_inc(hid_done, 1)

            def outputs(group_n, g, part):
                if part == 0:
                    pe.wait_ge(a_lo_done, BASE + GROUP * (group_n + 1))
                    pe.wait_ge(v_lo_done, BASE + GROUP * (group_n + 1))
                for k in range(part * YS, (part + 1) * YS):
                    t, half = y_place[k]
                    pe.wait_ge(y_added, BASE + YB * group_n + k - 1)
                    for j in range(GROUP):
                        toks, cols = slice(t * P, (t + 1) * P), slice(half * HALF, (half + 1) * HALF)
                        last = split_mm(pe, y[k % 2][:], a_hi[g][j][:, toks], a_lo[g][j][:, toks],
                                        v_hi[g][j][:, cols], v_lo[g][j][:, cols], j == 0, j == GROUP - 1)
                    last.then_inc(y_done, 1)

            def step(c, m, y_too=True, u_too=True, early=False):
                n = c * LOOP + m
                if u_too and not early:
                    turn(n + 1, m + 1)
                if not early:
                    hidden(n, m)
                if y_too:
                    outputs(2 * c + m // GROUP - 1, (m // GROUP + 1) % 2, m % GROUP)

            turn(0, 0)
            for m in range(LOOP):
                step(0, m, y_too=m >= GROUP)
            with pe.Fori(1, LATE - 1) as c:
                for m in range(LOOP):
                    step(c, m)
            for m in range(LOOP):
                step(LATE - 1, m, u_too=m < LOOP - 1)
            with pe.Fori(LATE, TURNS) as c:
                for m in range(LOOP):
                    step(c, m, early=True)
            for part in range(GROUP):
                outputs(NE // GROUP - 1, 1, part)

        @block.scalar
        def _(act):
            act.sem_inc(gelu_done, BASE)
            act.sem_inc(u_hi_done, BASE)
            act.sem_inc(v_hi_done, BASE)
            act.sem_inc(a_hi_done, BASE)

            def hi_u(n, m):
                act.wait_ge(u_turned, BASE + n + 1)
                act.wait_ge(hid_done, BASE + n - 1)
                nc.scalar.activation(u_hi[m % 2][:], u_ps[:], ACT.Copy, scale=S_U).then_inc(u_hi_done, 1)

            def step(c, m, u_too=True, early=False):
                n = c * LOOP + m
                g, j = m // GROUP, m % GROUP
                if u_too and not early:
                    hi_u(n + 1, m + 1)
                if j == 0:
                    act.wait_ge(y_done, BASE + YB * (2 * c + g - 1))
                act.wait_ge(v_loaded[m % 2], n * 8 + (16 - 8 * (m % 2)))
                nc.scalar.activation(v_hi[g][j][:], v_in[m % 2][:], ACT.Copy).then_inc(v_hi_done, 1)
                if not early:
                    act.wait_ge(hid_done, BASE + n + 1)
                    act.wait_ge(a_done, BASE + n - 1)
                    nc.scalar.activation(gel[m % 2][:], hid[m % 2][:], ACT.Gelu,
                                         scale=1.0 / (S_U * S_ACT)).then_inc(gelu_done, 1)
                act.wait_ge(a_done, BASE + n + 1)
                nc.scalar.activation(a_hi[g][j][:], a[m % 2][:], ACT.Copy).then_inc(a_hi_done, 1)

            hi_u(0, 0)
            with act.Fori(0, LATE - 1) as c:
                for m in range(LOOP):
                    step(c, m)
            for m in range(LOOP):
                step(LATE - 1, m, u_too=m < LOOP - 1)
            with act.Fori(LATE, TURNS) as c:
                for m in range(LOOP):
                    step(c, m, early=True)

        @block.gpsimd
        def _(pool):
            pool.sem_inc(v_lo_done, BASE)
            with pool.Fori(0, TURNS) as c:
                for m in range(LOOP):
                    n = c * LOOP + m
                    g, j = m // GROUP, m % GROUP
                    pool.wait_ge(v_hi_done, BASE + n + 1)
                    nc.gpsimd.tensor_tensor(v_lo[g][j][:], v_in[m % 2][:], v_hi[g][j][:],
                                            ALU.subtract).then_inc(v_lo_done, 1)

        @block.vector
        def _(dve):
            dve.sem_inc(u_lo_done, BASE)
            dve.sem_inc(a_done, BASE)
            dve.sem_inc(a_lo_done, BASE)
            dve.sem_inc(y_added, BASE)

            def lo_u(n, m):
                dve.wait_ge(u_hi_done, BASE + n + 1)
                nc.vector.scalar_tensor_tensor(u_lo[m % 2][:], u_ps[:], S_U, u_hi[m % 2][:], ALU.mult,
                                               ALU.subtract).then_inc(u_lo_done, 1)

            def add_y(group_n, k):
                t, half = y_place[k]
                cols = slice(half * HALF, (half + 1) * HALF)
                dve.wait_ge(y_done, BASE + YB * group_n + k + 1)
                dve.wait_ge(y_added, BASE + YB * (group_n - 1) + k + 1)
                nc.vector.scalar_tensor_tensor(T.h[:, t, cols], y[k % 2][:], 1.0 / S_A, T.h[:, t, cols], ALU.mult,
                                               ALU.add).then_inc(y_added, 1)

            def step(c, m, y_too=True, u_too=True, early=False):
                n = c * LOOP + m
                g, j = m // GROUP, m % GROUP
                if u_too and not early:
                    lo_u(n + 1, m + 1)
                if j == 0:
                    dve.wait_ge(g_loaded[g], c * 16 + 16)
                if early:
                    at = n - LATE * LOOP
                    dve.wait_ge(gel_loaded[m % 2], at * 8 + (16 - 8 * (m % 2)))
                    dve.wait_ge(a_hi_done, BASE + n - 1)
                else:
                    dve.wait_ge(gelu_done, BASE + n + 1)
                dve.wait_ge(a_lo_done, BASE + n - 1)
                nc.vector.scalar_tensor_tensor(
                    a[m % 2][:].rearrange("p (b t) -> p b t", t=TB), gel[m % 2][:].rearrange("p (b t) -> p b t", t=TB),
                    S_A / S_G, g_in[g][:].rearrange("p b (i t) -> p b i t", t=TB)[:, :, j, :], ALU.mult,
                    ALU.mult).then_inc(a_done, 1)
                if y_too:
                    add_y(2 * c + g - 1, j * YS)
                dve.wait_ge(a_hi_done, BASE + n + 1)
                nc.vector.tensor_tensor(a_lo[g][j][:], a[m % 2][:], a_hi[g][j][:], ALU.subtract).then_inc(a_lo_done, 1)
                if y_too:
                    for k in range(j * YS + 1, (j + 1) * YS):
                        add_y(2 * c + g - 1, k)

            lo_u(0, 0)
            for m in range(LOOP):
                step(0, m, y_too=m >= GROUP)
            with dve.Fori(1, LATE - 1) as c:
                for m in range(LOOP):
                    step(c, m)
            for m in range(LOOP):
                step(LATE - 1, m, u_too=m < LOOP - 1)
            with dve.Fori(LATE, TURNS) as c:
                for m in range(LOOP):
                    step(c, m, early=True)
            for k in range(YB):
                add_y(NE // GROUP - 1, k)


def allocate_constants(S):
    T = Names()
    T.ident = S.sb("ident", [P, P])
    T.causal = S.sb("causal", [P, P])
    T.tri = S.sb("tri", [P, P])
    T.iota = S.sb("iota", [P, P])
    T.iota_i = S.sb("iota_i", [P, P], I32)
    T.mhalf = S.sb("mhalf", [P, 8])
    T.eps = S.sb("eps", [P, 8])
    T.g_mix = S.sb("g_mix", [P, KT])
    T.g_ffn = S.sb("g_ffn", [P, KT])
    T.g_sub = S.sb("g_sub", [P, 1])
    T.b_gate = S.sb("b_gate", [P, 2])
    T.g_gla = S.sb("g_gla", [P, GLA_DV])
    T.g_q = S.sb("g_q", [P, DIFF_DK])
    T.g_k = S.sb("g_k", [P, DIFF_DK])
    T.w_gate = S.sb("w_gate", [GLA_RANK, GLA_H * GLA_DK])
    T.sin = S.sb("sin", [P, NT, HROPE])
    T.cos = S.sb("cos", [P, NT, HROPE])
    T.neg_lam = S.sb("neg_lam", [P, 1])
    T.act_hi = S.sb("act_hi", [P, KT, SEQ], F16)
    T.act_lo = S.sb("act_lo", [P, KT, SEQ], F16)
    return T


def allocate_diff(S, T):
    T.dq = S.sb("dq", [P, NT, HALF])
    T.dk = S.sb("dk", [P, NT, HALF])
    T.dv = S.sb("dv", [P, NT, HALF])


def allocate_gla(S, T):
    T.gqk = S.sb("gqk", [P, 4, SEQ])
    T.cum = S.sb("cum", [P, 2, SEQ])
    T.gv = S.sb("gv", [P, NT, HALF])
    T.gr = S.sb("gr", [P, NT, HALF])


def stage(nc, program, io, T):
    with nc.cleanup_on_exit():
        program(nc, io, T)


def hybrid_block(nc, io):
    dense = nc.dram_tensor("dense_weights", [NTB, NKEYS, NKEYS * TB], F32, kind="Internal").ap()
    kept = nc.dram_tensor("early_tiles", [N_EARLY * NKEYS, SEQ], F32, kind="Internal").ap()
    with ExitStack() as whole:
        T = allocate_constants(Space(nc, whole, "p"))
        T.dense, T.kept = dense, kept
        with ExitStack() as diff:
            allocate_diff(Space(nc, diff, "p"), T)
            with ExitStack() as gla:
                S = Space(nc, gla, "p")
                allocate_gla(S, T)
                stage(nc, project_in, io, T)
                T.state = S.sb("state", [P, NCH, 2, GLA_DV])
                stage(nc, gla_states, io, T)
                stage(nc, gla_outputs, io, T)
            stage(nc, diff_attention, io, T)
        T.h = Space(nc, whole, "p").sb("h", [P, NT, D])
        stage(nc, project_out, io, T)
        with ExitStack() as picks:
            S = Space(nc, picks, "p")
            T.picked_all = S.sb("picked_all", [P, 3 * SEQ])
            T.picked_t = [T.picked_all[:, n * SEQ:(n + 1) * SEQ] for n in range(3)]
            stage(nc, retrieve, io, T)
            stage(nc, spread_weights, io, T)
        stage(nc, experts, io, T)


_INS = ["x", "positions", "g_mix", "w_in", "w_gla_gate", "b_gla_gate", "g_gla_out", "g_q", "g_k", "lambda_q1",
        "lambda_k1", "lambda_q2", "lambda_k2", "g_diff_sub", "w_out", "g_ffn", "w_peer_q", "peer_sub_keys", "peer_u",
        "peer_v"]


def kernel(**inputs):
    import numpy as _np
    import concourse.bacc as _bacc
    from concourse import mybir as _mybir
    from concourse.bass_utils import run_bass_kernel_spmd as _run

    nc = _bacc.Bacc("TRN2", target_bir_lowering=False, num_devices=1)
    arrays, io = {}, Names()
    for name in _INS:
        a = _np.ascontiguousarray(inputs[name])
        arrays[f"in_{name}"] = a
        io.__dict__[name] = nc.dram_tensor(f"in_{name}", a.shape, _mybir.dt.from_np(a.dtype),
                                           kind="ExternalInput").ap()
    io.out = nc.dram_tensor("out", (1, SEQ, D), F32, kind="ExternalOutput").ap()
    hybrid_block(nc, io)
    r = _run(nc, [arrays], core_ids=[0])
    return r.results[0]["out"]
```

```python
from contextlib import ExitStack

import numpy as np
import concourse.bass as bass
from concourse import mybir

F32 = mybir.dt.float32
F16 = mybir.dt.float16
BF16 = mybir.dt.bfloat16
I32 = mybir.dt.int32
U32 = mybir.dt.uint32
ALU = mybir.AluOpType
ACT = mybir.ActivationFunctionType
AX = mybir.AxisListType

P = 128
SEQ = 1024
D = 1024
KT = D // P
NT = SEQ // P
HALF = 512

GLA_H, GLA_DK, GLA_DV, GLA_RANK, GLA_TAU, CHUNK = 4, 64, 128, 16, 16.0, 64
DIFF_H, DIFF_DK, DIFF_DV = 4, 64, 128
ROPE = DIFF_DK // 4
HROPE = ROPE // 2
ROPE_THETA = 500000.0
LAMBDA_INIT = 0.8 - 0.6 * float(np.exp(-0.3 * 0))
EPS = 1e-6

PEER_H, NKEYS, QDIM, TOPK = 8, 128, 256, 16
PICKS = PEER_H * TOPK

S_ACT = 16.0
S_W = 64.0
UNSCALE = 1.0 / (S_ACT * S_W)
BASE = 64


class Names:
    pass


class Chain:

    def __init__(self, eng, sem, at=0):
        self.eng, self.sem, self.at, self.n = eng, sem, at, 0

    def step(self, ins):
        self.n += 1
        ins.then_inc(self.sem, 1)

    def wait(self):
        self.eng.wait_ge(self.sem, self.at + self.n)

    def link(self, ins):
        self.step(ins)
        self.wait()


class Space:

    def __init__(self, nc, ctx, tag):
        self.nc, self.ctx, self.tag = nc, ctx, tag

    def sb(self, name, shape, dt=F32, side=None):
        return self.ctx.enter_context(self.nc.sbuf_tensor(f"{self.tag}_{name}", shape, dt, side=side))

    def ps(self, name, shape, dt=F32):
        return self.ctx.enter_context(self.nc.psum_tensor(f"{self.tag}_{name}", shape, dt))

    def sem(self, name):
        return self.nc.alloc_semaphore(f"{self.tag}_{name}")


def lanes(ap, *shape):
    axis = shape[0]
    return ap.unsqueeze(axis).broadcast_to(list(shape[1:]))


class Constants:

    def __init__(self, nc, io, T, S):
        self.nc, self.io, self.T = nc, io, T
        self.pos = S.sb("pos", [P, NT], I32)
        self.posf = S.sb("posf", [P, NT])
        self.freq = S.sb("freq", [P, HROPE])
        self.ang = S.sb("ang", [P, NT, HROPE])
        self.turns_i = S.sb("turns_i", [P, NT * HROPE], I32)
        self.turns = S.sb("turns", [P, NT * HROPE])
        self.wrap = S.sb("wrap", [P, NT * HROPE])
        self.lamv = S.sb("lamv", [P, 4, DIFF_DK])
        self.lamp = S.sb("lamp", [P, DIFF_DK])
        self.lams = S.sb("lams", [P, 2])
        self.lame = S.sb("lame", [P, 2])
        self.gain_loaded = S.sem("gain_loaded")
        self.gain_ready = S.sem("gain_ready")
        self.loaded = S.sem("loaded")
        self.masks_ready = S.sem("masks_ready")
        self.pool_step = S.sem("const_pool_step")
        self.vec_step = S.sem("const_vec_step")
        self.act_step = S.sem("const_act_step")
        self.gates = S.sem("gates")

    def load_gain(self, sp):
        nc, io, T = self.nc, self.io, self.T
        with nc.allow_non_contiguous_dma("a column of small weights"):
            sp.dma_start(T.g_mix[:], io.g_mix.rearrange("l (k p) -> p (l k)", p=P)).then_inc(
                self.gain_loaded, 16)

    def load(self, sp):
        nc, io, T = self.nc, self.io, self.T
        with nc.allow_non_contiguous_dma("columns of small weights"):
            sp.dma_start(self.pos[:], io.positions.rearrange("b (t p) -> p (b t)", p=P)).then_inc(self.loaded, 16)
            sp.dma_start(T.g_sub[:], io.g_diff_sub.rearrange("l p -> p l")).then_inc(self.loaded, 16)
            sp.dma_start(T.b_gate[:], io.b_gla_gate.rearrange("l (c p) -> p (l c)", p=P)).then_inc(self.loaded, 16)
        sp.dma_start(T.g_gla[:], io.g_gla_out[0, :].partition_broadcast(P)).then_inc(self.loaded, 16)
        sp.dma_start(T.g_q[:], io.g_q[0, :].partition_broadcast(P)).then_inc(self.loaded, 16)
        sp.dma_start(T.g_k[:], io.g_k[0, :].partition_broadcast(P)).then_inc(self.loaded, 16)
        sp.dma_start(T.w_gate[:], io.w_gla_gate[0]).then_inc(self.loaded, 16)
        for n, v in enumerate((io.lambda_q1, io.lambda_k1, io.lambda_q2, io.lambda_k2)):
            sp.dma_start(self.lamv[:, n, :], v[0, :].partition_broadcast(P)).then_inc(self.loaded, 16)

    def masks(self, pool):
        nc, T = self.nc, self.T
        c = Chain(pool, self.pool_step)
        c.step(nc.gpsimd.memset(T.ident[:], 0.0))
        c.step(nc.gpsimd.memset(T.causal[:], 0.0))
        c.step(nc.gpsimd.memset(T.tri[:], 1.0))
        c.step(nc.gpsimd.memset(T.mhalf[:], -0.5))
        c.step(nc.gpsimd.memset(T.eps[:], EPS))
        c.step(nc.gpsimd.iota(T.iota_i[:], [[1, P]], base=0, channel_multiplier=0))
        c.wait()
        c.step(nc.gpsimd.affine_select(out=T.ident[:], in_=T.ident[:], compare_op=ALU.not_equal, fill=1.0,
                                       base=0, pattern=[[-1, P]], channel_multiplier=1))
        c.step(nc.gpsimd.affine_select(out=T.causal[:], in_=T.causal[:], compare_op=ALU.is_ge, fill=-1e30,
                                       base=0, pattern=[[-1, P]], channel_multiplier=1))
        c.step(nc.gpsimd.affine_select(out=T.tri[:], in_=T.tri[:], compare_op=ALU.is_ge, fill=0.0,
                                       base=0, pattern=[[1, P]], channel_multiplier=-1))
        c.step(nc.gpsimd.tensor_copy(T.iota[:], T.iota_i[:]))
        c.wait()
        nc.gpsimd.memset(T.tri[0:CHUNK, CHUNK:P], 0.0).then_inc(self.masks_ready, 1)

    def gain(self, dve):
        nc, T = self.nc, self.T
        dve.wait_ge(self.gain_loaded, 16)
        nc.vector.tensor_scalar(T.g_mix[:], T.g_mix[:], S_W, None, ALU.mult).then_inc(self.gain_ready, 1)

    def tables(self, dve):
        nc, T = self.nc, self.T
        c = Chain(dve, self.vec_step)
        for j in range(HROPE):
            c.step(nc.vector.memset(self.freq[:, j:j + 1], float(np.float32(ROPE_THETA) ** np.float32(-2.0 * j / ROPE))))
        dve.wait_ge(self.loaded, 16 * 11)
        c.link(nc.vector.tensor_copy(self.posf[:], self.pos[:]))
        c.link(nc.vector.tensor_tensor(self.ang[:], lanes(self.posf[:], 2, P, NT, HROPE), lanes(self.freq[:], 1, P, NT, HROPE),
                                       ALU.mult))
        flat = self.ang[:].rearrange("p t j -> p (t j)")
        c.link(nc.vector.tensor_scalar(self.turns[:], flat, 1.0 / (2 * np.pi), None, ALU.mult))
        c.link(nc.vector.tensor_copy(self.turns_i[:], self.turns[:]))
        c.link(nc.vector.tensor_copy(self.turns[:], self.turns_i[:]))
        c1 = 6.28125
        c2 = float(np.floor((2 * np.pi - c1) * 2 ** 22) / 2 ** 22)
        c3 = float(2 * np.pi - c1 - c2)
        for part in (c1, c2, c3):
            c.link(nc.vector.scalar_tensor_tensor(flat, self.turns[:], -part, flat, ALU.mult, ALU.add))
        lim = 3.1415925
        c.link(nc.vector.tensor_scalar(T.sin[:].rearrange("p t j -> p (t j)"), flat, lim, -lim, ALU.min, ALU.max))
        c.link(nc.vector.tensor_scalar(self.wrap[:], flat, float(np.pi / 2), -2 * float(np.pi), ALU.is_gt, ALU.mult))
        c.link(nc.vector.scalar_tensor_tensor(flat, flat, float(np.pi / 2), self.wrap[:], ALU.add, ALU.add))
        c.link(nc.vector.tensor_scalar(T.cos[:].rearrange("p t j -> p (t j)"), flat, lim, -lim, ALU.min, ALU.max))
        for n in range(2):
            c.link(nc.vector.tensor_tensor(self.lamp[:], self.lamv[:, 2 * n, :], self.lamv[:, 2 * n + 1, :], ALU.mult))
            c.link(nc.vector.tensor_reduce(self.lams[:, n:n + 1], self.lamp[:], AX.X, ALU.add))
        nc.vector.tensor_scalar(T.g_sub[:], T.g_sub[:], S_ACT * (1.0 - LAMBDA_INIT), None,
                                ALU.mult).then_inc(self.gates, 1)

    def sines(self, act):
        nc, T = self.nc, self.T
        act.wait_ge(self.vec_step, HROPE + 16)
        nc.scalar.activation(self.lame[:], self.lams[:], ACT.Exp).then_inc(self.act_step, 1)
        nc.scalar.activation(T.sin[:], T.sin[:], ACT.Sin).then_inc(self.act_step, 1)
        nc.scalar.activation(T.cos[:], T.cos[:], ACT.Sin).then_inc(self.act_step, 1)

    def finish(self, dve):
        nc, T = self.nc, self.T
        c = Chain(dve, self.vec_step, HROPE + 16)
        dve.wait_ge(self.act_step, 3)
        c.link(nc.vector.scalar_tensor_tensor(T.neg_lam[:], self.lame[:, 1:2], -LAMBDA_INIT, self.lame[:, 0:1],
                                              ALU.add, ALU.subtract))


def split_mm(pe, out, a_hi, a_lo, b_hi, b_lo, first, last):
    pe.matmul(out, a_hi, b_hi, start=first, stop=False)
    pe.matmul(out, a_hi, b_lo, start=False, stop=False)
    return pe.matmul(out, a_lo, b_hi, start=False, stop=last)


COLS = [("qk", 0, 512), ("ga", 1024, GLA_RANK), ("gv", 512, 512), ("gr", 1040, 512), ("dq", 1552, 512),
        ("dk", 2064, 512), ("dv", 2576, 512)]
GA_T = SEQ // 4


XR = 4


def project_in(nc, io, T):
    with ExitStack() as ctx:
        S = Space(nc, ctx, "a")
        const = Constants(nc, io, T, S)
        x_in = S.sb("x_in", [P, XR, D])
        junk = S.sb("junk", [P, D], F16)
        ss = S.sb("ss", [P, NT])
        rstd = S.sb("rstd", [P, NT])
        w_in = S.sb("w_in", [P, 2, 2, HALF])
        w_hi = S.sb("w_hi", [P, 2, KT, HALF], F16)
        w_lo = S.sb("w_lo", [P, 2, KT, HALF], F16)
        sq = S.sb("sq", [P, 2, HALF])
        hss = S.sb("hss", [P, 2, 8])
        hr = S.sb("hr", [P, 2, 8])
        turned = [S.ps(f"turned{b}", [P, KT, P]) for b in range(2)]
        acc = [S.ps(f"acc{b}", [P, HALF]) for b in range(4)]

        x_loaded = [S.sem(f"x_loaded{b}") for b in range(XR)]
        w_loaded = [S.sem(f"w_loaded{b}") for b in range(2)]
        squared = S.sem("squared")
        rstd_done = S.sem("rstd_done")
        pool_step = S.sem("pool_step")
        normed = S.sem("normed")
        x_turned = S.sem("x_turned")
        hi_done = S.sem("hi_done")
        lo_done = S.sem("lo_done")
        w_hi_done = S.sem("w_hi_done")
        w_lo_done = S.sem("w_lo_done")
        acc_full = S.sem("acc_full")
        acc_free = S.sem("acc_free")
        head_sq = S.sem("head_sq")
        head_ss = S.sem("head_ss")
        head_r = S.sem("head_r")
        head_normed = S.sem("head_normed")
        rot_step = S.sem("rot_step")
        keep_done = S.sem("keep_done")
        ga_out = S.sem("ga_out")
        gate_done = S.sem("gate_done")
        z_done = S.sem("z_done")
        soft_step = S.sem("soft_step")
        soft_done = S.sem("soft_done")
        gate_step = S.sem("gate_step")
        cum_done = S.sem("cum_done")
        block = ctx.enter_context(nc.Block())

        PIECES = KT // 2
        gains = {"dq": T.g_q, "dk": T.g_k}
        dest = {"gv": T.gv, "gr": T.gr, "dq": T.dq, "dk": T.dk, "dv": T.dv}
        first_result = [0]
        for name, _, _ in COLS:
            first_result.append(first_result[-1] + (4 if name == "ga" else 8))
        keep = sq[:].rearrange("p a b -> p (a b)")
        z, soft = x_in[:, 0:2], x_in[:, 2:4]
        ga = x_in[0:GLA_RANK, 3]
        gate = [x[:].rearrange("p k t -> p (k t)") for x in turned]

        @block.sync
        def _(sp):
            def load_w(c, q):
                _, c0, n = COLS[c]
                r = c * PIECES + q
                if r >= 2:
                    sp.wait_ge(w_lo_done, r - 1)
                src = io.w_in[0, 2 * q * P:(2 * q + 2) * P, c0:c0 + n].rearrange("(k p) n -> p k n", p=P)
                sp.dma_start(w_in[:, r % 2, :, 0:n], src).then_inc(w_loaded[r % 2], 16)

            def load_x(t):
                if t >= XR:
                    sp.wait_ge(x_turned, t - XR + 1)
                sp.dma_start(x_in[:, t % XR, :], io.x[0, t * P:(t + 1) * P, :]).then_inc(x_loaded[t % XR], 16)

            load_x(0)
            const.load_gain(sp)
            load_x(1)
            for q in range(PIECES):
                load_x(q + 2)
                load_w(0, q)
            const.load(sp)
            for t in range(PIECES + 2, NT):
                load_x(t)
            for c in range(1, len(COLS)):
                for q in range(PIECES):
                    load_w(c, q)

        @block.gpsimd
        def _(pool):
            const.masks(pool)
            nc.gpsimd.memset(keep, 1.0).then_inc(keep_done, 1)
            pool.wait_ge(keep_done, 1)
            nc.gpsimd.memset(keep.rearrange("p (c s) -> p c s", s=CHUNK)[:, :, 0:1], 0.0).then_inc(keep_done, 1)
            c = Chain(pool, pool_step)
            for t in range(NT):
                pool.wait_ge(squared, t + 1)
                c.link(nc.gpsimd.tensor_scalar(rstd[:, t:t + 1], ss[:, t:t + 1], 1.0 / D, EPS, ALU.mult, ALU.add))
                nc.gpsimd.tensor_tensor(rstd[:, t:t + 1], rstd[:, t:t + 1], T.mhalf[:, 0:1],
                                        ALU.pow).then_inc(rstd_done, 1)
            base = c.n
            with pool.Fori(0, NT) as i:
                c = Chain(pool, pool_step, base + 2 * i)
                for b in range(2):
                    pool.wait_ge(head_ss, 2 * i + b + 1)
                    c.link(nc.gpsimd.tensor_tensor(hr[:, b, :], hss[:, b, :], T.eps[:, 0:8], ALU.add))
                    nc.gpsimd.tensor_tensor(hr[:, b, :], hr[:, b, :], T.mhalf[:, 0:8], ALU.pow).then_inc(head_r, 1)

        @block.scalar
        def _(act):
            act.sem_inc(acc_free, BASE)

            def split_w(c, pieces=range(PIECES)):
                n = COLS[c][2]
                if c >= 2:
                    act.wait_ge(acc_full, first_result[c - 1])
                for q in pieces:
                    r = c * PIECES + q
                    act.wait_ge(w_loaded[r % 2], 16 * (r // 2 + 1))
                    for j in range(2):
                        k = 2 * q + j
                        last = nc.scalar.activation(w_hi[:, c % 2, k, 0:n], w_in[:, r % 2, j, 0:n], ACT.Copy,
                                                    scale=T.g_mix[:, k:k + 1])
                    last.then_inc(w_hi_done, 1)

            def square(t):
                act.wait_ge(x_loaded[t % XR], 16 * (t // XR + 1))
                if t:
                    act.wait_ge(squared, t)
                nc.scalar.activation(junk[:], x_in[:, t % XR, :], ACT.Square,
                                     accum_out=ss[:, t:t + 1]).then_inc(squared, 1)

            square(0)
            square(1)
            act.wait_ge(const.gain_ready, 1)
            for t in range(NT):
                act.wait_ge(x_turned, t + 1)
                nc.scalar.activation(T.act_hi[:, :, t * P:(t + 1) * P], turned[t % 2][:], ACT.Copy,
                                     scale=S_ACT).then_inc(hi_done, 1)
                if t + 2 < NT:
                    square(t + 2)
                if t < PIECES:
                    split_w(0, [t])
            split_w(1)
            for half in range(2):
                if half:
                    const.sines(act)
                for j in range(4):
                    r = 4 * half + j
                    act.wait_ge(acc_full, r + 1)
                    nc.scalar.activation(T.gqk[:, j, half * HALF:(half + 1) * HALF], acc[r % 4][:], ACT.Copy,
                                         scale=UNSCALE).then_inc(acc_free, 1)
            split_w(2)
            for r in range(4):
                act.wait_ge(acc_full, first_result[1] + r + 1)
                nc.scalar.activation(ga[:, r * GA_T:(r + 1) * GA_T], acc[r][0:GLA_RANK, 0:GA_T], ACT.Copy,
                                     scale=UNSCALE).then_inc(ga_out, 1)
            act.wait_ge(ga_out, 4)
            act.sem_inc(acc_free, 4)
            for c in range(2, len(COLS)):
                name = COLS[c][0]
                if name == "gr":
                    steps = Chain(act, soft_step)
                    act.wait_ge(z_done, 2)
                    steps.link(nc.scalar.activation(soft, z, ACT.Abs))
                    steps.link(nc.scalar.activation(soft, soft, ACT.Exp, scale=-1.0))
                    nc.scalar.activation(soft, soft, ACT.Ln, bias=1.0).then_inc(soft_done, 1)
                if c + 1 < len(COLS):
                    split_w(c + 1)
                if name == "dq":
                    act.wait_ge(cum_done, 2)
                if name == "dv":
                    act.wait_ge(acc_free, BASE + first_result[c])
                with act.Fori(0, NT // 4) as i:
                    for b in range(4):
                        act.wait_ge(acc_full, first_result[c] + 4 * i + b + 1)
                        if name in gains:
                            n0 = 8 * (name == "dk")
                            nc.scalar.activation(sq[:, b % 2, :], acc[b][:], ACT.Square,
                                                 scale=UNSCALE * DIFF_DK ** -0.5).then_inc(head_sq, 1)
                            act.wait_ge(head_ss, n0 + 4 * i + b + 1)
                        else:
                            f = ACT.Silu if name == "gr" else ACT.Copy
                            nc.scalar.activation(dest[name][:, bass.ds(4 * i + b, 1), :].rearrange("p a n -> p (a n)"),
                                                 acc[b][:], f, scale=UNSCALE).then_inc(acc_free, 1)

        @block.vector
        def _(dve):
            def split_w(c, pieces=range(PIECES)):
                n = COLS[c][2]
                for q in pieces:
                    r = c * PIECES + q
                    dve.wait_ge(w_hi_done, r + 1)
                    for j in range(2):
                        k = 2 * q + j
                        last = nc.vector.scalar_tensor_tensor(w_lo[:, c % 2, k, 0:n], w_in[:, r % 2, j, 0:n],
                                                              T.g_mix[:, k:k + 1], w_hi[:, c % 2, k, 0:n], ALU.mult,
                                                              ALU.subtract)
                    last.then_inc(w_lo_done, 1)

            def scale(t):
                dve.wait_ge(rstd_done, t + 1)
                nc.vector.tensor_scalar(x_in[:, t % XR, :], x_in[:, t % XR, :], rstd[:, t:t + 1], None,
                                        ALU.mult).then_inc(normed, 1)

            def rope(x, c):
                v = x[:].rearrange("p t (h d) -> p t h d", d=DIFF_DK)
                x1, x2 = v[:, :, :, 0:HROPE], v[:, :, :, HROPE:ROPE]
                shape = [P, NT, 8, HROPE]
                tmp = [x_in[:, 2 + n // 2, n % 2 * HALF:(n % 2 + 1) * HALF].rearrange(
                    "p (t h d) -> p t h d", t=NT, h=8) for n in range(4)]
                cos, sin = (w[:].unsqueeze(2).broadcast_to(shape) for w in (T.cos, T.sin))
                for n, (u, w) in enumerate(((x1, cos), (x2, sin), (x2, cos), (x1, sin))):
                    c.step(nc.vector.tensor_tensor(tmp[n], u, w, ALU.mult))
                c.wait()
                c.step(nc.vector.tensor_tensor(x1, tmp[0], tmp[1], ALU.subtract))
                c.link(nc.vector.tensor_tensor(x2, tmp[2], tmp[3], ALU.add))

            const.gain(dve)
            scale(0)
            scale(1)
            for t in range(NT):
                dve.wait_ge(hi_done, t + 1)
                toks = slice(t * P, (t + 1) * P)
                nc.vector.scalar_tensor_tensor(T.act_lo[:, :, toks], turned[t % 2][:], S_ACT, T.act_hi[:, :, toks],
                                               ALU.mult, ALU.subtract).then_inc(lo_done, 1)
                if t + 2 < NT:
                    scale(t + 2)
                if t < PIECES:
                    dve.wait_ge(const.gain_ready, 1)
                    split_w(0, [t])
            split_w(1)
            const.tables(dve)
            turning = Chain(dve, rot_step)
            for c in range(2, len(COLS) + 1):
                if c < len(COLS):
                    split_w(c)
                if COLS[c - 1][0] == "gv":
                    for ct in range(2):
                        dve.wait_ge(gate_done, ct + 1)
                        nc.vector.tensor_scalar(z[:, ct, :], gate[ct], T.b_gate[:, ct:ct + 1], None,
                                                ALU.add).then_inc(z_done, 1)
                    dve.wait_ge(z_done, 2)
                    dve.wait_ge(soft_done, 1)
                    dve.wait_ge(keep_done, 2)
                    steps = Chain(dve, gate_step)
                    steps.link(nc.vector.scalar_tensor_tensor(z, z, 0.0, soft, ALU.min, ALU.subtract))
                    for ct in range(2):
                        nc.vector.tensor_tensor_scan(T.cum[:, ct, :], keep, z[:, ct, :], 0.0, ALU.mult,
                                                     ALU.add).then_inc(cum_done, 1)
                if COLS[c - 1][0] not in gains:
                    continue
                name = COLS[c - 1][0]
                n0 = 8 * (name == "dk")
                g = gains[name]
                with dve.Fori(0, NT // 4) as i:
                    for b in range(4):
                        dve.wait_ge(head_sq, n0 + 4 * i + b + 1)
                        nc.vector.tensor_reduce(hss[:, b % 2, :], sq[:, b % 2, :].rearrange("p (h d) -> p h d", h=8),
                                                AX.X, ALU.add).then_inc(head_ss, 1)
                        dve.wait_ge(head_r, n0 + 4 * i + b + 1)
                        tile = dest[name][:, bass.ds(4 * i + b, 1), :].rearrange("p a (h d) -> p (a h) d", h=8)
                        nc.vector.scalar_tensor_tensor(tile, acc[b][:].rearrange("p (h d) -> p h d", h=8), UNSCALE,
                                                       lanes(hr[:, b % 2, :], 2, P, 8, DIFF_DK), ALU.mult,
                                                       ALU.mult).then_inc(acc_free, 1)
                        dve.wait_ge(acc_free, BASE + first_result[c - 1] + 4 * i + b + 1)
                        nc.vector.tensor_tensor(tile, tile, lanes(g[:], 1, P, 8, DIFF_DK),
                                                ALU.mult).then_inc(head_normed, 1)
                if name == "dk":
                    const.finish(dve)
                    gr = T.gr[:].rearrange("p t (h v) -> p (t h) v", v=GLA_DV)
                    turning.link(nc.vector.tensor_tensor(gr, gr, lanes(T.g_gla[:], 1, P, NT * GLA_H, GLA_DV), ALU.mult))
                    dve.wait_ge(head_normed, 2 * NT)
                    rope(T.dq, turning)
                    rope(T.dk, turning)

        @block.tensor
        def _(pe):
            def turn(t):
                pe.wait_ge(normed, t + 1)
                if t >= 2:
                    pe.wait_ge(lo_done, t - 1)
                for k in range(KT):
                    last = pe.transpose(turned[t % 2][:, k, :], x_in[:, t % XR, k * P:(k + 1) * P], T.ident[:])
                last.then_inc(x_turned, 1)

            pe.wait_ge(const.masks_ready, 1)
            turns = iter(range(NT))
            for t in range(NT // 2 + 2):
                turn(next(turns))
            pe.wait_ge(lo_done, NT // 2)
            pe.wait_ge(w_lo_done, PIECES)
            pe.wait_ge(acc_free, BASE)
            for half in range(2):
                if half:
                    pe.wait_ge(lo_done, NT)
                toks = slice(half * HALF, (half + 1) * HALF)
                for j in range(4):
                    r = 4 * half + j
                    if r >= 4:
                        pe.wait_ge(acc_free, BASE + r - 3)
                    for k in range(KT):
                        last = split_mm(pe, acc[r % 4][:], w_hi[:, 0, k, j * P:(j + 1) * P],
                                        w_lo[:, 0, k, j * P:(j + 1) * P], T.act_hi[:, k, toks], T.act_lo[:, k, toks],
                                        k == 0, k == KT - 1)
                    last.then_inc(acc_full, 1)
                    for t in turns:
                        turn(t)
                        break
            pe.wait_ge(w_lo_done, PIECES * 2)
            for r in range(4):
                pe.wait_ge(acc_free, BASE - 3 + first_result[1] + r)
                toks = slice(r * GA_T, (r + 1) * GA_T)
                for k in range(KT):
                    last = split_mm(pe, acc[r][0:GLA_RANK, 0:GA_T], w_hi[:, 1, k, 0:GLA_RANK],
                                    w_lo[:, 1, k, 0:GLA_RANK], T.act_hi[:, k, toks], T.act_lo[:, k, toks],
                                    k == 0, k == KT - 1)
                last.then_inc(acc_full, 1)
            for c in range(2, len(COLS)):
                pe.wait_ge(w_lo_done, PIECES * (c + 1))
                with pe.Fori(0, NT // 4) as i:
                    for b in range(4):
                        pe.wait_ge(acc_free, BASE - 3 + first_result[c] + 4 * i + b)
                        toks = bass.ds(i * (4 * P) + b * P, P)
                        for k in range(KT):
                            last = split_mm(pe, acc[b][:], T.act_hi[:, k, toks], T.act_lo[:, k, toks],
                                            w_hi[:, c % 2, k, :], w_lo[:, c % 2, k, :], k == 0, k == KT - 1)
                        last.then_inc(acc_full, 1)
                if COLS[c][0] == "gv":
                    pe.wait_ge(ga_out, 4)
                    for ct in range(2):
                        for half in range(2):
                            toks = slice(half * HALF, (half + 1) * HALF)
                            last = pe.matmul(gate[ct][:, toks], T.w_gate[:, ct * P:(ct + 1) * P], ga[:, toks],
                                             start=True, stop=True)
                        last.then_inc(gate_done, 1)


NCH = SEQ // CHUNK


def gla_states(nc, io, T):
    KVR = 4
    with ExitStack() as ctx:
        S = Space(nc, ctx, "b")
        lent = [x[:].rearrange("p k t -> p (k t)").bitcast(F32).rearrange("p (a c t) -> p a c t", a=2, c=2)
                for x in (T.act_hi, T.act_lo)]
        soft, grow = lent[0][:, 0], lent[1][:, 0]
        ke_n = lent[1][:, 1].rearrange("p c t -> p (c t)").rearrange("p (t n) -> p t n", t=NT)
        fall = S.sb("fall", [P, 2, SEQ])
        ke = S.sb("ke", [P, 2, SEQ])
        decay = S.sb("decay", [P, 2, NCH])
        turned = [S.ps(f"turned{b}", [P, 2, P]) for b in range(2)]
        kv = [S.ps(f"kv{b}", [P, 2, HALF // 2])[:, :, 0:GLA_DV] for b in range(KVR)]
        vec_step = S.sem("vec_step")
        fall_ready = S.sem("fall_ready")
        fall_done = S.sem("fall_done")
        factor = S.sem("factor")
        zeroed = S.sem("zeroed")
        ke_done = S.sem("ke_done")
        ke_turned = S.sem("ke_turned")
        ke_out = S.sem("ke_out")
        kv_done = S.sem("kv_done")
        state_done = S.sem("state_done")
        decay_done = S.sem("decay_done")
        block = ctx.enter_context(nc.Block())

        @block.gpsimd
        def _(pool):
            nc.gpsimd.memset(T.state[:, 0], 0.0).then_inc(zeroed, 1)

        @block.tensor
        def _(pe):
            pe.wait_ge(ke_done, 2)
            for t in range(NT):
                if t >= 2:
                    pe.wait_ge(ke_out, t - 1)
                for ct in range(2):
                    last = pe.transpose(turned[t % 2][:, ct, :], ke[:, ct, t * P:(t + 1) * P], T.ident[:])
                last.then_inc(ke_turned, 1)
            for t in range(NT):
                pe.wait_ge(ke_out, t + 1)
                for c in range(2):
                    n = 2 * t + c
                    if n >= KVR:
                        pe.wait_ge(state_done, n - KVR + 1)
                    rows = slice(c * CHUNK, (c + 1) * CHUNK)
                    for head in range(GLA_H):
                        ct, hh = head // 2, head % 2
                        last = pe.matmul(kv[n % KVR][hh * GLA_DK:(hh + 1) * GLA_DK, ct, :],
                                         ke_n[rows, t, head * GLA_DK:(head + 1) * GLA_DK],
                                         T.gv[rows, t, head * GLA_DV:(head + 1) * GLA_DV], start=True, stop=True)
                    last.then_inc(kv_done, 1)

        @block.scalar
        def _(act):
            for ct in range(2):
                act.wait_ge(fall_ready, ct + 1)
                nc.scalar.activation(fall[:, ct, :], fall[:, ct, :], ACT.Exp, scale=1.0 / GLA_TAU).then_inc(fall_done, 1)
            for ct in range(2):
                nc.scalar.activation(grow[:, ct, :], T.cum[:, ct, :], ACT.Exp, scale=1.0 / GLA_TAU).then_inc(factor, 1)
                nc.scalar.activation(soft[:, ct, :], T.cum[:, ct, :], ACT.Exp, scale=-1.0 / GLA_TAU).then_inc(factor, 1)
            for t in range(NT):
                act.wait_ge(ke_turned, t + 1)
                nc.scalar.activation(ke_n[:, t, :], turned[t % 2][:].rearrange("p a b -> p (a b)"),
                                     ACT.Copy).then_inc(ke_out, 1)

        @block.vector
        def _(dve):
            c = Chain(dve, vec_step)
            for ct in range(2):
                by_chunk = T.cum[:, ct, :].rearrange("p (c s) -> p c s", s=CHUNK)
                nc.vector.tensor_tensor(fall[:, ct, :].rearrange("p (c s) -> p c s", s=CHUNK),
                                        by_chunk[:, :, CHUNK - 1:CHUNK].broadcast_to([P, NCH, CHUNK]), by_chunk,
                                        ALU.subtract).then_inc(fall_ready, 1)
            for ct in range(2):
                dve.wait_ge(fall_done, ct + 1)
                nc.vector.tensor_tensor(ke[:, ct, :], T.gqk[:, 2 + ct, :], fall[:, ct, :], ALU.mult).then_inc(ke_done, 1)
            dve.wait_ge(zeroed, 1)
            dve.wait_ge(ke_done, 2)
            for ct in range(2):
                dve.wait_ge(factor, 2 * ct + 2)
                q, k = T.gqk[:, ct, :], T.gqk[:, 2 + ct, :]
                nc.vector.tensor_copy(decay[:, ct, :], grow[:, ct, :].rearrange("p (c s) -> p c s", s=CHUNK)[:, :,
                                      CHUNK - 1]).then_inc(decay_done, 1)
                c.step(nc.vector.scalar_tensor_tensor(q, grow[:, ct, :], GLA_DK ** -0.5, q, ALU.mult, ALU.mult))
                c.step(nc.vector.tensor_tensor(k, k, soft[:, ct, :], ALU.mult))
            dve.wait_ge(decay_done, 2)
            for n in range(NCH - 1):
                dve.wait_ge(kv_done, n + 1)
                if n:
                    dve.wait_ge(state_done, n)
                for ct in range(2):
                    last = nc.vector.scalar_tensor_tensor(T.state[:, n + 1, ct, :], T.state[:, n, ct, :],
                                                          decay[:, ct, n:n + 1], kv[n % KVR][:, ct, :], ALU.mult,
                                                          ALU.add)
                last.then_inc(state_done, 1)


def by_parity(ap, hh):
    return ap.rearrange("p (c h v) -> p c h v", c=2, h=2)[:, :, hh, :]


def gla_outputs(nc, io, T):
    with ExitStack() as ctx:
        S = Space(nc, ctx, "g")
        att_m = S.sb("att_m", [P, 2, GLA_H, P])
        o_s = S.sb("o_s", [P, 2, HALF])
        sq = S.sb("sq", [P, 2, HALF])
        ss = S.sb("ss", [P, NT, GLA_H])
        o_n = S.sb("o_n", [P, 2, GLA_H, GLA_DV])
        att = [[S.ps(f"att{b}{hh}", [P, 2, HALF // 2])[:, :, 0:P] for hh in range(2)] for b in range(2)]
        o = [S.ps(f"o{hh}", [P, 2, HALF // 2])[:, :, 0:GLA_DV] for hh in range(2)]
        turned = [S.ps(f"turned{b}", [P, GLA_H, P]) for b in range(2)]
        att_done = S.sem("att_done")
        masked = S.sem("masked")
        o_done = S.sem("o_done")
        o_free = S.sem("o_free")
        squared = S.sem("squared")
        summed = S.sem("summed")
        pool_step = S.sem("pool_step")
        rstd_done = S.sem("rstd_done")
        o_out = S.sem("o_out")
        o_turned = S.sem("o_turned")
        hi_done = S.sem("hi_done")
        lo_done = S.sem("lo_done")
        block = ctx.enter_context(nc.Block())

        @block.gpsimd
        def _(pool):
            c = Chain(pool, pool_step)
            for t in range(NT):
                pool.wait_ge(summed, t + 1)
                c.link(nc.gpsimd.tensor_scalar(ss[:, t, :], ss[:, t, :], 1.0 / GLA_DV, EPS, ALU.mult, ALU.add))
                nc.gpsimd.tensor_tensor(ss[:, t, :], ss[:, t, :], T.mhalf[:, 0:GLA_H],
                                        ALU.pow).then_inc(rstd_done, 1)

        @block.tensor
        def _(pe):
            def scores(t):
                if t >= 2:
                    pe.wait_ge(masked, t - 1)
                for h in range(GLA_H):
                    r = slice((h % 2) * GLA_DK, (h % 2 + 1) * GLA_DK)
                    toks = slice(t * P, (t + 1) * P)
                    last = pe.matmul(att[t % 2][h % 2][:, h // 2, :], T.gqk[r, 2 + h // 2, toks], T.gqk[r, h // 2, toks],
                                     start=True, stop=True)
                last.then_inc(att_done, 1)

            def outputs(t):
                pe.wait_ge(masked, t + 1)
                if t:
                    pe.wait_ge(o_free, t)
                for h in range(GLA_H):
                    r = slice((h % 2) * GLA_DK, (h % 2 + 1) * GLA_DK)
                    last = pe.matmul(o[h % 2][:, h // 2, :], att_m[:, t % 2, h, :], T.gv[:, t, h * GLA_DV:(h + 1) * GLA_DV],
                                     start=True, stop=False)
                    for c in range(2):
                        toks = slice(t * P + c * CHUNK, t * P + (c + 1) * CHUNK)
                        last = pe.matmul(o[h % 2][c * CHUNK:(c + 1) * CHUNK, h // 2, :], T.gqk[r, h // 2, toks],
                                         T.state[r, 2 * t + c, h // 2, :], start=False, stop=True)
                last.then_inc(o_done, 1)

            def turn(t):
                pe.wait_ge(o_out, t + 1)
                if t >= 2:
                    pe.wait_ge(lo_done, t - 1)
                for h in range(GLA_H):
                    last = pe.transpose(turned[t % 2][:, h, :], o_n[:, t % 2, h, :], T.ident[:])
                last.then_inc(o_turned, 1)

            scores(0)
            for t in range(NT + 2):
                if t + 1 < NT:
                    scores(t + 1)
                if t < NT:
                    outputs(t)
                if t >= 2:
                    turn(t - 2)

        @block.scalar
        def _(act):
            for t in range(NT + 2):
                if t < NT:
                    act.wait_ge(o_done, t + 1)
                    if t >= 2:
                        act.wait_ge(o_out, t - 1)
                    for hh in range(2):
                        last = nc.scalar.activation(by_parity(o_s[:, t % 2, :], hh), o[hh], ACT.Copy)
                    last.then_inc(o_free, 1)
                    act.wait_ge(o_free, t + 1)
                    nc.scalar.activation(sq[:, t % 2, :], o_s[:, t % 2, :], ACT.Square).then_inc(squared, 1)
                if t >= 2:
                    act.wait_ge(o_turned, t - 1)
                    nc.scalar.activation(T.act_hi[:, 0:GLA_H, (t - 2) * P:(t - 1) * P], turned[t % 2][:], ACT.Copy,
                                         scale=S_ACT).then_inc(hi_done, 1)

        @block.vector
        def _(dve):
            def mask(t):
                dve.wait_ge(att_done, t + 1)
                if t >= 2:
                    dve.wait_ge(o_done, t - 1)
                for hh in range(2):
                    last = nc.vector.tensor_tensor(by_parity(att_m[:, t % 2].rearrange("p h c -> p (h c)"), hh),
                                                   att[t % 2][hh], lanes(T.tri[:], 1, P, 2, P), ALU.mult)
                last.then_inc(masked, 1)

            def norm(t):
                dve.wait_ge(squared, t + 1)
                nc.vector.tensor_reduce(ss[:, t, :], sq[:, t % 2, :].rearrange("p (h v) -> p h v", h=GLA_H), AX.X,
                                        ALU.add).then_inc(summed, 1)
                dve.wait_ge(rstd_done, t + 1)
                if t >= 2:
                    dve.wait_ge(o_turned, t - 1)
                for h in range(GLA_H):
                    cols = slice(h * GLA_DV, (h + 1) * GLA_DV)
                    last = nc.vector.scalar_tensor_tensor(o_n[:, t % 2, h, :], o_s[:, t % 2, cols], ss[:, t, h:h + 1],
                                                          T.gr[:, t, cols], ALU.mult, ALU.mult)
                last.then_inc(o_out, 1)

            mask(0)
            for t in range(NT + 2):
                if t + 1 < NT:
                    mask(t + 1)
                if 1 <= t <= NT:
                    norm(t - 1)
                if t >= 2:
                    dve.wait_ge(hi_done, t - 1)
                    toks = slice((t - 2) * P, (t - 1) * P)
                    nc.vector.scalar_tensor_tensor(T.act_lo[:, 0:GLA_H, toks], turned[t % 2][:], S_ACT,
                                                   T.act_hi[:, 0:GLA_H, toks], ALU.mult,
                                                   ALU.subtract).then_inc(lo_done, 1)


def diff_attention(nc, io, T):
    SCALE = DIFF_DK ** -0.5
    units = [(b, h) for b in range(NT) for h in range(DIFF_H)]
    with ExitStack() as ctx:
        S = Space(nc, ctx, "d")
        q_hi, q_lo, k_hi, k_lo = (S.sb(n, [P, DIFF_H, SEQ], F16) for n in ("q_hi", "q_lo", "k_hi", "k_lo"))
        ident = S.sb("ident", [P, P], BF16)
        causal = S.sb("causal", [P, P], BF16)
        mx = S.sb("mx", [P, 2, 2])
        sums = S.sb("sums", [P, 2, 2])
        inv = S.sb("inv", [P, 2, 2])
        mix = S.sb("mix", [P, 2])
        e = S.sb("e", [P, 2, 2, SEQ])
        a = S.sb("a", [P, 2, SEQ])
        a_t = S.sb("a_t", [P, 2, SEQ])
        junk = S.sb("junk", [P, DIFF_DV])
        ss = S.sb("ss", [P, 2])
        o_s = S.sb("o_s", [P, 2, DIFF_DV])
        o_n = S.sb("o_n", [P, 2, DIFF_H, DIFF_DV])
        sc = [S.ps(f"sc{m}", [P, SEQ]) for m in range(2)]
        qk_ps = [sc[n // 2][:, n % 2 * HALF:(n % 2 + 1) * HALF].rearrange("p (h t) -> p h t", h=DIFF_H)
                 for n in range(4)]
        a_ps = S.ps("a_ps", [P, SEQ])
        o = S.ps("o", [P, DIFF_DV])
        turned = S.ps("turned", [P, DIFF_H, P])
        mask_ready = S.sem("mask_ready")
        qk_turned = S.sem("qk_turned")
        qk_hi = S.sem("qk_hi")
        qk_lo = S.sem("qk_lo")
        scored = [S.sem(f"scored{m}") for m in range(2)]
        max_done = [S.sem(f"max_done{m}") for m in range(2)]
        vec_step = S.sem("vec_step")
        exp_done = [S.sem(f"exp_done{m}") for m in range(2)]
        combined = S.sem("combined")
        a_turned = S.sem("a_turned")
        a_out = S.sem("a_out")
        o_done = S.sem("o_done")
        o_scaled = S.sem("o_scaled")
        squared = S.sem("squared")
        pool_step = S.sem("pool_step")
        rstd_done = S.sem("rstd_done")
        o_out = S.sem("o_out")
        o_turned = S.sem("o_turned")
        hi_done = S.sem("hi_done")
        lo_done = S.sem("lo_done")
        w_out_loaded = S.sem("w_out_loaded")
        block = ctx.enter_context(nc.Block())

        @block.sync
        def _(sp):
            for k in range(KT):
                sp.dma_start(T.w_out[:, k, :], io.w_out[0, k * P:(k + 1) * P, :]).then_inc(w_out_loaded, 16)
            sp.wait_ge(w_out_loaded, 16 * KT)

        @block.gpsimd
        def _(pool):
            nc.gpsimd.tensor_copy(ident[:], T.ident[:]).then_inc(mask_ready, 1)
            nc.gpsimd.tensor_copy(causal[:], T.causal[:]).then_inc(mask_ready, 1)
            c = Chain(pool, pool_step)
            for u in range(len(units)):
                pool.wait_ge(squared, u + 1)
                s = ss[:, u % 2:u % 2 + 1]
                c.link(nc.gpsimd.tensor_scalar(s, s, 1.0 / DIFF_DV, EPS, ALU.mult, ALU.add))
                nc.gpsimd.tensor_tensor(s, s, T.mhalf[:, 0:1], ALU.pow).then_inc(rstd_done, 1)

        @block.tensor
        def _(pe):
            pe.wait_ge(mask_ready, 2)
            n = 0
            for t in range(NT):
                for x in (T.dq, T.dk):
                    if n >= 4:
                        pe.wait_ge(qk_lo, n - 3)
                    for h in range(DIFF_H):
                        last = pe.transpose(qk_ps[n % 4][:, h, :], x[:, t, h * P:(h + 1) * P], T.ident[:])
                    last.then_inc(qk_turned, 1)
                    n += 1
            pe.wait_ge(qk_lo, n)

            def scores(u, m):
                b, h = units[u]
                keys = (b + 1) * P
                if u:
                    pe.wait_ge(exp_done[m], u)
                r = slice(m * DIFF_DK, (m + 1) * DIFF_DK)
                for k0 in range(0, keys, HALF):
                    k1 = min(keys, k0 + HALF)
                    toks = slice(b * P, (b + 1) * P)
                    split_mm(pe, sc[m][:, k0:k1], q_hi[r, h, toks], q_lo[r, h, toks], k_hi[r, h, k0:k1],
                             k_lo[r, h, k0:k1], True, k1 < keys)
                pe.matmul(sc[m][:, b * P:keys], ident[:], causal[:], start=False, stop=True).then_inc(scored[m], 1)

            def turn_probs(u):
                b, h = units[u]
                pe.wait_ge(combined, u + 1)
                if u:
                    pe.wait_ge(a_out, u)
                for kb in range(b + 1):
                    last = pe.transpose(a_ps[:, kb * P:(kb + 1) * P], a[:, u % 2, kb * P:(kb + 1) * P], T.ident[:])
                last.then_inc(a_turned, 1)

            def values(u):
                b, h = units[u]
                pe.wait_ge(a_out, u + 1)
                if u:
                    pe.wait_ge(o_scaled, u)
                for kb in range(b + 1):
                    last = pe.matmul(o[:], a_t[:, u % 2, kb * P:(kb + 1) * P], T.dv[:, kb, h * DIFF_DV:(h + 1) * DIFF_DV],
                                     start=(kb == 0), stop=(kb == b))
                last.then_inc(o_done, 1)

            def turn(b):
                pe.wait_ge(o_out, DIFF_H * (b + 1))
                if b:
                    pe.wait_ge(lo_done, b)
                for h in range(DIFF_H):
                    last = pe.transpose(turned[:, h, :], o_n[:, b % 2, h, :], T.ident[:])
                last.then_inc(o_turned, 1)

            for m in range(2):
                scores(0, m)
            for u, (b, h) in enumerate(units):
                more = u + 1 < len(units)
                if more:
                    scores(u + 1, 0)
                turn_probs(u)
                if more:
                    scores(u + 1, 1)
                values(u)
                if h == 1 and b:
                    turn(b - 1)
            turn(NT - 1)

        @block.scalar
        def _(act):
            n = 0
            for t in range(NT):
                for x in (q_hi, k_hi):
                    act.wait_ge(qk_turned, n + 1)
                    nc.scalar.activation(x[:, :, t * P:(t + 1) * P], qk_ps[n % 4], ACT.Copy,
                                         scale=S_ACT).then_inc(qk_hi, 1)
                    n += 1

            def exps(u, m):
                b, h = units[u]
                act.wait_ge(max_done[m], u + 1)
                if u >= 2:
                    act.wait_ge(combined, u - 1)
                nc.scalar.activation(e[:, u % 2, m, 0:(b + 1) * P], sc[m][:, 0:(b + 1) * P], ACT.Exp,
                                     bias=mx[:, u % 2, m:m + 1], scale=SCALE / S_ACT ** 2,
                                     accum_out=sums[:, u % 2, m:m + 1]).then_inc(exp_done[m], 1)

            def probs_out(u):
                b, h = units[u]
                act.wait_ge(a_turned, u + 1)
                if u >= 2:
                    act.wait_ge(o_done, u - 1)
                nc.scalar.activation(a_t[:, u % 2, 0:(b + 1) * P], a_ps[:, 0:(b + 1) * P], ACT.Copy).then_inc(a_out, 1)

            def output(u):
                act.wait_ge(o_done, u + 1)
                if u >= 2:
                    act.wait_ge(o_out, u - 1)
                nc.scalar.activation(o_s[:, u % 2, :], o[:], ACT.Copy, scale=inv[:, u % 2, 0:1]).then_inc(o_scaled, 1)
                act.wait_ge(o_scaled, u + 1)
                if u:
                    act.wait_ge(squared, u)
                nc.scalar.activation(junk[:], o_s[:, u % 2, :], ACT.Square,
                                     accum_out=ss[:, u % 2:u % 2 + 1]).then_inc(squared, 1)

            def turned_hi(b):
                act.wait_ge(o_turned, b + 1)
                nc.scalar.activation(T.act_hi[:, DIFF_H:2 * DIFF_H, b * P:(b + 1) * P], turned[:], ACT.Copy,
                                     scale=T.g_sub[:, 0:1]).then_inc(hi_done, 1)

            for m in range(2):
                exps(0, m)
            for u, (b, h) in enumerate(units):
                probs_out(u)
                if u + 1 < len(units):
                    for m in range(2):
                        exps(u + 1, m)
                output(u)
                if h == 1 and b:
                    turned_hi(b - 1)
            turned_hi(NT - 1)

        @block.vector
        def _(dve):
            n = 0
            for t in range(NT):
                toks = slice(t * P, (t + 1) * P)
                for hi, lo in ((q_hi, q_lo), (k_hi, k_lo)):
                    dve.wait_ge(qk_hi, n + 1)
                    nc.vector.scalar_tensor_tensor(lo[:, :, toks], qk_ps[n % 4], S_ACT, hi[:, :, toks], ALU.mult,
                                                   ALU.subtract).then_inc(qk_lo, 1)
                    n += 1
            c = Chain(dve, vec_step)

            def maximum(u, m):
                b, h = units[u]
                dve.wait_ge(scored[m], u + 1)
                if u >= 2:
                    dve.wait_ge(exp_done[m], u - 1)
                c.link(nc.vector.tensor_reduce(mx[:, u % 2, m:m + 1], sc[m][:, 0:(b + 1) * P], AX.X, ALU.max))
                nc.vector.tensor_scalar(mx[:, u % 2, m:m + 1], mx[:, u % 2, m:m + 1], -SCALE / S_ACT ** 2, None,
                                        ALU.mult).then_inc(max_done[m], 1)

            def combine(u):
                b, h = units[u]
                for m in range(2):
                    dve.wait_ge(exp_done[m], u + 1)
                if u >= 2:
                    dve.wait_ge(o_scaled, u - 1)
                    dve.wait_ge(a_turned, u - 1)
                c.link(nc.vector.reciprocal(inv[:, u % 2, :], sums[:, u % 2, :]))
                c.link(nc.vector.scalar_tensor_tensor(mix[:, u % 2:u % 2 + 1], inv[:, u % 2, 1:2], sums[:, u % 2, 0:1],
                                                      T.neg_lam[:], ALU.mult, ALU.mult))
                nc.vector.scalar_tensor_tensor(a[:, u % 2, 0:(b + 1) * P], e[:, u % 2, 1, 0:(b + 1) * P],
                                               mix[:, u % 2:u % 2 + 1], e[:, u % 2, 0, 0:(b + 1) * P], ALU.mult,
                                               ALU.add).then_inc(combined, 1)

            def norm(u):
                b, h = units[u]
                dve.wait_ge(rstd_done, u + 1)
                if h == 0 and b >= 2:
                    dve.wait_ge(o_turned, b - 1)
                nc.vector.tensor_scalar(o_n[:, b % 2, h, :], o_s[:, u % 2, :], ss[:, u % 2:u % 2 + 1], None,
                                        ALU.mult).then_inc(o_out, 1)

            def turned_lo(b):
                dve.wait_ge(hi_done, b + 1)
                toks = slice(b * P, (b + 1) * P)
                nc.vector.scalar_tensor_tensor(T.act_lo[:, DIFF_H:2 * DIFF_H, toks], turned[:], T.g_sub[:, 0:1],
                                               T.act_hi[:, DIFF_H:2 * DIFF_H, toks], ALU.mult,
                                               ALU.subtract).then_inc(lo_done, 1)

            for m in range(2):
                maximum(0, m)
            for u, (b, h) in enumerate(units):
                combine(u)
                if u + 1 < len(units):
                    for m in range(2):
                        maximum(u + 1, m)
                if u:
                    norm(u - 1)
                if h == 2 and b:
                    turned_lo(b - 1)
            norm(len(units) - 1)
            turned_lo(NT - 1)


def project_out(nc, io, T):
    with ExitStack() as ctx:
        S = Space(nc, ctx, "o")
        w_hi = S.sb("w_hi", [P, KT, D], F16)
        w_lo = S.sb("w_lo", [P, KT, D], F16)
        x_in = S.sb("x_in", [P, 2, D])
        xs = S.sb("xs", [P, 2, D])
        gain = S.sb("gain", [P, D])
        junk = S.sb("junk", [P, D], F16)
        ss = S.sb("ss", [P, NT])
        acc = [S.ps(f"acc{b}", [P, D]) for b in range(2)]
        turned = [S.ps(f"turned{b}", [P, KT, P]) for b in range(2)]
        next_loaded = S.sem("next_loaded")
        x_loaded = [S.sem(f"x_loaded{b}") for b in range(2)]
        gain_loaded = S.sem("gain_loaded")
        w_hi_done = S.sem("w_hi_done")
        w_lo_done = S.sem("w_lo_done")
        acc_done = S.sem("acc_done")
        h_done = S.sem("h_done")
        squared = S.sem("squared")
        pool_step = S.sem("pool_step")
        rstd_done = S.sem("rstd_done")
        normed = S.sem("normed")
        x_turned = S.sem("x_turned")
        hi_done = S.sem("hi_done")
        lo_done = S.sem("lo_done")
        block = ctx.enter_context(nc.Block())

        @block.sync
        def _(sp):
            sp.dma_start(gain[:], io.g_ffn[0, :].partition_broadcast(P)).then_inc(gain_loaded, 16)
            for t in range(NT):
                if t >= 2:
                    sp.wait_ge(h_done, t - 1)
                sp.dma_start(x_in[:, t % 2, :], io.x[0, t * P:(t + 1) * P, :]).then_inc(x_loaded[t % 2], 16)
            sp.dma_start(T.w_peer[:], io.w_peer_q[0, :, 0:QDIM].rearrange("(k p) c -> p k c", p=P)).then_inc(
                next_loaded, 16)
            sp.dma_start(T.keys[:], io.peer_sub_keys[0].rearrange("h m k q -> k (h m) q")).then_inc(next_loaded, 16)
            sp.wait_ge(next_loaded, 32)

        @block.gpsimd
        def _(pool):
            c = Chain(pool, pool_step)
            for t in range(NT):
                pool.wait_ge(squared, t + 1)
                c.link(nc.gpsimd.tensor_scalar(ss[:, t:t + 1], ss[:, t:t + 1], 1.0 / D, EPS, ALU.mult, ALU.add))
                nc.gpsimd.tensor_tensor(ss[:, t:t + 1], ss[:, t:t + 1], T.mhalf[:, 0:1], ALU.pow).then_inc(rstd_done, 1)

        @block.tensor
        def _(pe):
            def project(t):
                if t >= 2:
                    pe.wait_ge(h_done, t - 1)
                toks = slice(t * P, (t + 1) * P)
                for k in range(KT):
                    if t == 0:
                        pe.wait_ge(w_lo_done, k + 1)
                    for half in range(2):
                        cols = slice(half * HALF, (half + 1) * HALF)
                        last = split_mm(pe, acc[t % 2][:, cols], T.act_hi[:, k, toks], T.act_lo[:, k, toks],
                                        w_hi[:, k, cols], w_lo[:, k, cols], k == 0, k == KT - 1)
                last.then_inc(acc_done, 1)

            def turn(t):
                pe.wait_ge(normed, t + 1)
                if t >= 2:
                    pe.wait_ge(lo_done, t - 1)
                for k in range(KT):
                    last = pe.transpose(turned[t % 2][:, k, :], xs[:, t % 2, k * P:(k + 1) * P], T.ident[:])
                last.then_inc(x_turned, 1)

            project(0)
            for t in range(NT):
                if t + 1 < NT:
                    project(t + 1)
                turn(t)

        @block.scalar
        def _(act):
            for k in range(KT):
                nc.scalar.activation(w_hi[:, k, :], T.w_out[:, k, :], ACT.Copy, scale=S_W).then_inc(w_hi_done, 1)
            for t in range(NT + 1):
                if t < NT:
                    act.wait_ge(h_done, t + 1)
                    if t:
                        act.wait_ge(squared, t)
                    nc.scalar.activation(junk[:], T.h[:, t, :], ACT.Square,
                                         accum_out=ss[:, t:t + 1]).then_inc(squared, 1)
                if t:
                    act.wait_ge(x_turned, t)
                    nc.scalar.activation(T.act_hi[:, :, (t - 1) * P:t * P], turned[(t - 1) % 2][:], ACT.Copy,
                                         scale=S_ACT).then_inc(hi_done, 1)

        @block.vector
        def _(dve):
            for k in range(KT):
                dve.wait_ge(w_hi_done, k + 1)
                nc.vector.scalar_tensor_tensor(w_lo[:, k, :], T.w_out[:, k, :], S_W, w_hi[:, k, :], ALU.mult,
                                               ALU.subtract).then_inc(w_lo_done, 1)
            dve.wait_ge(gain_loaded, 16)
            for t in range(NT + 1):
                if t < NT:
                    dve.wait_ge(acc_done, t + 1)
                    dve.wait_ge(x_loaded[t % 2], 16 * (t // 2 + 1))
                    nc.vector.scalar_tensor_tensor(T.h[:, t, :], acc[t % 2][:], UNSCALE, x_in[:, t % 2, :], ALU.mult,
                                                   ALU.add).then_inc(h_done, 1)
                    dve.wait_ge(rstd_done, t + 1)
                    if t >= 2:
                        dve.wait_ge(x_turned, t - 1)
                    nc.vector.scalar_tensor_tensor(xs[:, t % 2, :], T.h[:, t, :], ss[:, t:t + 1], gain[:], ALU.mult,
                                                   ALU.mult).then_inc(normed, 1)
                if t:
                    dve.wait_ge(hi_done, t)
                    toks = slice((t - 1) * P, t * P)
                    nc.vector.scalar_tensor_tensor(T.act_lo[:, :, toks], turned[(t - 1) % 2][:], S_ACT,
                                                   T.act_hi[:, :, toks], ALU.mult, ALU.subtract).then_inc(lo_done, 1)


S_U = 64.0
EARLY_R = 2
EARLY_S = 3
BLOCK = 64
NBLOCK = SEQ // BLOCK
TB = 32
NTB = SEQ // TB
N_EARLY = EARLY_R * PEER_H + EARLY_S * NBLOCK


class EarlyTiles:

    def __init__(self, nc, io, T, S, ring, first, count):
        self.nc, self.T, self.ring = nc, T, ring
        rows = io.peer_u[0, first * P:(first + count) * P, :]
        self.u_rows = rows.rearrange("(c b p) d -> c b p d", b=ring, p=P)
        self.kept_rows = T.kept[first * P:(first + count) * P, :].rearrange("(c b p) t -> c b p t", b=ring, p=P)
        self.u_in = [S.sb(f"u_in{b}", [P, D]) for b in range(ring)]
        self.u_hi = [S.sb(f"u_hi{b}", [P, KT, P], F16) for b in range(ring)]
        self.u_lo = [S.sb(f"u_lo{b}", [P, KT, P], F16) for b in range(ring)]
        self.u_all = S.sb("u_all", [P, KT, P])
        self.gel = [S.sb(f"gel{b}", [P, SEQ]) for b in range(ring)]
        self.u_ps = S.ps("u_ps", [P, KT, P])
        self.hid = [S.ps(f"hid{b}", [P, HALF]) for b in range(2)]
        self.u_loaded = [S.sem(f"u_loaded{b}") for b in range(ring)]
        self.u_turned = S.sem("u_turned")
        self.u_hi_done = S.sem("u_hi_done")
        self.u_all_done = S.sem("u_all_done")
        self.u_lo_done = S.sem("u_lo_done")
        self.hid_done = S.sem("hid_done")
        self.gelu_done = S.sem("gelu_done")
        self.kept = [S.sem(f"kept{b}") for b in range(ring)]

    def prime_tensor(self, pe):
        pe.sem_inc(self.hid_done, BASE)

    def prime_scalar(self, act):
        act.sem_inc(self.u_all_done, BASE)
        act.sem_inc(self.gelu_done, BASE)
        for b in range(self.ring):
            act.sem_inc(self.kept[b], BASE)

    def prime_gpsimd(self, pool):
        pool.sem_inc(self.u_lo_done, BASE)

    def load(self, sp, c, b, again=True):
        if again:
            sp.wait_ge(self.u_turned, (c - 1) * self.ring + b + 1)
        sp.dma_start(self.u_in[b][:], self.u_rows[c, b]).then_inc(self.u_loaded[b], 16)

    def keep(self, queue, c, b):
        queue.wait_ge(self.gelu_done, BASE + 2 * (c * self.ring + b) + 2)
        queue.dma_start(self.kept_rows[c, b], self.gel[b][:]).then_inc(self.kept[b], 16)

    def all_kept(self, sp, count):
        for b in range(self.ring):
            sp.wait_ge(self.kept[b], BASE + 16 * (count // self.ring))

    def turn(self, pe, c, b):
        pe.wait_ge(self.u_loaded[b], c * 16 + 16)
        pe.wait_ge(self.u_all_done, BASE + c * self.ring + b)
        for k in range(KT):
            last = pe.transpose(self.u_ps[:, k, :], self.u_in[b][:, k * P:(k + 1) * P], self.T.ident[:])
        last.then_inc(self.u_turned, 1)

    def split(self, act, c, b):
        n = c * self.ring + b
        act.wait_ge(self.u_turned, n + 1)
        act.wait_ge(self.hid_done, BASE + 2 * (n - self.ring) + 2)
        self.nc.scalar.activation(self.u_hi[b][:], self.u_ps[:], ACT.Copy, scale=S_U).then_inc(self.u_hi_done, 1)
        act.wait_ge(self.u_lo_done, BASE + n)
        self.nc.scalar.activation(self.u_all[:], self.u_ps[:], ACT.Copy, scale=S_U).then_inc(self.u_all_done, 1)

    def low(self, pool, c, b):
        n = c * self.ring + b
        pool.wait_ge(self.u_hi_done, n + 1)
        pool.wait_ge(self.u_all_done, BASE + n + 1)
        self.nc.gpsimd.tensor_tensor(self.u_lo[b][:], self.u_all[:], self.u_hi[b][:],
                                     ALU.subtract).then_inc(self.u_lo_done, 1)

    def hidden(self, pe, c, b, half):
        n = c * self.ring + b
        if half == 0:
            pe.wait_ge(self.u_lo_done, BASE + n + 1)
        pe.wait_ge(self.gelu_done, BASE + 2 * (n - 1) + half + 1)
        toks = slice(half * HALF, (half + 1) * HALF)
        for k in range(KT):
            last = split_mm(pe, self.hid[half][:], self.u_hi[b][:, k, :], self.u_lo[b][:, k, :],
                            self.T.act_hi[:, k, toks], self.T.act_lo[:, k, toks], k == 0, k == KT - 1)
        last.then_inc(self.hid_done, 1)

    def gelu(self, act, c, b, half):
        n = c * self.ring + b
        if half == 0:
            act.wait_ge(self.kept[b], BASE + 16 * c)
        act.wait_ge(self.hid_done, BASE + 2 * n + half + 1)
        self.nc.scalar.activation(self.gel[b][:, half * HALF:(half + 1) * HALF], self.hid[half][:], ACT.Gelu,
                                  scale=1.0 / (S_U * S_ACT)).then_inc(self.gelu_done, 1)


NSET = 2 * PEER_H
FLOOR = -3.0e38


def retrieve(nc, io, T):
    with ExitStack() as ctx:
        S = Space(nc, ctx, "r")
        E = EarlyTiles(nc, io, T, S, EARLY_R, 0, EARLY_R * PEER_H)
        w_in = T.w_peer
        w_hi = [S.sb(f"w_hi{b}", [P, KT, QDIM], F16) for b in range(2)]
        w_lo = [S.sb(f"w_lo{b}", [P, KT, QDIM], F16) for b in range(2)]
        keys_t = S.sb("keys_t", [P, NSET, P])
        q_t = S.sb("q_t", [P, 2, SEQ])
        s = T.picked_all[:, 0:2 * SEQ].rearrange("p (t m k) -> p t m k", t=NT, m=2)
        keys = T.keys
        s2 = keys[:].rearrange("p (t m) k -> p t m k", m=2)
        top = S.sb("top", [P, NT, 2, TOPK])
        top_i = S.sb("top_i", [P, NT, 2, TOPK], U32)
        top_f = S.sb("top_f", [P, 2, NT, 2, TOPK], F16)
        cand = S.sb("cand", [P, NT, TOPK * TOPK])
        cand2 = s2.rearrange("p t m k -> p t (m k)")
        best = S.sb("best", [P, NT, TOPK])
        pos = S.sb("pos", [P, NT * TOPK], U32)
        part = S.sb("part", [P, 2, NT * TOPK], U32)
        part_f = S.sb("part_f", [P, 2, NT * TOPK], F16)
        weight = S.sb("weight", [P, NT, TOPK])
        total = S.sb("total", [P, NT])
        carrier = S.sb("carrier", [1, 5])
        match = S.sb("match", [P, 2, NT * TOPK, TOPK], F16)
        picked = [S.sb(f"picked{n}", [P, NT, PICKS]) for n in range(3)]
        bank = [S.ps(f"bank{r}", [P, 4, NKEYS]) for r in range(4)]

        w_loaded = S.sem("w_loaded")
        w_scaled = S.sem("w_scaled")
        w_hi_done = S.sem("w_hi_done")
        w_lo_done = S.sem("w_lo_done")
        keys_turned = S.sem("keys_turned")
        keys_out = S.sem("keys_out")
        q_done = S.sem("q_done")
        q_out = S.sem("q_out")
        scored = S.sem("scored")
        s_out = S.sem("s_out")
        vec_step = S.sem("vec_step")
        s_used = S.sem("s_used")
        shifted = S.sem("shifted")
        weighted = S.sem("weighted")
        found = S.sem("found")
        matched = S.sem("matched")
        index_done = S.sem("index_done")
        weight_done = S.sem("weight_done")
        all_turned = S.sem("all_turned")
        all_out = S.sem("all_out")
        block = ctx.enter_context(nc.Block())
        PAIRS = PEER_H // 2

        @block.sync
        def _(sp):
            w_v = io.w_peer_q[0].rearrange("(k p) (h c) -> h p k c", p=P, c=QDIM)

            def load_w(h):
                sp.dma_start(w_in[:], w_v[h]).then_inc(w_loaded, 16)

            def step(hh, b, first=False, last=False):
                h = 2 * hh + b
                if not last:
                    sp.wait_ge(w_lo_done, h + 2)
                    load_w(h + 2)
                if not (first and b == 0):
                    E.load(sp, h, 1)
                if not (last and b):
                    E.load(sp, h + 1, 0)

            sp.sem_inc(w_loaded, 16)
            for r in range(EARLY_R):
                E.load(sp, 0, r, again=False)
            sp.wait_ge(w_lo_done, 1)
            load_w(1)
            for b in range(2):
                step(0, b, first=True)
            with sp.Fori(1, PAIRS - 1) as hh:
                for b in range(2):
                    step(hh, b)
            for b in range(2):
                step(PAIRS - 1, b, last=True)
            E.all_kept(sp, EARLY_R * PEER_H)

        @block.tensor
        def _(pe):
            E.prime_tensor(pe)

            def queries(h, slot, first=False, sets=(0, 1)):
                pe.wait_ge(w_lo_done, h + 1)
                for m, half in ((m, half) for m in sets for half in range(2)):
                    r = 2 * m + half
                    if first:
                        pe.wait_ge(keys_out, r + 1)
                    else:
                        pe.wait_ge(s_out, 4 * (h - 1) + r + 1)
                    toks, cols = slice(half * HALF, (half + 1) * HALF), slice(m * P, (m + 1) * P)
                    for k in range(KT):
                        last = split_mm(pe, bank[r][:].rearrange("p a b -> p (a b)"), w_hi[slot][:, k, cols],
                                        w_lo[slot][:, k, cols], T.act_hi[:, k, toks], T.act_lo[:, k, toks],
                                        k == 0, k == KT - 1)
                    last.then_inc(q_done, 1)

            def scores(h, sets=(0, 1)):
                for m in sets:
                    pe.wait_ge(q_out, 4 * h + 2 * m + 2)
                    for g in range(2):
                        for j in range(4):
                            t = 4 * g + j
                            last = pe.matmul(bank[2 * m + g][:, j, :], q_t[:, m, t * P:(t + 1) * P],
                                             keys_t[:, bass.ds(2 * h + m, 1), :].rearrange("p a k -> p (a k)"),
                                             start=True, stop=True)
                        last.then_inc(scored, 1)

            def step(hh, b, first=False, last=False):
                h = 2 * hh + b
                before = not (first and b == 0)
                if before:
                    E.turn(pe, h - 1, 1)
                else:
                    E.turn(pe, h, 0)
                if not (last and b):
                    queries(h + 1, 1 - b)
                    scores(h + 1)
                if before:
                    E.hidden(pe, h - 1, 1, 0)
                    E.turn(pe, h, 0)
                    E.hidden(pe, h - 1, 1, 1)
                E.hidden(pe, h, 0, 0)
                if last and b:
                    E.turn(pe, h, 1)
                E.hidden(pe, h, 0, 1)
                if last and b:
                    E.hidden(pe, h, 1, 0)
                    E.hidden(pe, h, 1, 1)

            for r in range(4):
                for j in range(4):
                    last = pe.transpose(bank[r][:, j, :], keys[:, 4 * r + j, :], T.ident[:])
                last.then_inc(keys_turned, 1)
            for m in range(2):
                queries(0, 0, first=True, sets=(m,))
                scores(0, sets=(m,))
            for b in range(2):
                step(0, b, first=True)
            with pe.Fori(1, PAIRS - 1) as hh:
                for b in range(2):
                    step(hh, b)
            for b in range(2):
                step(PAIRS - 1, b, last=True)
            pe.wait_ge(index_done, BASE + 2 * PEER_H)
            pe.wait_ge(weight_done, PEER_H)
            for n in range(3):
                for g in range(2):
                    r = 2 * n + g
                    if r >= 4:
                        pe.wait_ge(all_out, r - 3)
                    for j in range(4):
                        last = pe.transpose(bank[r % 4][:, j, :], picked[n][:, 4 * g + j, :], T.ident[:])
                    last.then_inc(all_turned, 1)

        @block.scalar
        def _(act):
            E.prime_scalar(act)

            def split_w(h, slot):
                act.wait_ge(w_loaded, 16 * h + 16)
                nc.scalar.activation(w_in[:], w_in[:], ACT.Copy, scale=S_W).then_inc(w_scaled, 1)
                act.wait_ge(w_scaled, h)
                nc.scalar.activation(w_hi[slot][:], w_in[:], ACT.Copy).then_inc(w_hi_done, 1)

            def queries_out(h, sets=(0, 1)):
                for m, half in ((m, half) for m in sets for half in range(2)):
                    r = 2 * m + half
                    act.wait_ge(q_done, 4 * h + r + 1)
                    nc.scalar.activation(q_t[:, m, half * HALF:(half + 1) * HALF],
                                         bank[r][:].rearrange("p a b -> p (a b)"), ACT.Copy,
                                         scale=UNSCALE).then_inc(q_out, 1)

            def scores_out(h, first=False, sets=(0, 1)):
                if not first:
                    act.wait_ge(s_used, h)
                for m in sets:
                    for g in range(2):
                        act.wait_ge(scored, 4 * h + 2 * m + g + 1)
                        nc.scalar.activation(s[:, 4 * g:4 * g + 4, m, :], bank[2 * m + g][:],
                                             ACT.Copy).then_inc(s_out, 1)

            def step(hh, b, first=False, last=False):
                h = 2 * hh + b
                before = not (first and b == 0)
                if before:
                    E.split(act, h - 1, 1)
                else:
                    E.split(act, h, 0)
                if not last:
                    split_w(h + 2, b)
                if not (last and b):
                    act.wait_ge(scored, 4 * h + 4)
                    queries_out(h + 1)
                    scores_out(h + 1)
                if before:
                    E.gelu(act, h - 1, 1, 0)
                    E.split(act, h, 0)
                    E.gelu(act, h - 1, 1, 1)
                    E.keep(act, h - 1, 1)
                if last and b:
                    E.gelu(act, h, 0, 0)
                    E.split(act, h, 1)
                    E.gelu(act, h, 0, 1)
                    E.keep(act, h, 0)
                    for half in range(2):
                        E.gelu(act, h, 1, half)
                    E.keep(act, h, 1)
                act.wait_ge(shifted, h + 1)
                nc.scalar.activation(weight[:], weight[:], ACT.Exp).then_inc(weighted, 1)
                if not (last and b):
                    for half in range(2):
                        E.gelu(act, h, 0, half)
                    E.keep(act, h, 0)

            nc.scalar.activation(w_hi[0][:], w_in[:], ACT.Copy, scale=S_W).then_inc(w_hi_done, 1)
            for r in range(4):
                act.wait_ge(keys_turned, r + 1)
                nc.scalar.activation(keys_t[:, 4 * r:4 * r + 4, :], bank[r][:], ACT.Copy).then_inc(keys_out, 1)
            split_w(1, 1)
            for m in range(2):
                queries_out(0, sets=(m,))
                scores_out(0, first=True, sets=(m,))
            for b in range(2):
                step(0, b, first=True)
            with act.Fori(1, PAIRS - 1) as hh:
                for b in range(2):
                    step(hh, b)
            for b in range(2):
                step(PAIRS - 1, b, last=True)
            for r in range(6):
                act.wait_ge(all_turned, r + 1)
                n, g = r // 2, r % 2
                nc.scalar.activation(T.picked_t[n][:, g * HALF:(g + 1) * HALF], bank[r % 4][:].rearrange(
                    "p a b -> p (a b)"), ACT.Copy).then_inc(all_out, 1)

        @block.gpsimd
        def _(pool):
            E.prime_gpsimd(pool)

            def low_w(h, slot):
                pool.wait_ge(w_hi_done, h + 1)
                nc.gpsimd.tensor_tensor(w_lo[slot][:], w_in[:], w_hi[slot][:], ALU.subtract).then_inc(w_lo_done, 1)

            def step(hh, b, first=False, last=False):
                h = 2 * hh + b
                if not (first and b == 0):
                    E.low(pool, h - 1, 1)
                else:
                    E.low(pool, h, 0)
                if not last:
                    low_w(h + 2, b)
                if not (first and b == 0):
                    E.low(pool, h, 0)
                if last and b:
                    E.low(pool, h, 1)
                for n in range(2):
                    pool.wait_ge(found, 2 * h + n + 1)
                    got = match[:, n].rearrange("p (t k) a -> p t k a", t=NT)
                    nc.gpsimd.tensor_tensor(got, got, top_f[:, b, :, n, :].unsqueeze(2).broadcast_to(
                        [P, NT, TOPK, TOPK]), ALU.mult).then_inc(matched, 1)

            low_w(1, 1)
            for b in range(2):
                step(0, b, first=True)
            with pool.Fori(1, PAIRS - 1) as hh:
                for b in range(2):
                    step(hh, b)
            for b in range(2):
                step(PAIRS - 1, b, last=True)

        @block.vector
        def _(dve):
            dve.sem_inc(index_done, BASE)
            dve.wait_ge(w_hi_done, 1)
            nc.vector.scalar_tensor_tensor(w_lo[0][:], w_in[:], S_W, w_hi[0][:], ALU.mult,
                                           ALU.subtract).then_inc(w_lo_done, 1)

            def top16(c, groups):
                marks = [0, 0]
                steps = 0

                def settled(g):
                    dve.wait_ge(c.sem, c.at + marks[g])
                    c.step(nc.vector.tensor_copy(carrier[:, steps % 4:steps % 4 + 1], T.iota[0:1, 0:1]))

                for step in range(4):
                    for g, rows in enumerate(groups):
                        if step:
                            settled(g)
                            steps += 1
                        for v, w, o, i in rows:
                            if step == 0:
                                c.step(nc.vector.max(o[:, 0:8], v))
                            elif step == 1:
                                c.step(nc.vector.max_index(i[:, 0:8], o[:, 0:8], v))
                                c.step(nc.vector.match_replace(w, o[:, 0:8], v, FLOOR))
                            elif step == 2:
                                c.step(nc.vector.max(o[:, 8:16], w))
                            else:
                                c.step(nc.vector.max_index(i[:, 8:16], o[:, 8:16], w))
                        marks[g] = c.n
                c.wait()

            def hold(c):
                c.step(nc.vector.tensor_copy(carrier[:, 4:5], T.iota[0:1, 0:1]))

            def index_sum(h, n):
                dve.wait_ge(matched, 2 * h + n + 1)
                out = picked[n][:, :, bass.ds(h * TOPK, TOPK)]
                nc.vector.tensor_reduce(out, match[:, n].rearrange("p (t k) a -> p t k a", t=NT), AX.X,
                                        ALU.add).then_inc(index_done, 1)

            STEPS = 140

            def step(hh, b, first=False):
                h = 2 * hh + b
                c = Chain(dve, vec_step, STEPS * h)
                if not (first and b == 0):
                    c.wait()
                dve.wait_ge(s_out, 4 * h + 4)
                hold(c)
                top16(c, [[(s[:, t, m, :], s2[:, t, m, :], top[:, t, m, :], top_i[:, t, m, :]) for t in range(NT)]
                          for m in range(2)])
                nc.vector.tensor_copy(top_f[:, b], top_i[:]).then_inc(s_used, 1)
                c.step(nc.vector.tensor_tensor(
                    cand[:].rearrange("p t (a b) -> p t a b", a=TOPK),
                    top[:, :, 0, :].unsqueeze(3).broadcast_to([P, NT, TOPK, TOPK]),
                    top[:, :, 1, :].unsqueeze(2).broadcast_to([P, NT, TOPK, TOPK]), ALU.add))
                c.wait()
                hold(c)
                top16(c, [[(cand[:, t, :], cand2[:, t, :], best[:, t, :], pos[:, t * TOPK:(t + 1) * TOPK])
                           for t in range(g * NT // 2, (g + 1) * NT // 2)] for g in range(2)])
                nc.vector.tensor_tensor(weight[:], best[:], best[:, :, 0:1].broadcast_to([P, NT, TOPK]),
                                        ALU.subtract).then_inc(shifted, 1)
                c.step(nc.vector.tensor_scalar(part[:, 0, :], pos[:], 4, None, ALU.logical_shift_right))
                c.step(nc.vector.tensor_scalar(part[:, 1, :], pos[:], TOPK - 1, None, ALU.bitwise_and))
                c.wait()
                c.step(nc.vector.tensor_copy(part_f[:], part[:]))
                if not (first and b == 0):
                    for n in range(2):
                        index_sum(h - 1, n)
                c.wait()
                for n in range(2):
                    dve.wait_ge(index_done, BASE + 2 * h)
                    nc.vector.tensor_tensor(match[:, n], lanes(part_f[:, n, :], 2, P, NT * TOPK, TOPK),
                                            lanes(T.iota[:, 0:TOPK], 1, P, NT * TOPK, TOPK),
                                            ALU.is_equal).then_inc(found, 1)
                dve.wait_ge(weighted, h + 1)
                c.link(nc.vector.tensor_reduce(total[:], weight[:], AX.X, ALU.add))
                c.link(nc.vector.reciprocal(total[:], total[:]))
                nc.vector.tensor_tensor(picked[2][:, :, bass.ds(h * TOPK, TOPK)], weight[:],
                                        lanes(total[:], 2, P, NT, TOPK), ALU.mult).then_inc(weight_done, 1)
                assert c.n == STEPS, c.n

            for b in range(2):
                step(0, b, first=True)
            with dve.Fori(1, PAIRS) as hh:
                for b in range(2):
                    step(hh, b)
            for n in range(2):
                index_sum(PEER_H - 1, n)


BANK_T = 4
S_G = 1024.0


def spread_weights(nc, io, T):
    RING = 4
    STEPS = BLOCK // BANK_T
    with ExitStack() as ctx:
        S = Space(nc, ctx, "e")
        E = EarlyTiles(nc, io, T, S, EARLY_S, EARLY_R * PEER_H, EARLY_S * NBLOCK)
        iota = S.sb("iota", [P, P], F16)
        left = [S.sb(f"left{r}", [P, BANK_T, P], F16) for r in range(RING)]
        right = [S.sb(f"right{r}", [P, 2, BANK_T, P], F16) for r in range(RING)]
        w_hi16 = S.sb("w_hi16", [P, SEQ], F16)
        w_hi = S.sb("w_hi", [P, SEQ])
        stage = [S.sb(f"stage{b}", [P, NKEYS, TB]) for b in range(2)]
        tab = [S.ps(f"tab{r}", [P, BANK_T, P]) for r in range(RING)]
        vec_step = S.sem("vec_step")
        built = S.sem("built")
        spread = S.sem("spread")
        out = S.sem("out")
        stored = [S.sem(f"stored{b}") for b in range(2)]
        F = T.first
        next_loaded = S.sem("next_loaded")
        next_turned = S.sem("next_turned")
        next_hi = S.sem("next_hi")
        next_lo = S.sem("next_lo")
        next_hidden = S.sem("next_hidden")
        block = ctx.enter_context(nc.Block())
        key1_t, key2_t, w_lo = T.picked_t
        HALVES = {(r * STEPS + 1) // (2 * EARLY_S): (r // 2, r % 2) for r in range(2 * EARLY_S)}

        @block.vector
        def _(dve):
            c = Chain(dve, vec_step)
            c.link(nc.vector.tensor_scalar(w_lo, w_lo, S_G, None, ALU.mult))
            c.step(nc.vector.tensor_copy(iota[:], T.iota[:]))
            c.link(nc.vector.tensor_copy(w_hi16[:], w_lo))
            c.link(nc.vector.tensor_copy(w_hi[:], w_hi16[:]))
            c.link(nc.vector.tensor_tensor(w_lo, w_lo, w_hi[:], ALU.subtract))
            with dve.Fori(0, NBLOCK) as blk:
                for s in range(STEPS):
                    r = s % RING
                    dve.wait_ge(spread, BASE - RING + 1 + blk * STEPS + s)
                    nc.vector.tensor_tensor(left[r][:], lanes(T.iota[:], 1, P, BANK_T, P),
                                            lanes(key2_t[:, bass.ds(blk * BLOCK + s * BANK_T, BANK_T)], 2, P, BANK_T, P),
                                            ALU.is_equal)
                    for j in range(BANK_T):
                        tok = bass.ds(blk * BLOCK + (s * BANK_T + j), 1)
                        nc.vector.tensor_scalar(right[r][:, 0, j, :], iota[:], key1_t[:, tok], w_hi[:, tok],
                                                ALU.is_equal, ALU.mult)
                        last = nc.vector.tensor_scalar(right[r][:, 1, j, :], iota[:], key1_t[:, tok], w_lo[:, tok],
                                                       ALU.is_equal, ALU.mult)
                    last.then_inc(built, 1)
            for b in range(2):
                dve.wait_ge(next_hi, b + 1)
                nc.vector.scalar_tensor_tensor(F.u_lo[b][:], E.u_ps[:], S_U, F.u_hi[b][:], ALU.mult,
                                               ALU.subtract).then_inc(next_lo, 1)

        @block.tensor
        def _(pe):
            E.prime_tensor(pe)
            pe.sem_inc(spread, BASE)

            def step(blk, last):
                for s in range(STEPS):
                    n, r = blk * STEPS + s, s % RING
                    pe.wait_ge(built, n + 1)
                    pe.wait_ge(out, BASE - RING + 1 + n)
                    for j in range(BANK_T):
                        for part in range(2):
                            mm = pe.matmul(tab[r][:, j, :], left[r][:, j, :], right[r][:, part, j, :],
                                           start=part == 0, stop=part == 1)
                    mm.then_inc(spread, 1)
                    if s in HALVES:
                        b, half = HALVES[s]
                        if half == 0 and b + 1 < EARLY_S:
                            E.turn(pe, blk, b + 1)
                        elif half == 0 and not last:
                            E.turn(pe, blk + 1, 0)
                        E.hidden(pe, blk, b, half)

            E.turn(pe, 0, 0)
            with pe.Fori(0, NBLOCK - 1) as blk:
                step(blk, False)
            step(NBLOCK - 1, True)

            def turn(b):
                for k in range(KT):
                    last = pe.transpose(E.u_ps[:, k, :], F.u_in[b][:, k * P:(k + 1) * P], T.ident[:])
                last.then_inc(next_turned, 1)

            pe.wait_ge(next_loaded, 32)
            turn(0)
            pe.wait_ge(next_lo, 1)
            turn(1)
            pe.wait_ge(E.gelu_done, BASE + 2 * EARLY_S * NBLOCK)
            for half in range(2):
                toks = slice(half * HALF, (half + 1) * HALF)
                for k in range(KT):
                    last = split_mm(pe, E.hid[half][:], F.u_hi[0][:, k, :], F.u_lo[0][:, k, :], T.act_hi[:, k, toks],
                                    T.act_lo[:, k, toks], k == 0, k == KT - 1)
                last.then_inc(next_hidden, 1)

        @block.scalar
        def _(act):
            E.prime_scalar(act)
            act.sem_inc(out, BASE)
            for b in range(2):
                act.sem_inc(stored[b], BASE)

            def step(blk, last):
                for s in range(STEPS):
                    n, r = blk * STEPS + s, s % RING
                    slot, at = s // (STEPS // 2), s % (STEPS // 2) * BANK_T
                    if at == 0:
                        act.wait_ge(stored[slot], BASE + blk * 16)
                    act.wait_ge(spread, BASE + 1 + n)
                    nc.scalar.activation(stage[slot][:, :, at:at + BANK_T],
                                         tab[r][:].rearrange("p t i -> p i t"), ACT.Copy).then_inc(out, 1)
                    if s in HALVES:
                        b, half = HALVES[s]
                        if half == 0 and b + 1 < EARLY_S:
                            E.split(act, blk, b + 1)
                        elif half == 0 and not last:
                            E.split(act, blk + 1, 0)
                        E.gelu(act, blk, b, half)

            E.split(act, 0, 0)
            with act.Fori(0, NBLOCK - 1) as blk:
                step(blk, False)
            step(NBLOCK - 1, True)
            for b in range(2):
                act.wait_ge(next_turned, b + 1)
                nc.scalar.activation(F.u_hi[b][:], E.u_ps[:], ACT.Copy, scale=S_U).then_inc(next_hi, 1)
            for half in range(2):
                act.wait_ge(next_hidden, half + 1)
                nc.scalar.activation(F.gel[0][:, half * HALF:(half + 1) * HALF], E.hid[half][:], ACT.Gelu,
                                     scale=1.0 / (S_U * S_ACT))

        @block.gpsimd
        def _(pool):
            E.prime_gpsimd(pool)
            with pool.Fori(0, NBLOCK) as blk:
                for b in range(EARLY_S):
                    E.low(pool, blk, b)

        @block.sync
        def _(sp):
            def step(blk, last):
                for b in range(EARLY_S):
                    E.keep(sp, blk, b)
                    if not last:
                        E.load(sp, blk + 1, b)
                    if b >= 1:
                        sp.wait_ge(out, BASE + blk * STEPS + b * (STEPS // 2))
                        sp.dma_start(T.dense.rearrange("(c b) j r -> c b j r", b=2)[blk, b - 1],
                                     stage[b - 1][:].rearrange("p i t -> p (i t)")).then_inc(stored[b - 1], 16)

            for b in range(EARLY_S):
                E.load(sp, 0, b, again=False)
            for b in range(2):
                rows = slice((N_EARLY + b) * P, (N_EARLY + b + 1) * P)
                sp.dma_start(F.u_in[b][:], io.peer_u[0, rows, :]).then_inc(next_loaded, 16)
            with sp.Fori(0, NBLOCK - 1) as blk:
                step(blk, False)
            step(NBLOCK - 1, True)
            for slot in range(2):
                sp.wait_ge(stored[slot], BASE + 16 * NBLOCK)
            E.all_kept(sp, EARLY_S * NBLOCK)


S_A = 64.0
GROUP = 4
NE = NKEYS


def experts(nc, io, T):
    LOOP = 2 * GROUP
    LATE = (NE - N_EARLY) // LOOP
    TURNS = NE // LOOP
    with ExitStack() as ctx:
        S = Space(nc, ctx, "f")
        v_in = [S.sb(f"v_in{b}", [P, D]) for b in range(2)]
        g_in = [S.sb(f"g_in{b}", [P, NTB, GROUP * TB]) for b in range(2)]
        u_in, u_hi, u_lo, gel = T.first.u_in, T.first.u_hi, T.first.u_lo, T.first.gel
        a = [S.sb(f"a{b}", [P, SEQ]) for b in range(2)]
        a_hi = [[S.sb(f"a_hi{g}{j}", [P, SEQ], F16) for j in range(GROUP)] for g in range(2)]
        a_lo = [[S.sb(f"a_lo{g}{j}", [P, SEQ], F16) for j in range(GROUP)] for g in range(2)]
        v_hi = [[S.sb(f"v_hi{g}{j}", [P, D], F16) for j in range(GROUP)] for g in range(2)]
        v_lo = [[S.sb(f"v_lo{g}{j}", [P, D], F16) for j in range(GROUP)] for g in range(2)]
        u_ps = S.ps("u_ps", [P, KT, P])
        hid = [S.ps(f"hid{b}", [P, SEQ]) for b in range(2)]
        y = [S.ps(f"y{b}", [P, HALF]) for b in range(2)]

        v_loaded = [S.sem(f"v_loaded{b}") for b in range(2)]
        g_loaded = [S.sem(f"g_loaded{b}") for b in range(2)]
        u_loaded = [S.sem(f"u_loaded{b}") for b in range(2)]
        gel_loaded = [S.sem(f"gel_loaded{b}") for b in range(2)]
        u_turned = S.sem("u_turned")
        u_hi_done = S.sem("u_hi_done")
        u_lo_done = S.sem("u_lo_done")
        hid_done = S.sem("hid_done")
        gelu_done = S.sem("gelu_done")
        stored = S.sem("stored")
        y_done = S.sem("y_done")
        v_hi_done = S.sem("v_hi_done")
        a_hi_done = S.sem("a_hi_done")
        a_done = S.sem("a_done")
        a_lo_done = S.sem("a_lo_done")
        y_added = S.sem("y_added")
        v_lo_done = S.sem("v_lo_done")
        block = ctx.enter_context(nc.Block())

        YB = NT * (D // HALF)
        YS = YB // GROUP
        y_place = [(k // 2, k % 2) for k in range(YB)]

        @block.sync
        def _(sp):
            u_v = io.peer_u[0, N_EARLY * P:NE * P, :].rearrange("(c m p) d -> c m p d", m=LOOP, p=P)
            kept_v = T.kept.rearrange("(c m p) t -> c m p t", m=LOOP, p=P)
            out_v = io.out[0].rearrange("(t p) d -> p t d", p=P)

            def step(c, view, early=False, first=False):
                at, count = (0, N_EARLY) if early else (N_EARLY, NE - N_EARLY)
                v_v = io.peer_v[0, at * P:(at + count) * P, :].rearrange("(c m p) d -> c m p d", m=LOOP, p=P)
                g_v = T.dense[:, :, at * TB:(at + count) * TB].rearrange("b j (c g r) -> c g j b r", g=2,
                                                                              r=GROUP * TB)
                def load_g(g, n):
                    sp.wait_ge(a_done, BASE + n - GROUP)
                    sp.dma_start(g_in[g][:], g_v[view, g]).then_inc(g_loaded[g], 16)

                for m in range(LOOP):
                    n = c * LOOP + m
                    if m % GROUP == 0 and not (first and m == 0):
                        load_g(m // GROUP, n)
                    if early:
                        sp.wait_ge(a_done, BASE + n - 1)
                        sp.dma_start(gel[m % 2][:], kept_v[view, m]).then_inc(gel_loaded[m % 2], 16)
                    elif not (first and m < 2):
                        sp.wait_ge(u_turned, BASE + n - 1)
                        sp.dma_start(u_in[m % 2][:], u_v[view, m]).then_inc(u_loaded[m % 2], 16)
                    if first and m == 2:
                        load_g(0, 0)
                    sp.wait_ge(v_lo_done, BASE + n - 1)
                    sp.dma_start(v_in[m % 2][:], v_v[view, m]).then_inc(v_loaded[m % 2], 16)

            for b in range(2):
                sp.sem_inc(u_loaded[b], 16)
            step(0, 0, first=True)
            with sp.Fori(1, LATE) as c:
                step(c, c)
            with sp.Fori(0, TURNS - LATE) as e:
                step(e + LATE, e, early=True)
            for t in range(NT):
                sp.wait_ge(y_added, BASE + YB * (NE // GROUP - 1) + 2 * t + 2)
                sp.dma_start(out_v[:, t, :], T.h[:, t, :]).then_inc(stored, 16)
            sp.wait_ge(stored, 16 * NT)

        @block.tensor
        def _(pe):
            pe.sem_inc(u_turned, BASE + 2)
            pe.sem_inc(hid_done, BASE + 1)
            pe.sem_inc(y_done, BASE)

            def turn(n, m):
                pe.wait_ge(u_loaded[m % 2], n * 8 + (16 - 8 * (m % 2)))
                pe.wait_ge(u_lo_done, BASE + n)
                for k in range(KT):
                    last = pe.transpose(u_ps[:, k, :], u_in[m % 2][:, k * P:(k + 1) * P], T.ident[:])
                last.then_inc(u_turned, 1)

            def hidden(n, m, between=None):
                pe.wait_ge(u_lo_done, BASE + n + 1)
                pe.wait_ge(gelu_done, BASE + n - 1)
                for half in range(2):
                    if half and between is not None:
                        turn(between, between)
                    toks = slice(half * HALF, (half + 1) * HALF)
                    for k in range(KT):
                        last = split_mm(pe, hid[m % 2][:, toks], u_hi[m % 2][:, k, :], u_lo[m % 2][:, k, :],
                                        T.act_hi[:, k, toks], T.act_lo[:, k, toks], k == 0, k == KT - 1)
                last.then_inc(hid_done, 1)

            def outputs(group_n, g, part):
                if part == 0:
                    pe.wait_ge(a_lo_done, BASE + GROUP * (group_n + 1))
                    pe.wait_ge(v_lo_done, BASE + GROUP * (group_n + 1))
                for k in range(part * YS, (part + 1) * YS):
                    t, half = y_place[k]
                    pe.wait_ge(y_added, BASE + YB * group_n + k - 1)
                    for j in range(GROUP):
                        toks, cols = slice(t * P, (t + 1) * P), slice(half * HALF, (half + 1) * HALF)
                        last = split_mm(pe, y[k % 2][:], a_hi[g][j][:, toks], a_lo[g][j][:, toks],
                                        v_hi[g][j][:, cols], v_lo[g][j][:, cols], j == 0, j == GROUP - 1)
                    last.then_inc(y_done, 1)

            def step(c, m, y_too=True, u_too=True, early=False):
                n = c * LOOP + m
                if u_too and not early:
                    turn(n + 1, m + 1)
                if not early:
                    hidden(n, m)
                if y_too:
                    outputs(2 * c + m // GROUP - 1, (m // GROUP + 1) % 2, m % GROUP)

            hidden(1, 1, between=2)
            for m in range(2, LOOP):
                step(0, m, y_too=m >= GROUP)
            with pe.Fori(1, LATE - 1) as c:
                for m in range(LOOP):
                    step(c, m)
            for m in range(LOOP):
                step(LATE - 1, m, u_too=m < LOOP - 1)
            with pe.Fori(LATE, TURNS) as c:
                for m in range(LOOP):
                    step(c, m, early=True)
            for part in range(GROUP):
                outputs(NE // GROUP - 1, 1, part)

        @block.scalar
        def _(act):
            act.sem_inc(gelu_done, BASE + 1)
            act.sem_inc(u_hi_done, BASE + 2)
            act.sem_inc(v_hi_done, BASE)
            act.sem_inc(a_hi_done, BASE)

            def hi_u(n, m):
                act.wait_ge(u_turned, BASE + n + 1)
                act.wait_ge(hid_done, BASE + n - 1)
                nc.scalar.activation(u_hi[m % 2][:], u_ps[:], ACT.Copy, scale=S_U).then_inc(u_hi_done, 1)

            def step(c, m, u_too=True, early=False, first=False):
                n = c * LOOP + m
                g, j = m // GROUP, m % GROUP
                if u_too and not early and not first:
                    hi_u(n + 1, m + 1)
                if j == 0:
                    act.wait_ge(y_done, BASE + YB * (2 * c + g - 1))
                act.wait_ge(v_loaded[m % 2], n * 8 + (16 - 8 * (m % 2)))
                nc.scalar.activation(v_hi[g][j][:], v_in[m % 2][:], ACT.Copy).then_inc(v_hi_done, 1)
                if not early and not first:
                    act.wait_ge(hid_done, BASE + n + 1)
                    act.wait_ge(a_done, BASE + n - 1)
                    nc.scalar.activation(gel[m % 2][:], hid[m % 2][:], ACT.Gelu,
                                         scale=1.0 / (S_U * S_ACT)).then_inc(gelu_done, 1)
                act.wait_ge(a_done, BASE + n + 1)
                nc.scalar.activation(a_hi[g][j][:], a[m % 2][:], ACT.Copy).then_inc(a_hi_done, 1)

            for m in range(LOOP):
                step(0, m, first=m == 0)
            with act.Fori(1, LATE - 1) as c:
                for m in range(LOOP):
                    step(c, m)
            for m in range(LOOP):
                step(LATE - 1, m, u_too=m < LOOP - 1)
            with act.Fori(LATE, TURNS) as c:
                for m in range(LOOP):
                    step(c, m, early=True)

        @block.gpsimd
        def _(pool):
            pool.sem_inc(v_lo_done, BASE)
            with pool.Fori(0, TURNS) as c:
                for m in range(LOOP):
                    n = c * LOOP + m
                    g, j = m // GROUP, m % GROUP
                    pool.wait_ge(v_hi_done, BASE + n + 1)
                    nc.gpsimd.tensor_tensor(v_lo[g][j][:], v_in[m % 2][:], v_hi[g][j][:],
                                            ALU.subtract).then_inc(v_lo_done, 1)

        @block.vector
        def _(dve):
            dve.sem_inc(u_lo_done, BASE + 2)
            dve.sem_inc(a_done, BASE)
            dve.sem_inc(a_lo_done, BASE)
            dve.sem_inc(y_added, BASE)

            def lo_u(n, m):
                dve.wait_ge(u_hi_done, BASE + n + 1)
                nc.vector.scalar_tensor_tensor(u_lo[m % 2][:], u_ps[:], S_U, u_hi[m % 2][:], ALU.mult,
                                               ALU.subtract).then_inc(u_lo_done, 1)

            def add_y(group_n, k):
                t, half = y_place[k]
                cols = slice(half * HALF, (half + 1) * HALF)
                dve.wait_ge(y_done, BASE + YB * group_n + k + 1)
                dve.wait_ge(y_added, BASE + YB * (group_n - 1) + k + 1)
                nc.vector.scalar_tensor_tensor(T.h[:, t, cols], y[k % 2][:], 1.0 / S_A, T.h[:, t, cols], ALU.mult,
                                               ALU.add).then_inc(y_added, 1)

            def step(c, m, y_too=True, u_too=True, early=False):
                n = c * LOOP + m
                g, j = m // GROUP, m % GROUP
                if u_too and not early:
                    lo_u(n + 1, m + 1)
                if j == 0:
                    dve.wait_ge(g_loaded[g], c * 16 + 16)
                if early:
                    at = n - LATE * LOOP
                    dve.wait_ge(gel_loaded[m % 2], at * 8 + (16 - 8 * (m % 2)))
                    dve.wait_ge(a_hi_done, BASE + n - 1)
                else:
                    dve.wait_ge(gelu_done, BASE + n + 1)
                dve.wait_ge(a_lo_done, BASE + n - 1)
                nc.vector.scalar_tensor_tensor(
                    a[m % 2][:].rearrange("p (b t) -> p b t", t=TB), gel[m % 2][:].rearrange("p (b t) -> p b t", t=TB),
                    S_A / S_G, g_in[g][:].rearrange("p b (i t) -> p b i t", t=TB)[:, :, j, :], ALU.mult,
                    ALU.mult).then_inc(a_done, 1)
                if y_too:
                    add_y(2 * c + g - 1, j * YS)
                dve.wait_ge(a_hi_done, BASE + n + 1)
                nc.vector.tensor_tensor(a_lo[g][j][:], a[m % 2][:], a_hi[g][j][:], ALU.subtract).then_inc(a_lo_done, 1)
                if y_too:
                    for k in range(j * YS + 1, (j + 1) * YS):
                        add_y(2 * c + g - 1, k)

            for m in range(LOOP):
                step(0, m, y_too=m >= GROUP, u_too=m > 0)
            with dve.Fori(1, LATE - 1) as c:
                for m in range(LOOP):
                    step(c, m)
            for m in range(LOOP):
                step(LATE - 1, m, u_too=m < LOOP - 1)
            with dve.Fori(LATE, TURNS) as c:
                for m in range(LOOP):
                    step(c, m, early=True)
            for k in range(YB):
                add_y(NE // GROUP - 1, k)


def allocate_constants(S):
    T = Names()
    T.ident = S.sb("ident", [P, P])
    T.causal = S.sb("causal", [P, P])
    T.tri = S.sb("tri", [P, P])
    T.iota = S.sb("iota", [P, P])
    T.iota_i = S.sb("iota_i", [P, P], I32)
    T.mhalf = S.sb("mhalf", [P, 8])
    T.eps = S.sb("eps", [P, 8])
    T.g_mix = S.sb("g_mix", [P, KT])
    T.g_sub = S.sb("g_sub", [P, 1])
    T.b_gate = S.sb("b_gate", [P, 2])
    T.g_gla = S.sb("g_gla", [P, GLA_DV])
    T.g_q = S.sb("g_q", [P, DIFF_DK])
    T.g_k = S.sb("g_k", [P, DIFF_DK])
    T.w_gate = S.sb("w_gate", [GLA_RANK, GLA_H * GLA_DK])
    T.sin = S.sb("sin", [P, NT, HROPE])
    T.cos = S.sb("cos", [P, NT, HROPE])
    T.neg_lam = S.sb("neg_lam", [P, 1])
    T.act_hi = S.sb("act_hi", [P, KT, SEQ], F16)
    T.act_lo = S.sb("act_lo", [P, KT, SEQ], F16)
    return T


def allocate_diff(S, T):
    T.dq = S.sb("dq", [P, NT, HALF])
    T.dk = S.sb("dk", [P, NT, HALF])
    T.dv = S.sb("dv", [P, NT, HALF])


def allocate_gla(S, T):
    T.gqk = S.sb("gqk", [P, 4, SEQ])
    T.cum = S.sb("cum", [P, 2, SEQ])
    T.gv = S.sb("gv", [P, NT, HALF])
    T.gr = S.sb("gr", [P, NT, HALF])


def stage(nc, program, io, T):
    with nc.cleanup_on_exit():
        program(nc, io, T)


def allocate_w_peer(S, T):
    T.w_peer = S.sb("w_peer", [P, KT, QDIM], side="right")
    T.keys = S.sb("keys", [P, NSET, NKEYS], side="right")


def allocate_first(S):
    F = Names()
    F.u_in = [S.sb(f"u_in{b}", [P, D], side="right") for b in range(2)]
    F.u_hi = [S.sb(f"u_hi{b}", [P, KT, P], F16, side="right") for b in range(2)]
    F.u_lo = [S.sb(f"u_lo{b}", [P, KT, P], F16, side="right") for b in range(2)]
    F.gel = [S.sb(f"gel{b}", [P, SEQ], side="right") for b in range(2)]
    return F


def hybrid_block(nc, io):
    dense = nc.dram_tensor("dense_weights", [NTB, NKEYS, NKEYS * TB], F32, kind="Internal").ap()
    kept = nc.dram_tensor("early_tiles", [N_EARLY * NKEYS, SEQ], F32, kind="Internal").ap()
    with ExitStack() as whole, ExitStack() as peer, ExitStack() as out:
        T = allocate_constants(Space(nc, whole, "p"))
        T.dense, T.kept = dense, kept
        with ExitStack() as diff:
            allocate_diff(Space(nc, diff, "p"), T)
            with ExitStack() as gla:
                S = Space(nc, gla, "p")
                allocate_gla(S, T)
                stage(nc, project_in, io, T)
                T.state = S.sb("state", [P, NCH, 2, GLA_DV])
                stage(nc, gla_states, io, T)
                stage(nc, gla_outputs, io, T)
            allocate_w_peer(Space(nc, peer, "x"), T)
            T.w_out = Space(nc, out, "x").sb("w_out", [P, KT, D], side="right")
            stage(nc, diff_attention, io, T)
        T.h = Space(nc, whole, "p").sb("h", [P, NT, D])
        stage(nc, project_out, io, T)
        out.close()
        with ExitStack() as picks:
            S = Space(nc, picks, "p")
            T.picked_all = S.sb("picked_all", [P, 3 * SEQ])
            T.picked_t = [T.picked_all[:, n * SEQ:(n + 1) * SEQ] for n in range(3)]
            stage(nc, retrieve, io, T)
            peer.close()
            T.first = allocate_first(Space(nc, whole, "x"))
            stage(nc, spread_weights, io, T)
        stage(nc, experts, io, T)


_INS = ["x", "positions", "g_mix", "w_in", "w_gla_gate", "b_gla_gate", "g_gla_out", "g_q", "g_k", "lambda_q1",
        "lambda_k1", "lambda_q2", "lambda_k2", "g_diff_sub", "w_out", "g_ffn", "w_peer_q", "peer_sub_keys", "peer_u",
        "peer_v"]


def kernel(**inputs):
    import numpy as _np
    import concourse.bacc as _bacc
    from concourse import mybir as _mybir
    from concourse.bass_utils import run_bass_kernel_spmd as _run

    nc = _bacc.Bacc("TRN2", target_bir_lowering=False, num_devices=1)
    arrays, io = {}, Names()
    for name in _INS:
        a = _np.ascontiguousarray(inputs[name])
        arrays[f"in_{name}"] = a
        io.__dict__[name] = nc.dram_tensor(f"in_{name}", a.shape, _mybir.dt.from_np(a.dtype),
                                           kind="ExternalInput").ap()
    io.out = nc.dram_tensor("out", (1, SEQ, D), F32, kind="ExternalOutput").ap()
    hybrid_block(nc, io)
    r = _run(nc, [arrays], core_ids=[0])
    return r.results[0]["out"]
```
